# Optimizing a Trainium2 kernel written in Bass

```python
import math
import jax
import jax.numpy as jnp
from jax import lax
import numpy as np

D_MODEL = 1024
BATCH = 1
SEQ = 1024
DEPTH = 2
DEC_BATCH = 1
DEC_SEQ = 64
PAST_LEN = 512

CHUNK = 64
HEAD_DIM = 64
SB_WIDTH = D_MODEL // 2
SB_HEADS = SB_WIDTH // HEAD_DIM
SGU_WIDTH = D_MODEL // 2
SGU_GROUPS = 8
SGU_GROUP_DIM = SGU_WIDTH // SGU_GROUPS
SGU_CHUNK = 128
QBLK = 128
IN_WIDTH = 3 * SB_WIDTH + 2 * SGU_WIDTH
MIX_WIDTH = SB_WIDTH + SGU_WIDTH
SSM_GROUP = 16
SSM_GROUPS = D_MODEL // SSM_GROUP
SSM_STATE = 64
STEP_MIN = 1e-3
STEP_MAX = 1e-1
_FFN_RAW = (8 * D_MODEL + 2) // 3
FFN_HIDDEN = ((_FFN_RAW + 255) // 256) * 256
N_AB = (DEPTH + 1) // 2
N_SSM = DEPTH // 2
RMS_EPS = 1e-6

kernel_name = 'stream_sb_gmlp_s5_step'

def rmsnorm(x, g):
    xf = x.astype(jnp.float32)
    y = xf * lax.rsqrt(jnp.mean(xf * xf, axis=-1, keepdims=True) + RMS_EPS)
    return (y * g.astype(jnp.float32)).astype(x.dtype)

def swiglu(h, w_gate, w_up, w_down):
    return (jax.nn.silu(h @ w_gate) * (h @ w_up)) @ w_down

def ab_project(h, w_in):
    bsz, L = h.shape[:2]
    z = h @ w_in
    q, k, v, u, g = jnp.split(z, [SB_WIDTH, 2 * SB_WIDTH, 3 * SB_WIDTH, 3 * SB_WIDTH + SGU_WIDTH], axis=-1)
    heads = lambda t: t.reshape(bsz, L, SB_HEADS, HEAD_DIM)
    return heads(q), heads(k), heads(v), jax.nn.gelu(u), jax.nn.gelu(g)

def sb_attend(q, k, v, q_pos, k_pos):
    z = jnp.einsum('bqhd,bkhd->bhqk', q.astype(jnp.float32), k.astype(jnp.float32)) * (HEAD_DIM ** -0.5)
    mask = k_pos[None, :] < q_pos[:, None]
    log_stay = jnp.where(mask, jax.nn.log_sigmoid(-z), 0.0)
    log_after = lax.cumsum(log_stay, axis=3, reverse=True) - log_stay
    w = jnp.where(mask, jnp.exp(jax.nn.log_sigmoid(z) + log_after), 0.0)
    return jnp.einsum('bhqk,bkhd->bqhd', w, v.astype(jnp.float32))

def sb_prompt(q, k, v):
    bsz, L = q.shape[:2]
    nblk = L // QBLK
    qb = jnp.moveaxis(q.reshape(bsz, nblk, QBLK, SB_HEADS, HEAD_DIM), 1, 0)
    pos = jnp.arange(L)
    qpos = pos.reshape(nblk, QBLK)
    out = lax.map(lambda a: sb_attend(a[0], k, v, a[1], pos), (qb, qpos))
    return jnp.moveaxis(out, 0, 1).reshape(bsz, L, SB_WIDTH)

def sb_sample(q, k, v, cache_k, cache_v):
    past, n = cache_k.shape[1], q.shape[1]
    k_all = jnp.concatenate([cache_k.astype(k.dtype), k], axis=1)
    v_all = jnp.concatenate([cache_v.astype(v.dtype), v], axis=1)
    out = sb_attend(q, k_all, v_all, past + jnp.arange(n), jnp.arange(past + n))
    return out.reshape(q.shape[0], n, SB_WIDTH)

def sgu_prompt(u, g, w_s, b_s):
    bsz, L = g.shape[:2]
    nc = L // SGU_CHUNK
    tri = jnp.tril(jnp.ones((SGU_CHUNK, SGU_CHUNK), dtype=bool))
    ws = jnp.where(tri, w_s, 0.0).astype(jnp.float32)
    gc = g.reshape(bsz, nc, SGU_CHUNK, SGU_GROUPS, SGU_GROUP_DIM).astype(jnp.float32)
    mixed = jnp.einsum('gts,bcsgd->bctgd', ws, gc) + b_s.T.astype(jnp.float32)[:, :, None]
    return u.astype(jnp.float32) * mixed.reshape(bsz, L, SGU_WIDTH)

def sgu_sample(u, g, w_s, b_s):
    bsz, n = g.shape[:2]
    tri = jnp.tril(jnp.ones((n, n), dtype=bool))
    ws = jnp.where(tri, w_s[:, :n, :n], 0.0).astype(jnp.float32)
    gs = g.reshape(bsz, n, SGU_GROUPS, SGU_GROUP_DIM).astype(jnp.float32)
    mixed = jnp.einsum('gts,bsgd->btgd', ws, gs) + b_s[:, :n].T.astype(jnp.float32)[:, :, None]
    return u.astype(jnp.float32) * mixed.reshape(bsz, n, SGU_WIDTH)

def ab_mixer_prompt(h, w_in, w_s, b_s, w_out):
    q, k, v, u, g = ab_project(h, w_in)
    att = sb_prompt(q, k, v)
    sg = sgu_prompt(u, g, w_s, b_s)
    out = jnp.concatenate([att, sg], axis=-1).astype(h.dtype) @ w_out
    return out, k, v

def ab_mixer_sample(h, cache_k, cache_v, w_in, w_s, b_s, w_out):
    q, k, v, u, g = ab_project(h, w_in)
    att = sb_sample(q, k, v, cache_k, cache_v)
    sg = sgu_sample(u, g, w_s, b_s)
    out = jnp.concatenate([att, sg], axis=-1).astype(h.dtype) @ w_out
    return out, k, v, g

def _cplx_affine_combine(e1, e2):
    a1r, a1i, b1r, b1i = e1
    a2r, a2i, b2r, b2i = e2
    return (a1r * a2r - a1i * a2i,
            a1r * a2i + a1i * a2r,
            a2r * b1r - a2i * b1i + b2r,
            a2r * b1i + a2i * b1r + b2i)

def s5_mixer(h, h0_re, h0_im, lam_re, lam_im, log_step, b_re, b_im, c_re, c_im, d_skip, w_glu):
    f32 = jnp.float32
    bsz, L = h.shape[:2]
    u = h.astype(f32)
    lr, li = lam_re.astype(f32), lam_im.astype(f32)
    step = jnp.exp(log_step.astype(f32))[:, None]
    mag, ang = jnp.exp(lr * step), li * step
    ab_re, ab_im = mag * jnp.cos(ang), mag * jnp.sin(ang)
    den = lr * lr + li * li
    nr = ab_re - 1.0
    co_re = (nr * lr + ab_im * li) / den
    co_im = (ab_im * lr - nr * li) / den
    br, bi = b_re.astype(f32), b_im.astype(f32)
    bb_re = co_re[..., None] * br - co_im[..., None] * bi
    bb_im = co_re[..., None] * bi + co_im[..., None] * br
    ug = u.reshape(bsz, L, SSM_GROUPS, SSM_GROUP)
    x_re = jnp.einsum('gpc,blgc->blgp', bb_re, ug)
    x_im = jnp.einsum('gpc,blgc->blgp', bb_im, ug)
    h0r, h0i = h0_re.astype(f32), h0_im.astype(f32)
    x_re = x_re.at[:, 0].add(ab_re * h0r - ab_im * h0i)
    x_im = x_im.at[:, 0].add(ab_re * h0i + ab_im * h0r)
    a_re = jnp.broadcast_to(ab_re, x_re.shape)
    a_im = jnp.broadcast_to(ab_im, x_im.shape)
    _, _, s_re, s_im = lax.associative_scan(_cplx_affine_combine, (a_re, a_im, x_re, x_im), axis=1)
    y = (jnp.einsum('gcp,blgp->blgc', c_re.astype(f32), s_re)
         - jnp.einsum('gcp,blgp->blgc', c_im.astype(f32), s_im))
    y = y.reshape(bsz, L, D_MODEL) + d_skip.astype(f32) * u
    gl = jax.nn.gelu(y).astype(h.dtype) @ w_glu
    ga, gb = jnp.split(gl, 2, axis=-1)
    out = (ga.astype(f32) * jax.nn.sigmoid(gb.astype(f32))).astype(h.dtype)
    return out, s_re[:, -1], s_im[:, -1]

def setup_inputs(seed: int = 0) -> dict:
    key = jax.random.key(seed)
    ks = iter(jax.random.split(key, 32))
    nrm = lambda shape, scale: jax.random.normal(next(ks), shape, jnp.float32) * scale
    x_prompt = nrm((BATCH, SEQ, D_MODEL), 1.0)
    x_sample = nrm((DEC_BATCH, DEC_SEQ, D_MODEL), 1.0)
    cache_sb_k = nrm((N_AB, DEC_BATCH, PAST_LEN, SB_HEADS, HEAD_DIM), 1.0)
    cache_sb_v = nrm((N_AB, DEC_BATCH, PAST_LEN, SB_HEADS, HEAD_DIM), 1.0)
    state_ssm_re = nrm((N_SSM, DEC_BATCH, SSM_GROUPS, SSM_STATE), 0.1)
    state_ssm_im = nrm((N_SSM, DEC_BATCH, SSM_GROUPS, SSM_STATE), 0.1)
    norm_mix = 1.0 + nrm((DEPTH, D_MODEL), 0.02)
    norm_ffn = 1.0 + nrm((DEPTH, D_MODEL), 0.02)
    norm_final = 1.0 + nrm((D_MODEL,), 0.02)
    ab_w_in = nrm((N_AB, D_MODEL, IN_WIDTH), D_MODEL ** -0.5)
    sgu_w = nrm((N_AB, SGU_GROUPS, SGU_CHUNK, SGU_CHUNK), SGU_CHUNK ** -0.5)
    sgu_b = 1.0 + nrm((N_AB, SGU_GROUPS, SGU_CHUNK), 0.02)
    ab_w_out = nrm((N_AB, MIX_WIDTH, D_MODEL), MIX_WIDTH ** -0.5)
    ssm_lam_re = -0.5 + nrm((N_SSM, SSM_GROUPS, SSM_STATE), 0.01)
    ssm_lam_im = jnp.pi * jnp.arange(SSM_STATE, dtype=jnp.float32) + nrm((N_SSM, SSM_GROUPS, SSM_STATE), 0.01)
    ssm_log_step = jax.random.uniform(next(ks), (N_SSM, SSM_GROUPS), jnp.float32,
                                      math.log(STEP_MIN), math.log(STEP_MAX))
    ssm_b_re = nrm((N_SSM, SSM_GROUPS, SSM_STATE, SSM_GROUP), (2 * SSM_GROUP) ** -0.5)
    ssm_b_im = nrm((N_SSM, SSM_GROUPS, SSM_STATE, SSM_GROUP), (2 * SSM_GROUP) ** -0.5)
    ssm_c_re = nrm((N_SSM, SSM_GROUPS, SSM_GROUP, SSM_STATE), SSM_STATE ** -0.5)
    ssm_c_im = nrm((N_SSM, SSM_GROUPS, SSM_GROUP, SSM_STATE), SSM_STATE ** -0.5)
    ssm_d = nrm((N_SSM, D_MODEL), 1.0)
    ssm_w_glu = nrm((N_SSM, D_MODEL, 2 * D_MODEL), D_MODEL ** -0.5)
    ffn_w_gate = nrm((DEPTH, D_MODEL, FFN_HIDDEN), D_MODEL ** -0.5)
    ffn_w_up = nrm((DEPTH, D_MODEL, FFN_HIDDEN), D_MODEL ** -0.5)
    ffn_w_down = nrm((DEPTH, FFN_HIDDEN, D_MODEL), FFN_HIDDEN ** -0.5)
    return {'x_prompt': x_prompt, 'x_sample': x_sample,
            'cache_sb_k': cache_sb_k, 'cache_sb_v': cache_sb_v,
            'state_ssm_re': state_ssm_re, 'state_ssm_im': state_ssm_im,
            'norm_mix': norm_mix, 'norm_ffn': norm_ffn, 'norm_final': norm_final,
            'ab_w_in': ab_w_in, 'sgu_w': sgu_w, 'sgu_b': sgu_b, 'ab_w_out': ab_w_out,
            'ssm_lam_re': ssm_lam_re, 'ssm_lam_im': ssm_lam_im, 'ssm_log_step': ssm_log_step,
            'ssm_b_re': ssm_b_re, 'ssm_b_im': ssm_b_im, 'ssm_c_re': ssm_c_re, 'ssm_c_im': ssm_c_im,
            'ssm_d': ssm_d, 'ssm_w_glu': ssm_w_glu,
            'ffn_w_gate': ffn_w_gate, 'ffn_w_up': ffn_w_up, 'ffn_w_down': ffn_w_down}

def reference(x_prompt, x_sample, cache_sb_k, cache_sb_v, state_ssm_re, state_ssm_im,
              norm_mix, norm_ffn, norm_final, ab_w_in, sgu_w, sgu_b, ab_w_out,
              ssm_lam_re, ssm_lam_im, ssm_log_step, ssm_b_re, ssm_b_im, ssm_c_re, ssm_c_im,
              ssm_d, ssm_w_glu, ffn_w_gate, ffn_w_up, ffn_w_down):
    xp, xs = x_prompt, x_sample
    k_p, v_p, k_s, v_s, g_s = [], [], [], [], []
    sr_p, si_p, sr_s, si_s = [], [], [], []
    for layer in range(DEPTH):
        i = layer // 2
        hp = rmsnorm(xp, norm_mix[layer])
        hs = rmsnorm(xs, norm_mix[layer])
        if layer % 2 == 0:
            mp, kp, vp = ab_mixer_prompt(hp, ab_w_in[i], sgu_w[i], sgu_b[i], ab_w_out[i])
            ms, kn, vn, gn = ab_mixer_sample(hs, cache_sb_k[i], cache_sb_v[i],
                                             ab_w_in[i], sgu_w[i], sgu_b[i], ab_w_out[i])
            k_p.append(kp); v_p.append(vp); k_s.append(kn); v_s.append(vn); g_s.append(gn)
        else:
            zeros = jnp.zeros((xp.shape[0], SSM_GROUPS, SSM_STATE), jnp.float32)
            mp, rp, ip = s5_mixer(hp, zeros, zeros, ssm_lam_re[i], ssm_lam_im[i], ssm_log_step[i],
                                  ssm_b_re[i], ssm_b_im[i], ssm_c_re[i], ssm_c_im[i], ssm_d[i], ssm_w_glu[i])
            ms, rs, is_ = s5_mixer(hs, state_ssm_re[i], state_ssm_im[i], ssm_lam_re[i], ssm_lam_im[i],
                                   ssm_log_step[i], ssm_b_re[i], ssm_b_im[i], ssm_c_re[i], ssm_c_im[i],
                                   ssm_d[i], ssm_w_glu[i])
            sr_p.append(rp); si_p.append(ip); sr_s.append(rs); si_s.append(is_)
        xp = xp + mp
        xs = xs + ms
        xp = xp + swiglu(rmsnorm(xp, norm_ffn[layer]), ffn_w_gate[layer], ffn_w_up[layer], ffn_w_down[layer])
        xs = xs + swiglu(rmsnorm(xs, norm_ffn[layer]), ffn_w_gate[layer], ffn_w_up[layer], ffn_w_down[layer])
    y_prompt = rmsnorm(xp, norm_final)
    y_sample = rmsnorm(xs, norm_final)
    return (y_prompt, y_sample,
            jnp.stack(k_p), jnp.stack(v_p), jnp.stack(k_s), jnp.stack(v_s), jnp.stack(g_s),
            jnp.stack(sr_p), jnp.stack(si_p), jnp.stack(sr_s), jnp.stack(si_s))


_drawn_inputs = setup_inputs


def setup_inputs(seed=0):
    import zlib

    import numpy as np

    out = dict(_drawn_inputs(seed))
    spreads = {}
    factors = {'norm_ffn': 3.106,
     'norm_final': 26.561,
     'sgu_b': 6.292,
     'ssm_lam_re': 53.012,
     'cache_sb_k': 3.997,
     'ssm_c_re': 22.891,
     'ssm_c_im': 22.201}
    for name, (base, spread) in spreads.items():
        noise = np.random.default_rng([zlib.crc32(name.encode()), seed]).standard_normal(out[name].shape)
        drawn = base * np.exp(spread * noise) if base else spread * noise
        out[name] = jnp.asarray(drawn.astype(out[name].dtype))
    for name, factor in factors.items():
        out[name] = (out[name] * factor).astype(out[name].dtype)
    return out
```

```python
from contextlib import ExitStack

import concourse.bass as bass
from concourse import mybir
from concourse.alu_op_type import AluOpType as ALU

F32 = mybir.dt.float32
F32R = mybir.dt.float32r
ACT = mybir.ActivationFunctionType

P = 128
D = 1024
KD = D // P
SEQ, DEC = 1024, 64
T = SEQ + DEC
TILES = [(i * P, min(P, T - i * P)) for i in range((T + P - 1) // P)]
CHUNKS = [(0, 384), (384, 384), (768, 320)]
NC = len(CHUNKS)
HD = 64
HEADS = 8
SB = HEADS * HD
PAST = 512
QT, KT, VT, UT, GT = 0, 4, 8, 12, 16
IN_TILES = 20
FF = 2816
PARTS = FF // (2 * P)
EPS = 1e-6
NEG = -1.0e30
GELU = ACT.Gelu_apprx_tanh
L = 8
NCH = T // L
CW = (L + 1) * 16
GP = 32
TWO_PI = 6.283185307179586
TURN = (6.28125, 0.0019350051879882812, 3.019916050e-07)
MAGIC = 12582912.0

SLAB_OUT = IN_TILES
SLAB_FF0 = SLAB_OUT + KD
PART_SLABS = 6
SLAB_GLU = SLAB_FF0 + PARTS * PART_SLABS
SLAB_FF1 = SLAB_GLU + 2 * KD
SLAB_END = SLAB_FF1 + PARTS * PART_SLABS
ACC_OUT = IN_TILES * NC
ACC_FF0 = ACC_OUT + KD * NC
ACC_FF1 = ACC_FF0 + PARTS * KD * NC
PAIR_GLU = 2 * PARTS * NC
PAIR_FF1 = PAIR_GLU + KD * NC


def slot(t):
    return t % 4 if t < SLAB_FF0 else (t - SLAB_FF0 + 4) % 6


def step(c, i, b):
    return c if i is None else c + i * b


def build(nc, A, O):
    with ExitStack() as ctx:
        sems = {}

        def sem(name):
            if name not in sems:
                sems[name] = ctx.enter_context(nc.semaphore(name))
            return sems[name]

        SIZE = 53200 * 4
        ctx.enter_context(nc.sbuf_tensor("arena", [P, SIZE // 4], F32))
        base = nc.sbuf_base - SIZE

        def plan(off, *specs):
            got = []
            for name, shape, dt in specs:
                n = 4
                for s in shape[1:]:
                    n *= s
                assert off + n <= SIZE, (name, off + n)
                got.append(nc.alloc_sbuf_tensor_at(name, shape, dt, offset=base + off))
                off += n
            return got + [off]

        ident, ones, cols, off = plan(0, ("ident", [P, P], F32), ("ones", [P, P], F32), ("cols", [P, 64], F32))
        abuf, fbuf, rms, off = plan(off, ("abuf", [P, 2, 384], F32), ("fbuf", [P, 2, 384], F32), ("rms", [P, 2, 384], F32))
        raw, off_w = plan(off, ("raw", [P, 2, D], F32))
        whi, wlo, off_h = plan(off_w, ("whi", [P, 6, D], F32R), ("wlo", [P, 6, D], F32R))
        hhi, hlo, off_x = plan(off_h, ("hhi", [P, KD * T], F32R), ("hlo", [P, KD * T], F32R))
        x, off_g = plan(off_x, ("x", [P, KD * T], F32))
        gh, gl, off_end = plan(off_g, ("gh", [P, 4 * T], F32R), ("gl", [P, 4 * T], F32R))
        xin, nrow, _ = plan(off_g, ("xin", [P, 2, D], F32), ("nrow", [P, P], F32))
        zst, _ = plan(off_g, ("zst", [P, 2, T], F32))
        zt, tok, wsr, wsT, bT, ug, mg, tri0, _ = plan(
            off_x, ("zt", [P, 2, T], F32), ("tok", [P, 2, 9, P], F32), ("wsr", [P, 8, P], F32), ("wsT", [P, 8, P], F32),
            ("bT", [P, 4, P], F32), ("ug", [P, 2, T], F32), ("mg", [P, 2, 384], F32), ("tri0", [P, P], F32))
        KCOL = T + 64 + PAST
        kS, qS, kq, vS, vr, tri, comp, ww, oa = plan(
            off_x, ("kS", [P, 2, KCOL], F32R),
            ("qS", [P, 2, 2, T], F32R),
            ("kq", [P, 2, T + PAST], F32), ("vS", [P, 2, 13, P], F32R), ("vr", [P, 13, HD], F32),
            ("tri", [P, P], F32R), ("comp", [P, P], F32R),
            ("ww", [P, 2, 2, 512], F32R))
        assert oa <= off_end
        ebuf, tbuf, _ = plan(off_w + 2 * D * 4, ("ebuf", [P, 2, 2, 512], F32), ("tbuf", [P, 2, 2, 512], F32))
        sphi, splo, _ = plan(off_w + 8 * D * 4, ("sphi", [P, 2, 2, 512], F32R), ("splo", [P, 2, 2, 512], F32R))

        eb, bo, co_, pb, _ = plan(off_x, ("eb", [P, 3, 8, NCH], F32), ("bo", [P, 8, 2, P], F32), ("co", [P, 8, 2, CW], F32),
                                  ("pb", [P, 2, GP, L], F32))
        assert _ <= off_g
        ct, bb, pc, sc, ek, par, pp, off_t, = plan(
            off_g + 2 * T * 4, ("ct", [P, 2, GP, 16], F32), ("bb", [P, 2, GP, 16], F32), ("pc", [P, 2, GP, L + 1], F32),
            ("sc", [P, 20, GP], F32), ("ek", [P, 2, GP, 7], F32), ("par", [P, 5, GP], F32), ("pp", [P, 4, GP], F32))
        t1, t2, _ = plan(off_t, ("t1", [P, 8 * CW], F32), ("t2", [P, 8 * CW], F32))
        assert _ <= off_end
        lt, craw, lstep, _ = plan(off_t, ("lt", [P, 5, P], F32), ("craw", [P, 2, 8, 64], F32), ("lstep", [P, 2], F32))
        (S_step, S_mag, S_lrs, S_r8, S_sin, S_cos, S_ang, S_k, S_r, S_rc, S_a, S_b, S_c, S_nr, S_cor, S_coi, *S_ef) = (
            sc[:, n, :] for n in range(20))
        S_e, S_f = S_ef[0:2], S_ef[2:4]
        rr, rs, br, bt, _ = plan(off_w, ("rr", [P, 8, P], F32), ("rs", [P, 8, P], F32), ("br", [P, 4, 2, P], F32), ("bt", [P, 4, 2, P], F32))
        tm, kt, rp, _ = plan(off_w + 6 * D * 4, ("tm", [P, 2, 8, P], F32), ("kt", [P, 8, P], F32), ("rp", [P, L, P], F32))
        u, ca, sh, yy, p4, _ = plan(off_h, ("u", [P, 2, 8, NCH], F32), ("ca", [P, 2, 4, 2, CW], F32), ("sh", [P, 2, 2, 4, NCH], F32),
                                    ("yy", [P, 8, NCH], F32), ("p4", [P, 4, GP], F32))
        yp, _ = plan(off_h + KD * T * 4, ("yp", [P, KD * T], F32))
        e3, xx, v1, v2, v3, w1, w2, rps, _ = plan(
            off_x, ("e3", [P, 3, 4, NCH], F32), ("xx", [P, 8 * NCH], F32), ("v1", [P, 4 * NCH], F32), ("v2", [P, 4 * NCH], F32),
            ("v3", [P, 4 * NCH], F32), ("w1", [P, 4 * NCH], F32), ("w2", [P, 4 * NCH], F32), ("rps", [P, L, P], F32))
        v1, v2, v3, w1, w2 = v1[:], v2[:], v3[:], w1[:], w2[:]
        hp, _ = plan(off_g, ("hp", [P, KD * T], F32))
        fin, fout, _ = plan(off_w - 2 * D * 4 - 3072, ("fin", [P, 4, GP], F32), ("fout", [P, 4, P], F32))
        yf, _ = plan(off_h, ("yf", [P, KD * T], F32))
        yo, _ = plan(off_g, ("yo", [P, 2, D], F32))

        ps = ctx.enter_context(nc.psum_tensor("ps", [P, 8, 512], F32))

        zT = nc.dram_tensor("zT", [IN_TILES * P, T], F32).ap()
        kcT = nc.dram_tensor("kcT", [SB, PAST], F32).ap()
        dE = nc.dram_tensor("dE", [P, 3, GP, NCH], F32).ap()
        dB = nc.dram_tensor("dB", [P, GP, 2, P], F32).ap()
        dC = nc.dram_tensor("dC", [P, GP, 2, CW], F32).ap()
        dP = nc.dram_tensor("dP", [P, 4, GP], F32).ap()
        xs = nc.dram_tensor("xs", [P, KD * T], F32).ap()

        xp = A["x_prompt"].rearrange("b t d -> (b t) d")
        xd = A["x_sample"].rearrange("b t d -> (b t) d")

        x3 = x[:].rearrange("p (f t) -> p f t", f=KD)
        epsb = cols[:, 48:49]
        dmask, dneg = rms[:, 0, 0:P], rms[:, 1, 0:P]

        def kview(w):
            return w.rearrange("(k p) n -> p k n", p=P)

        w_in, w_out = kview(A["ab_w_in"][0]), kview(A["ab_w_out"][0])
        w_gate = [kview(A["ffn_w_gate"][l]) for l in range(2)]
        w_up = [kview(A["ffn_w_up"][l]) for l in range(2)]
        w_down = [A["ffn_w_down"][l] for l in range(2)]
        w_glu = kview(A["ssm_w_glu"][0])
        k_new = [O["k_p"].rearrange("a b t h d -> (a b t) (h d)"), O["k_s"].rearrange("a b t h d -> (a b t) (h d)")]
        v_new = [O["v_p"].rearrange("a b t h d -> (a b t) (h d)"), O["v_s"].rearrange("a b t h d -> (a b t) (h d)")]
        g_new = O["g_s"].rearrange("a b t d -> (a b t) d")
        y_new = [O["y_p"].rearrange("b t d -> (b t) d"), O["y_s"].rearrange("b t d -> (b t) d")]
        ck = A["cache_sb_k"].rearrange("a b t h d -> (a b t) (h d)")
        cv = A["cache_sb_v"].rearrange("a b t h d -> (a b t) (h d)")

        def xcol(m, c, buf=x):
            s, n = CHUNKS[c]
            return buf[:, bass.ds(m * T + s, n)]

        def load_slab(sp, t, src, i=None, b=0):
            if t >= 2:
                sp.wait_ge(sem("w_lo"), step(t - 1, i, b))
            dst = raw[:, t % 2, :]
            if len(src.shape) == 3:
                dst = dst.rearrange("p (k n) -> p k n", k=KD)
            sp.dma_start(dst, src).then_inc(sem(f"raw_loaded{t % 2}"), 16)

        def slab_hi(act, t, left=None, count=0, i=None, b=0, per=0):
            act.wait_ge(sem(f"raw_loaded{t % 2}"), step(16 * (t // 2 + 1), i, 8 * b))
            if left:
                act.wait_ge(sem(left), step(count, i, per))
            act.activation(whi[:, slot(t), :], raw[:, t % 2, :], ACT.Copy).then_inc(sem("w_hi"), 1)

        def slab_lo(pool, t, i=None, b=0):
            pool.wait_ge(sem("w_hi"), step(t + 1, i, b))
            pool.tensor_tensor(wlo[:, slot(t), :], raw[:, t % 2, :], whi[:, slot(t), :].bitcast(F32),
                               ALU.subtract).then_inc(sem("w_lo"), 1)

        def three(pe, out, s, col, rh, rl, first, last):
            wh, wl = whi[:, s, col:col + P], wlo[:, s, col:col + P]
            pe.matmul(out, wh, rh, start=first, stop=False)
            pe.matmul(out, wh, rl, start=False, stop=False)
            return pe.matmul(out, wl, rh, start=False, stop=last)

        def eight(pe, out, s, c):
            s0, n = CHUNKS[c]
            for k in range(KD):
                o = k * T + s0
                mm = three(pe, out[:, 0:n], s, k * P, hhi[:, o:o + n], hlo[:, o:o + n], k == 0, k == KD - 1)
            return mm

        def acc(v):
            return ps[:, 4 + v % 4, :]

        def pe_single(pe, t, i=None, b=0, ready=None):
            pe.wait_ge(sem("w_lo"), step(t + 1, i, b))
            for c in range(NC):
                v = NC * t + c
                if ready:
                    ready(c)
                if v >= 4:
                    pe.wait_ge(sem("acc_used"), step(v - 3, i, NC * b))
                eight(pe, acc(v), slot(t), c).then_inc(sem("acc_ready"), 1)

        def pe_pair(pe, t, v0, i=None, b=0, per=0, ready=None):
            pe.wait_ge(sem("w_lo"), step(t + 2, i, b))
            for c in range(NC):
                v = v0 + c
                if ready:
                    ready(c)
                if v >= 2:
                    pe.wait_ge(sem("pair_used"), step(v - 1, i, per))
                eight(pe, ps[:, 2 * (v % 2), :], slot(t), c)
                eight(pe, ps[:, 2 * (v % 2) + 1, :], slot(t + 1), c).then_inc(sem("pair_ready"), 1)

        SPLIT = {0: 0, 1: 1, 3: 2}

        def n_units(k, e=NC * KD):
            return NC * KD * k + e

        def n_split(k, e=NC * KD):
            return NC * KD * SPLIT[k] + e

        def norm_act(act, k, xin_ready, split, hlast=None):
            def squares(c):
                s, n = CHUNKS[c]
                xin_ready(act, c)
                for f in range(KD):
                    e = c * KD + f
                    if e >= 2:
                        act.wait_ge(sem("n_sum"), n_units(k, e - 1))
                    act.activation(abuf[:, e % 2, 0:n], x[:, f * T + s:f * T + s + n], ACT.Square).then_inc(sem("n_sq"), 1)

            def root(c):
                n = CHUNKS[c][1]
                act.wait_ge(sem("n_sum"), n_units(k, KD * (c + 1)))
                if c >= 2:
                    act.wait_ge(sem("n_f"), n_units(k, KD * (c - 1)))
                act.activation(rms[:, c % 2, 0:n], ps[:, c, 0:n], ACT.Sqrt, bias=epsb[:, 0:1], scale=1.0 / D).then_inc(sem("n_rt"), 1)

            def his(c):
                s, n = CHUNKS[c]
                for f in range(KD):
                    e = c * KD + f
                    act.wait_ge(sem("n_f"), n_units(k, e + 1))
                    act.activation(hhi[:, f * T + s:f * T + s + n], fbuf[:, e % 2, 0:n], ACT.Copy).then_inc(sem("n_hi"), 1)

            squares(0)
            root(0)
            squares(1)
            root(1)
            squares(2)
            if split:
                his(0)
            root(2)
            if split:
                his(1)
                his(2)

        def norm_pe(pe, k):
            pe.wait_ge(sem("consts"), 1)
            for c, (s, n) in enumerate(CHUNKS):
                for f in range(KD):
                    pe.wait_ge(sem("n_sq"), n_units(k, c * KD + f + 1))
                    pe.matmul(ps[:, c, 0:n], ones[:], abuf[:, (c * KD + f) % 2, 0:n], start=f == 0,
                              stop=f == KD - 1).then_inc(sem("n_sum"), 1)

        def norm_dve(dve, k, row, plain=None):
            for c, (s, n) in enumerate(CHUNKS):
                dve.wait_ge(sem("n_rt"), NC * k + c + 1)
                dve.reciprocal(rms[:, c % 2, 0:n], rms[:, c % 2, 0:n]).then_inc(sem("n_rr"), 1)
                dve.wait_ge(sem("n_rr"), NC * k + c + 1)
                for f in range(KD):
                    e = c * KD + f
                    out = fbuf[:, e % 2, 0:n]
                    if plain is not None:
                        out = plain[:, f * T + s:f * T + s + n]
                    elif e >= 2:
                        dve.wait_ge(sem("n_lo"), n_split(k, e - 1))
                    dve.scalar_tensor_tensor(out, x[:, f * T + s:f * T + s + n], cols[:, row + f:row + f + 1],
                                             rms[:, c % 2, 0:n], ALU.mult, ALU.mult).then_inc(sem("n_f"), 1)

        def norm_pool(pool, k):
            for c, (s, n) in enumerate(CHUNKS):
                for f in range(KD):
                    e = c * KD + f
                    o = f * T + s
                    pool.wait_ge(sem("n_hi"), n_split(k, e + 1))
                    pool.tensor_tensor(hlo[:, o:o + n], fbuf[:, e % 2, 0:n], hhi[:, o:o + n].bitcast(F32),
                                       ALU.subtract).then_inc(sem("n_lo"), 1)

        def h_ready(k):
            return lambda eng: (lambda c: eng.wait_ge(sem("n_lo"), n_split(k, KD * (c + 1))))

        class Ffn:
            def __init__(self, layer):
                self.l = layer
                self.slab = (SLAB_FF0, SLAB_FF1)[layer]
                self.pair = (0, PAIR_FF1)[layer]
                self.acc = (ACC_FF0, ACC_FF1)[layer]
                self.hid = (0, 2 * PARTS * NC)[layer]
                self.norm = (1, 3)[layer]

        F = [Ffn(0), Ffn(1)]

        def ffn_sp(sp, f, skip=0):
            def gu(tile, t, i=None):
                o = step(tile * P, i, 2 * P)
                for w, tt in ((w_gate[f.l], t), (w_up[f.l], t + 1)):
                    load_slab(sp, tt, w[:, :, bass.ds(o, P)] if i is not None else w[:, :, o:o + P], i, 6)

            def down(tile, t, i=None):
                for j in range(2):
                    o = step((tile + j) * P, i, 2 * P)
                    load_slab(sp, t + j, w_down[f.l][bass.ds(o, P), :] if i is not None else w_down[f.l][o:o + P, :], i, 6)

            if not skip:
                gu(0, f.slab)
                return
            gu(1, f.slab + 2)
            with sp.Fori(0, PARTS - 1) as i:
                gu(2, f.slab + 4, i)
                gu(3, f.slab + 6, i)
                down(0, f.slab + 8, i)
            down(2 * PARTS - 2, f.slab + 64)

        def ffn_act(act, f, start_sem, start_count):
            def silu(v0, i=None):
                for c, (s, n) in enumerate(CHUNKS):
                    v = v0 + c
                    act.wait_ge(sem("pair_ready"), step(v + 1, i, 6))
                    if v >= 2:
                        act.wait_ge(sem("pair_used"), step(v - 1, i, 6))
                    act.activation(abuf[:, v % 2, 0:n], ps[:, 2 * (v % 2), 0:n], ACT.Silu).then_inc(sem("pair_act"), 1)

            for q in range(2):
                for j in range(2):
                    slab_hi(act, f.slab + 2 * q + 2 + j, start_sem, start_count)
                silu(f.pair + NC * q)
            with act.Fori(0, PARTS - 1) as i:
                t = f.slab + 4
                for j in range(2):
                    slab_hi(act, t + 2 + j, "pair_ready", f.pair + 2 * NC, i, 6, 6)
                silu(f.pair + 2 * NC, i)
                for j in range(2):
                    slab_hi(act, t + 4 + j, "acc_ready", f.acc, i, 6, KD * NC)
                silu(f.pair + 3 * NC, i)
                for j in range(2):
                    slab_hi(act, t + 6 + j, "pair_ready", f.pair + 3 * NC, i, 6, 6)
            if f.l == 0:
                for j in range(2):
                    slab_hi(act, SLAB_GLU + j, "pair_ready", PAIR_GLU)

        def ffn_pool(pool, f):
            def lo(v0, half, i=None):
                for c, (s, n) in enumerate(CHUNKS):
                    v, h = v0 + c, f.hid + v0 - f.pair + c
                    o = (half if i is None else ((i + 1) % 2) * (2 * T) + half) + s
                    pool.wait_ge(sem("hid_hi"), step(h + 1, i, 6))
                    pool.tensor_tensor(gl[:, bass.ds(o, n)], fbuf[:, v % 2, 0:n], gh[:, bass.ds(o, n)].bitcast(F32),
                                       ALU.subtract).then_inc(sem("hid_lo"), 1)

            for q in range(2):
                for j in range(2):
                    slab_lo(pool, f.slab + 2 * q + 2 + j)
                lo(f.pair + NC * q, q * T)
            with pool.Fori(0, PARTS - 1) as i:
                t = f.slab + 4
                for q in range(2):
                    for j in range(2):
                        slab_lo(pool, t + 2 * q + 2 + j, i, 6)
                    lo(f.pair + (2 + q) * NC, q * T, i)
                for j in range(2):
                    slab_lo(pool, t + 6 + j, i, 6)
            if f.l == 0:
                for j in range(2):
                    slab_lo(pool, SLAB_GLU + j)

        def ffn_pe(pe, f):
            def down(t, v0, h0, i=None, buf=None):
                buf = (i % 2) * (2 * T) if buf is None else buf
                pe.wait_ge(sem("w_lo"), step(t + 2, i, 6))
                for c, (s, n) in enumerate(CHUNKS):
                    pe.wait_ge(sem("hid_lo"), step(h0 + c + 1, i, 6))
                    for m in range(KD):
                        v = v0 + c * KD + m
                        pe.wait_ge(sem("acc_used"), step(v - 3, i, KD * NC))
                        for j in range(2):
                            o = buf + j * T + s
                            mm = three(pe, acc(v)[:, 0:n], slot(t + j), m * P, gh[:, bass.ds(o, n)], gl[:, bass.ds(o, n)],
                                       j == 0, j == 1)
                        mm.then_inc(sem("acc_ready"), 1)

            pe_pair(pe, f.slab, f.pair, ready=h_ready(f.norm)(pe))
            pe_pair(pe, f.slab + 2, f.pair + NC)
            with pe.Fori(0, PARTS - 1) as i:
                pe_pair(pe, f.slab + 4, f.pair + 2 * NC, i, 6, 6)
                pe_pair(pe, f.slab + 6, f.pair + 3 * NC, i, 6, 6)
                down(f.slab + 8, f.acc, f.hid + NC, i)
            down(f.slab + 64, f.acc + (PARTS - 1) * KD * NC, f.hid + NC * (2 * PARTS - 1), buf=((PARTS - 1) % 2) * 2 * T)

        def ffn_dve(dve, f):
            def hidden(v0, half, i=None):
                for c, (s, n) in enumerate(CHUNKS):
                    v, h = v0 + c, f.hid + v0 - f.pair + c
                    o = (half if i is None else ((i + 1) % 2) * (2 * T) + half) + s
                    dve.wait_ge(sem("pair_act"), step(v + 1, i, 6))
                    if h >= 2:
                        dve.wait_ge(sem("hid_lo"), step(h - 1, i, 6))
                    dve.tensor_tensor(fbuf[:, v % 2, 0:n], ps[:, 2 * (v % 2) + 1, 0:n], abuf[:, v % 2, 0:n],
                                      ALU.mult).then_inc(sem("pair_used"), 1)
                    dve.wait_ge(sem("pair_used"), step(v + 1, i, 6))
                    dve.tensor_copy(gh[:, bass.ds(o, n)], fbuf[:, v % 2, 0:n]).then_inc(sem("hid_hi"), 1)

            def residual(v0, i=None):
                for c, (s, n) in enumerate(CHUNKS):
                    for m in range(KD):
                        v = v0 + c * KD + m
                        dve.wait_ge(sem("acc_ready"), step(v + 1, i, KD * NC))
                        xo = x[:, m * T + s:m * T + s + n]
                        dve.tensor_tensor(xo, acc(v)[:, 0:n], xo, ALU.add).then_inc(sem("acc_used"), 1)

            dve.wait_ge(sem("n_lo"), n_split(f.norm))
            hidden(f.pair, 0)
            hidden(f.pair + NC, T)
            with dve.Fori(0, PARTS - 1) as i:
                hidden(f.pair + 2 * NC, 0, i)
                hidden(f.pair + 3 * NC, T, i)
                residual(f.acc, i)
            residual(f.acc + (PARTS - 1) * KD * NC)

        def zrow(n):
            return (KT + n if n < 8 else GT + n - 12) * P

        tp_units = [(n, b) for n in range(16) for b in range(1 if 8 <= n < 12 else NC)]
        tp_no = {nb: u for u, nb in enumerate(tp_units)}
        TP_V = sum(n < 12 for n, _ in tp_units)

        def tp_taken(eng, u):
            if u < TP_V:
                eng.wait_ge(sem("tp_used_v"), u + 1)
            else:
                eng.wait_ge(sem("tp_used_a"), u + 1 - TP_V)

        def tr_sp(sp):
            for n in range(3):
                sp.wait_ge(sem(f"prep_out{n}"), 64)
            sp.wait_ge(sem("z_stored0"), 16 * IN_TILES // 2)
            sp.wait_ge(sem("z_stored1"), 16 * IN_TILES // 2)
            sp.dma_start(wsr[:], A["sgu_w"][0].rearrange("g t s -> t g s")).then_inc(sem("ws_loaded"), 16)
            for j in range(4):
                for a in range(2):
                    sp.dma_start(bT[64 * a:64 * a + 64, j, :], A["sgu_b"][0, 2 * j + a:2 * j + a + 1, :].to_broadcast([64, P])
                                 ).then_inc(sem("bT_loaded"), 16)
            for n in range(17):
                if n < 16:
                    if n >= 2:
                        sp.wait_ge(sem("tp_mm"), tp_no[(n - 1, 0)])
                    if 8 <= n < 12:
                        sp.dma_start(zt[:, n % 2, 0:512].rearrange("p (b n) -> p b n", b=4),
                                     ck[:, (n - 8) * P:(n - 7) * P].rearrange("(b p) n -> p b n", p=P)).then_inc(sem(f"zt_loaded{n % 2}"), 16)
                    else:
                        sp.dma_start(zt[:, n % 2, :], zT[zrow(n):zrow(n) + P, :]).then_inc(sem(f"zt_loaded{n % 2}"), 16)
                    if n >= 12:
                        j = n - 12
                        if j >= 2:
                            sp.wait_ge(sem("mix_f"), 2 * NC * (j - 1))
                        sp.dma_start(ug[:, j % 2, :], zT[(UT + j) * P:(UT + j + 1) * P, :]).then_inc(sem(f"ug_loaded{j % 2}"), 16)
                if n >= 1:
                    m = n - 1
                    tp_taken(sp, tp_no[(m, 0 if 8 <= m < 12 else 2)])
                    cs = slice((m % 4) * P, (m % 4 + 1) * P)
                    if m < 8:
                        dst = (k_new, v_new)[m // 4]
                        sp.dma_start(dst[0][:, cs].rearrange("(t p) n -> p t n", p=P), tok[:, m % 2, 0:8, :]).then_inc(sem(f"tok_out{m % 2}"), 16)
                        sp.dma_start(dst[1][:, cs], tok[0:DEC, m % 2, 8, :]).then_inc(sem(f"tok_out{m % 2}"), 16)
                    elif m < 12:
                        sp.dma_start(kcT[cs, :], tok[:, m % 2, 0:4, :].rearrange("p b n -> p (b n)")).then_inc(sem(f"tok_out{m % 2}"), 16)
                    else:
                        sp.dma_start(g_new[:, cs], tok[0:DEC, m % 2, 8, :]).then_inc(sem(f"tok_out{m % 2}"), 16)

        def tok_free(eng, n):
            if n >= 2:
                done = sum((32 if m < 8 else 16) for m in range(n - 1) if m % 2 == n % 2)
                eng.wait_ge(sem(f"tok_out{n % 2}"), done)
            if n >= 14:
                eng.wait_ge(sem("mix_mm"), NC * (n - 13))

        def tr_pe(pe):
            pe.wait_ge(sem("ws_loaded"), 16)
            pe.wait_ge(sem("acc_used"), NC * IN_TILES)
            for g in range(8):
                mm = pe.transpose(ps[:, 6 + g // 4, (g % 4) * P:(g % 4 + 1) * P], wsr[:, g, :], ident[:])
            mm.then_inc(sem("ws_mm"), 1)
            for u, (n, b) in enumerate(tp_units):
                if b == 0:
                    pe.wait_ge(sem(f"zt_loaded{n % 2}"), 16 * (n // 2 + 1))
                if u >= 6:
                    tp_taken(pe, u - 6)
                for r in range(4 if 8 <= n < 12 else 3):
                    if 8 <= n < 12:
                        mm = pe.transpose(ps[:, u % 6, r * P:(r + 1) * P], zt[:, n % 2, r * P:(r + 1) * P], ident[:])
                    else:
                        s, w = TILES[3 * b + r]
                        mm = pe.transpose(ps[0:w, u % 6, r * P:(r + 1) * P], zt[:, n % 2, s:s + w], ident[:])
                mm.then_inc(sem("tp_mm"), 1)
                if n >= 12 and b == 2:
                    gate_pe(pe, n - 12)

        def gate_pe(pe, j):
            tp_taken(pe, tp_no[(12 + j, 2)])
            pe.wait_ge(sem("ws_t"), 8)
            for c in range(NC):
                s = NC * j + c
                if s >= 2:
                    pe.wait_ge(sem("mix_f"), 2 * (s - 1) - 1)
                for r in range(3):
                    w = TILES[3 * c + r][1]
                    for a in range(2):
                        mm = pe.matmul(ps[64 * a:64 * a + 64, 6 + s % 2, r * P:r * P + w],
                                       tok[0:w, (12 + j) % 2, 3 * c + r, 64 * a:64 * a + 64], wsT[0:w, 2 * j + a, 0:w],
                                       start=True, stop=True, skip_group_check=True)
                mm.then_inc(sem("mix_mm"), 1)

        def tr_dve(dve):
            dve.wait_ge(sem("ws_mm"), 1)
            dve.wait_ge(sem("tri0_made"), 1)
            for g in range(8):
                dve.tensor_tensor(wsT[:, g, :], ps[:, 6 + g // 4, (g % 4) * P:(g % 4 + 1) * P], tri0[:], ALU.mult).then_inc(sem("ws_t"), 1)
            for u, (n, b) in enumerate(tp_units[:TP_V]):
                if b == 0:
                    tok_free(dve, n)
                dve.wait_ge(sem("tp_mm"), u + 1)
                if 8 <= n < 12:
                    dve.tensor_copy(tok[:, n % 2, 0:4, :], ps[:, u % 6, 0:512].rearrange("p (b n) -> p b n", b=4)).then_inc(sem("tp_used_v"), 1)
                elif b < 2:
                    dve.tensor_copy(tok[:, n % 2, 3 * b:3 * b + 3, :], ps[:, u % 6, 0:384].rearrange("p (b n) -> p b n", b=3)
                                    ).then_inc(sem("tp_used_v"), 1)
                else:
                    dve.tensor_copy(tok[0:DEC, n % 2, 8, :], ps[0:DEC, u % 6, 256:384]).then_inc(sem("tp_part"), 1)
                    dve.wait_ge(sem("tp_part"), sum(1 for m, bb in tp_units[:u + 1] if bb == 2))
                    dve.tensor_copy(tok[:, n % 2, 6:8, :], ps[:, u % 6, 0:256].rearrange("p (b n) -> p b n", b=2)).then_inc(sem("tp_used_v"), 1)
            dve.wait_ge(sem("bT_loaded"), 16 * 8)
            for s in range(4 * NC):
                j, c = divmod(s, NC)
                s0, n = CHUNKS[c]
                dve.wait_ge(sem("mix_mm"), s + 1)
                if s >= 2:
                    dve.wait_ge(sem("mix_lo"), s - 1)
                for r in range(3):
                    w = TILES[3 * c + r][1]
                    ins = dve.tensor_tensor(mg[:, s % 2, r * P:r * P + w], ps[:, 6 + s % 2, r * P:r * P + w], bT[:, j, 0:w], ALU.add)
                    ins.then_inc(sem("mix_f" if r == 2 else "mix_part"), 1)
                dve.wait_ge(sem("mix_f"), 2 * s + 1)
                dve.wait_ge(sem("mix_part"), 2 * s + 2)
                dve.wait_ge(sem("ug_act"), j + 1)
                dve.tensor_tensor(mg[:, s % 2, 0:n], mg[:, s % 2, 0:n], ug[:, j % 2, s0:s0 + n], ALU.mult).then_inc(sem("mix_f"), 1)

        def tr_act(act):
            for j in range(4):
                n = 12 + j
                act.wait_ge(sem(f"ug_loaded{j % 2}"), 16 * (j // 2 + 1))
                act.activation(ug[:, j % 2, :], ug[:, j % 2, :], GELU).then_inc(sem("ug_act"), 1)
                tok_free(act, n)
                for b in range(NC):
                    u = tp_no[(n, b)]
                    act.wait_ge(sem("tp_mm"), u + 1)
                    if b < 2:
                        act.activation(tok[:, n % 2, 3 * b:3 * b + 3, :], ps[:, u % 6, 0:384].rearrange("p (b n) -> p b n", b=3), GELU
                                       ).then_inc(sem("tp_used_a"), 1)
                    else:
                        act.activation(tok[0:DEC, n % 2, 8, :], ps[0:DEC, u % 6, 256:384], GELU).then_inc(sem("tp_part_a"), 1)
                        act.wait_ge(sem("tp_part_a"), j + 1)
                        act.activation(tok[:, n % 2, 6:8, :], ps[:, u % 6, 0:256].rearrange("p (b n) -> p b n", b=2), GELU
                                       ).then_inc(sem("tp_used_a"), 1)
                for c in range(NC):
                    s = NC * j + c
                    s0, w = CHUNKS[c]
                    act.wait_ge(sem("mix_f"), 2 * s + 2)
                    o = (4 + j) * T + s0
                    act.activation(hhi[:, o:o + w], mg[:, s % 2, 0:w], ACT.Copy).then_inc(sem("mix_hi"), 1)

        def tr_pool(pool):
            for n in range(3):
                pool.wait_ge(sem(f"prep_out{n}"), 64)
            pool.wait_ge(sem("p_out"), 16)
            pool.wait_ge(sem("z_stored0"), 16 * IN_TILES // 2)
            pool.wait_ge(sem("z_stored1"), 16 * IN_TILES // 2)
            pool.memset(tri0[:], 1.0).then_inc(sem("pool"), 1)
            pool.wait_ge(sem("pool"), POOL0 + 1)
            pool.affine_select(out=tri0[:], in_=tri0[:], compare_op=ALU.is_ge, fill=0.0, base=0, pattern=[[1, P]],
                               channel_multiplier=-1).then_inc(sem("tri0_made"), 1)
            for s in range(4 * NC):
                j, c = divmod(s, NC)
                s0, w = CHUNKS[c]
                o = (4 + j) * T + s0
                pool.wait_ge(sem("mix_hi"), s + 1)
                pool.tensor_tensor(hlo[:, o:o + w], mg[:, s % 2, 0:w], hhi[:, o:o + w].bitcast(F32), ALU.subtract).then_inc(sem("mix_lo"), 1)

        units = []
        for pr in range(HEADS // 2):
            for q0, w, blocks in ((0, 512, range(3, -1, -1)), (512, 512, range(7, -1, -1)), (SEQ, DEC, range(4, -1, -1))):
                blocks = list(blocks)
                for b in blocks:
                    if q0 < SEQ:
                        off = max(0, b * P - q0)
                        units.append(dict(pr=pr, q0=q0, off=off, w=w - off, kc=b * P, vb=b, diag=b * P >= q0))
                    else:
                        units.append(dict(pr=pr, q0=q0, off=0, w=w, kc=SEQ if b == 4 else T + 64 + b * P,
                                          vb=8 if b == 4 else 9 + b, diag=b == 4))
                    units[-1].update(first=b == blocks[0], last=b == blocks[-1], total=w)
        NU = len(units)
        PAIR_U = NU // (HEADS // 2)
        group_no = {i: sum(v["last"] for v in units[:i]) for i in range(NU)}
        diags = [sum(v["diag"] for v in units[:i]) for i in range(NU + 1)]

        def at_sp(sp):
            sp.wait_ge(sem("mix_lo"), 4 * NC)
            sp.wait_ge(sem("tok_out0"), sum((32 if m < 8 else 16) for m in range(0, 16, 2)))
            sp.wait_ge(sem("tok_out1"), sum((32 if m < 8 else 16) for m in range(1, 16, 2)))
            sp.wait_ge(sem("at_made"), 2)
            for g in range(HEADS):
                if g:
                    sp.wait_ge(sem("k_lo"), 2 * g)
                kr = slice((KT * P + g * HD), (KT * P + g * HD + HD))
                for a in range(2):
                    sp.dma_start(kq[64 * a:64 * a + 64, 0, 0:T], zT[kr, :]).then_inc(sem("k_loaded"), 16)
                    sp.dma_start(kq[64 * a:64 * a + 64, 0, T:T + PAST], kcT[g * HD:g * HD + HD, :]).then_inc(sem("k_loaded"), 16)
                if g:
                    sp.wait_ge(sem("q_lo"), 2 * g)
                for a in range(2):
                    sp.dma_start(kq[64 * a:64 * a + 64, 1, 0:T], zT[g * HD:g * HD + HD, :]).then_inc(sem("q_loaded"), 16)
                if g:
                    sp.wait_ge(sem("v_lo"), g)
                cs = slice(g * HD, g * HD + HD)
                sp.dma_start(vr[:, 0:8, :], v_new[0][:, cs].rearrange("(t p) n -> p t n", p=P)).then_inc(sem("v_loaded"), 16)
                sp.dma_start(vr[0:DEC, 8, :], v_new[1][:, cs]).then_inc(sem("v_loaded"), 16)
                sp.dma_start(vr[:, 9:13, :], cv[:, cs].rearrange("(t p) n -> p t n", p=P)).then_inc(sem("v_loaded"), 16)
            sp.wait_ge(sem("u_pv"), NU)
            sp.wait_ge(sem("o_lo"), 12)
            sp.dma_start(x[:], xs).then_inc(sem("x_back"), 16)

        def at_pool_make(pool):
            pool.wait_ge(sem("mix_lo"), 4 * NC)
            pool.wait_ge(sem("tok_out0"), sum((32 if m < 8 else 16) for m in range(0, 16, 2)))
            pool.wait_ge(sem("tok_out1"), sum((32 if m < 8 else 16) for m in range(1, 16, 2)))
            pool.memset(vr[:, 8, :], 0.0).then_inc(sem("pool"), 1)
            pool.memset(kS[:, :, T:T + 64].bitcast(F32), 0.0).then_inc(sem("pool"), 1)
            pool.memset(dmask, 1.0).then_inc(sem("pool"), 1)
            pool.memset(dneg, 0.0).then_inc(sem("pool"), 1)
            pool.memset(ebuf[:, 0, 0, 0:P], 1.0).then_inc(sem("pool"), 1)
            pool.memset(ebuf[:, 0, 1, 0:P], 1.0).then_inc(sem("pool"), 1)
            pool.wait_ge(sem("pool"), POOL0 + 7)
            pool.affine_select(out=dmask, in_=dmask, compare_op=ALU.is_gt, fill=0.0, base=0, pattern=[[1, P]],
                               channel_multiplier=-1).then_inc(sem("pool"), 1)
            pool.affine_select(out=dneg, in_=dneg, compare_op=ALU.is_gt, fill=NEG, base=0, pattern=[[1, P]],
                               channel_multiplier=-1).then_inc(sem("pool"), 1)
            pool.affine_select(out=ebuf[:, 0, 0, 0:P], in_=ebuf[:, 0, 0, 0:P], compare_op=ALU.is_ge, fill=0.0, base=0,
                               pattern=[[-1, P]], channel_multiplier=1).then_inc(sem("pool"), 1)
            pool.affine_select(out=ebuf[:, 0, 1, 0:P], in_=ebuf[:, 0, 1, 0:P], compare_op=ALU.is_gt, fill=0.0, base=0,
                               pattern=[[1, P]], channel_multiplier=-1).then_inc(sem("pool"), 1)
            pool.wait_ge(sem("pool"), POOL0 + 11)
            pool.tensor_copy(tri[:], ebuf[:, 0, 0, 0:P]).then_inc(sem("at_made"), 1)
            pool.tensor_copy(comp[:], ebuf[:, 0, 1, 0:P]).then_inc(sem("at_made"), 1)

        def pair_start(i):
            return i < NU and i % PAIR_U == 0

        def at_act(act):
            act.wait_ge(sem("at_made"), 2)

            def prepare(pr):
                if pr:
                    act.wait_ge(sem("u_pv"), PAIR_U * pr)
                for g in (2 * pr, 2 * pr + 1):
                    act.wait_ge(sem("k_loaded"), 64 * (g + 1))
                    act.activation(kS[:, g % 2, 0:T], kq[:, 0, 0:T], ACT.Copy).then_inc(sem("k_hi"), 1)
                    act.activation(kS[:, g % 2, T + 64:KCOL], kq[:, 0, T:T + PAST], ACT.Copy).then_inc(sem("k_hi"), 1)
                    act.wait_ge(sem("q_loaded"), 32 * (g + 1))
                    for v in range(2):
                        act.activation(qS[:, g % 2, v, :], kq[:, 1, 0:T], ACT.Copy, scale=HD ** -0.5).then_inc(sem("q_hi"), 1)

            for i in range(NU + 2):
                if pair_start(i):
                    if i:
                        weigh(act, i - 1)
                    prepare(i // PAIR_U)
                if i < NU:
                    u, w = units[i], units[i]["w"]
                    e = ebuf[:, i % 2, :, 0:w]
                    act.wait_ge(sem("u_z"), i + 1)
                    if i >= 2:
                        act.wait_ge(sem("u_splo"), i - 1)
                    act.activation(e, ps[:, 2 * (i % 2):2 * (i % 2) + 2, 0:w], ACT.Abs).then_inc(sem("u_e"), 1)
                    act.wait_ge(sem("u_e"), 3 * i + 1)
                    act.activation(e, e, ACT.Exp, scale=-1.0).then_inc(sem("u_e"), 1)
                    act.wait_ge(sem("u_e"), 3 * i + 2)
                    act.activation(e, e, ACT.Ln, bias=1.0).then_inc(sem("u_e"), 1)
                if 1 <= i <= NU and not pair_start(i):
                    weigh(act, i - 1)
                if i >= 2 and units[i - 2]["last"]:
                    u = units[i - 2]
                    act.wait_ge(sem("o_f"), 4 * (group_no[i - 2] + 1))
                    o = u["pr"] * T + u["q0"]
                    act.activation(hhi[:, o:o + u["total"]], fflat[:, 0:u["total"]], ACT.Copy).then_inc(sem("o_hi"), 1)

        def weigh(act, i):
            act.wait_ge(sem("u_t"), i + 1 + diags[i + 1])
            tb = tbuf[:, i % 2, :, 0:units[i]["w"]]
            act.activation(tb, tb, ACT.Exp).then_inc(sem("u_w"), 1)

        aflat = abuf[:].rearrange("p a n -> p (a n)")
        fflat = fbuf[:].rearrange("p a n -> p (a n)")

        def at_dve(dve):
            def prepare(pr):
                for g in (2 * pr, 2 * pr + 1):
                    dve.wait_ge(sem("k_hi"), 2 * g + 2)
                    for d0, s0, n in ((0, 0, T), (T + 64, T, PAST)):
                        kl = kS[64:P, g % 2, d0:d0 + n]
                        dve.tensor_tensor(kl, kq[64:P, 0, s0:s0 + n], kl.bitcast(F32), ALU.subtract).then_inc(sem("k_lo"), 1)
                    dve.wait_ge(sem("q_hi"), 2 * g + 2)
                    for v in range(2):
                        r = slice(64, P) if v == 0 else slice(0, 64)
                        ql = qS[r, g % 2, v, :]
                        dve.scalar_tensor_tensor(ql, kq[r, 1, 0:T], HD ** -0.5, ql.bitcast(F32), ALU.mult, ALU.subtract).then_inc(sem("q_lo"), 1)

            for i in range(NU + 2):
                if pair_start(i):
                    if i:
                        take_w(dve, i - 1)
                    prepare(i // PAIR_U)
                if i < NU:
                    u, w = units[i], units[i]["w"]
                    e, z = ebuf[:, i % 2, :, 0:w], ps[:, 2 * (i % 2):2 * (i % 2) + 2, 0:w]
                    dw = min(P, w)
                    dve.wait_ge(sem("u_e"), 3 * i + 3)
                    dve.scalar_tensor_tensor(e, z, 0.0, e, ALU.max, ALU.add).then_inc(sem("u_sp"), 1)
                    dve.wait_ge(sem("u_sp"), i + 1 + diags[i])
                    if u["diag"]:
                        for a in range(2):
                            ins = dve.tensor_tensor(e[:, a, 0:dw], e[:, a, 0:dw], dmask[:, 0:dw], ALU.mult)
                            ins.then_inc(sem("u_sp" if a else "u_part"), 1)
                        dve.wait_ge(sem("u_sp"), i + 1 + diags[i + 1])
                        dve.wait_ge(sem("u_part"), 2 * diags[i] + 1)
                if 1 <= i <= NU and not pair_start(i):
                    take_w(dve, i - 1)
                if i < NU:
                    if i >= 2:
                        dve.wait_ge(sem("u_pv"), i - 1)
                    dve.tensor_copy(sphi[:, i % 2, :, 0:w], e).then_inc(sem("u_sphi"), 1)
                    dve.wait_ge(sem("u_tri"), i + 1)
                    tb = tbuf[:, i % 2, :, 0:w]
                    if i >= 2:
                        dve.wait_ge(sem("u_wlo"), i - 1)
                    dve.tensor_copy(tb, z).then_inc(sem("u_tc"), 1)
                    dve.wait_ge(sem("u_tc"), i + 1)
                    dve.tensor_tensor(tb, tb, ps[:, 4:6, u["off"]:u["off"] + w], ALU.subtract).then_inc(sem("u_t"), 1)
                    if u["diag"]:
                        dve.wait_ge(sem("u_t"), i + 1 + diags[i])
                        for a in range(2):
                            ins = dve.tensor_tensor(tb[:, a, 0:dw], tb[:, a, 0:dw], dneg[:, 0:dw], ALU.add)
                            ins.then_inc(sem("u_t" if a else "u_part"), 1)
                if 1 <= i <= NU and units[i - 1]["last"]:
                    u, g = units[i - 1], group_no[i - 1]
                    n = u["total"]
                    dve.wait_ge(sem("u_pv"), i)
                    if g:
                        dve.wait_ge(sem("o_lo"), g)
                    for a in range(2):
                        dve.tensor_copy(aflat[0:64, 0:n], ps[64:P, 6 + a, 0:n]).then_inc(sem("o_f"), 1)
                        dve.wait_ge(sem("o_f"), 4 * g + 2 * a + 1)
                        dve.tensor_tensor(fflat[64 * a:64 * a + 64, 0:n], ps[0:64, 6 + a, 0:n], aflat[0:64, 0:n], ALU.add
                                          ).then_inc(sem("o_f"), 1)
                        dve.wait_ge(sem("o_f"), 4 * g + 2 * a + 2)

        def take_w(dve, i):
            w = units[i]["w"]
            dve.wait_ge(sem("u_w"), i + 1)
            if i >= 1:
                dve.wait_ge(sem("u_pv"), i)
            dve.tensor_copy(ww[:, 0, :, 0:w], tbuf[:, i % 2, :, 0:w]).then_inc(sem("u_whi"), 1)

        def at_pool(pool):
            def prepare(pr):
                if pr:
                    pool.wait_ge(sem("u_pv"), PAIR_U * pr)
                for g in (2 * pr, 2 * pr + 1):
                    pool.wait_ge(sem("v_loaded"), 48 * (g + 1))
                    pool.tensor_copy(vS[:, g % 2, :, 0:HD], vr[:]).then_inc(sem("v_hi"), 1)
                    pool.wait_ge(sem("v_hi"), g + 1)
                    pool.tensor_tensor(vS[:, g % 2, :, HD:P], vr[:], vS[:, g % 2, :, 0:HD].bitcast(F32), ALU.subtract).then_inc(sem("v_lo"), 1)

            def w_lo(i):
                w = units[i]["w"]
                pool.wait_ge(sem("u_whi"), i + 1)
                pool.tensor_tensor(ww[:, 1, :, 0:w], tbuf[:, i % 2, :, 0:w], ww[:, 0, :, 0:w].bitcast(F32), ALU.subtract).then_inc(sem("u_wlo"), 1)

            for i in range(NU + 2):
                if pair_start(i):
                    if i:
                        w_lo(i - 1)
                    prepare(i // PAIR_U)
                elif 1 <= i <= NU:
                    w_lo(i - 1)
                if i < NU:
                    w = units[i]["w"]
                    pool.wait_ge(sem("u_sphi"), i + 1)
                    pool.tensor_tensor(splo[:, i % 2, :, 0:w], ebuf[:, i % 2, :, 0:w], sphi[:, i % 2, :, 0:w].bitcast(F32),
                                       ALU.subtract).then_inc(sem("u_splo"), 1)
                if i >= 2 and units[i - 2]["last"]:
                    u = units[i - 2]
                    pool.wait_ge(sem("o_hi"), group_no[i - 2] + 1)
                    o = u["pr"] * T + u["q0"]
                    n = u["total"]
                    pool.tensor_tensor(hlo[:, o:o + n], fflat[:, 0:n], hhi[:, o:o + n].bitcast(F32), ALU.subtract).then_inc(sem("o_lo"), 1)

        def at_pe(pe):
            def scores(i):
                u = units[i]
                if i >= 2:
                    pe.wait_ge(sem("u_t"), i - 1 + diags[i - 1])
                if pair_start(i):
                    pe.wait_ge(sem("k_lo"), 4 * (u["pr"] + 1))
                    pe.wait_ge(sem("q_lo"), 4 * (u["pr"] + 1))
                for a in range(2):
                    q = u["q0"] + u["off"]
                    out = ps[:, 2 * (i % 2) + a, 0:u["w"]]
                    pe.matmul(out, kS[:, a, u["kc"]:u["kc"] + P], qS[:, a, 0, q:q + u["w"]], start=True, stop=False)
                    mm = pe.matmul(out, kS[:, a, u["kc"]:u["kc"] + P], qS[:, a, 1, q:q + u["w"]], start=False, stop=True)
                mm.then_inc(sem("u_z"), 1)

            def sums(i, mat):
                u = units[i]
                for a in range(2):
                    out = ps[:, 4 + a, u["off"]:u["off"] + u["w"]]
                    for j, r in enumerate((sphi, splo)):
                        mm = pe.matmul(out, mat[:], r[:, i % 2, a, 0:u["w"]], start=mat is tri and u["first"] and j == 0,
                                       stop=True, skip_group_check=True)
                return mm

            def values(i):
                u = units[i]
                pe.wait_ge(sem("u_wlo"), i + 1)
                if u["first"] and group_no[i]:
                    pe.wait_ge(sem("o_f"), 4 * group_no[i])
                if pair_start(i):
                    pe.wait_ge(sem("v_lo"), 2 * (u["pr"] + 1))
                for a in range(2):
                    out = ps[:, 6 + a, u["off"]:u["off"] + u["w"]]
                    for j in range(2):
                        mm = pe.matmul(out, vS[:, a, u["vb"], :], ww[:, j, a, 0:u["w"]], start=u["first"] and j == 0,
                                       stop=True, skip_group_check=True)
                mm.then_inc(sem("u_pv"), 1)

            pe.wait_ge(sem("at_made"), 2)
            pe.wait_ge(sem("mix_f"), 8 * NC)
            scores(0)
            for i in range(NU):
                if i + 1 < NU and not pair_start(i + 1):
                    scores(i + 1)
                u = units[i]
                pe.wait_ge(sem("u_splo"), i + 1)
                if u["first"] and i:
                    pe.wait_ge(sem("u_t"), i + diags[i])
                sums(i, tri).then_inc(sem("u_tri"), 1)
                if i:
                    if not pair_start(i):
                        values(i - 1)
                if not u["last"]:
                    pe.wait_ge(sem("u_t"), i + 1 + diags[i])
                    sums(i, comp)
                if pair_start(i + 1) or i + 1 == NU:
                    values(i)
                    if i + 1 < NU:
                        scores(i + 1)

        def prep_sp(sp):
            for j, (src, n) in enumerate((("ssm_lam_re", 1), ("ssm_lam_im", 2), ("state_ssm_re", 3), ("state_ssm_im", 4))):
                v = A[src].rearrange("o g p -> (o g p)" if src[0:3] == "ssm" else "o b g p -> (o b g p)")
                sp.dma_start(lt[0:GP, n, :], v.rearrange("(j q) -> j q", q=P)).then_inc(sem("par_loaded"), 16)
            sp.dma_start(lstep[0:GP, :], A["ssm_log_step"].rearrange("o (j a) -> (o j) a", a=2)).then_inc(sem("step_loaded"), 16)
            for r, src in enumerate(("ssm_c_re", "ssm_c_im")):
                sp.dma_start(craw[:, r, :, :], A[src].rearrange("o g c p -> (o g c) p").rearrange("(t q) p -> q t p", q=P)
                             ).then_inc(sem("c_loaded"), 16)
            for r, src in enumerate(("ssm_b_re", "ssm_b_im")):
                sp.dma_start(bb[:, r, :, :], A[src].rearrange("o (j a) p c -> (o a p) j c", a=2)).then_inc(sem("b_loaded"), 16)

        def prep_pe(pe):
            pe.wait_ge(sem("par_loaded"), 16 * 4)
            pe.wait_ge(sem("step_spread"), 1)
            for n in range(5):
                mm = pe.transpose(ps[:, 4, 64 + n * GP:64 + (n + 1) * GP], lt[0:GP, n, :], ident[0:GP, 0:GP])
            mm.then_inc(sem("par_mm"), 1)
            pe.wait_ge(sem("c_loaded"), 32)
            for q in range(4):
                if q == 3:
                    pe.wait_ge(sem("ct_made"), 2)
                for t in range(4):
                    mm = pe.transpose(ps[0:64, 5 + q % 3, t * P:(t + 1) * P], craw[:, q // 2, 4 * (q % 2) + t, :], ident[:])
                mm.then_inc(sem("c_mm"), 1)

        def prep_dve_in(dve):
            dve.wait_ge(sem("step_loaded"), 16)
            dve.tensor_copy(lt[0:GP, 0, :].rearrange("j (a p) -> j a p", a=2), lstep[0:GP, :].unsqueeze(2).to_broadcast([GP, 2, 64])
                            ).then_inc(sem("step_spread"), 1)
            dve.wait_ge(sem("par_mm"), 1)
            dve.tensor_copy(par[:], ps[:, 4, 64:64 + 5 * GP].rearrange("p (n j) -> p n j", n=5)).then_inc(sem("par_made"), 1)
            for q in range(4):
                dve.wait_ge(sem("c_mm"), q + 1)
                v = ps[0:64, 5 + q % 3, :].rearrange("p (j a c) -> p j a c", a=2, c=16)
                for a in range(2):
                    dve.tensor_copy(ct[64 * a:64 * a + 64, q // 2, 16 * (q % 2):16 * (q % 2) + 16, :], v[:, :, a, :]
                                    ).then_inc(sem("ct_made"), 1)

        def prep_act_scalars(act):
            act.wait_ge(sem("par_made"), 1)
            act.activation(S_step, par[:, 0, :], ACT.Exp).then_inc(sem("pa"), 1)
            act.wait_ge(sem("pd_exp"), 1)
            act.activation(S_mag, S_lrs, ACT.Exp).then_inc(sem("pa"), 1)
            act.activation(S_r8, S_lrs, ACT.Exp, scale=float(L)).then_inc(sem("pa"), 1)
            act.wait_ge(sem("pd_ang"), 1)
            act.activation(S_sin, S_r, ACT.Sin).then_inc(sem("pa"), 1)
            act.activation(S_cos, S_rc, ACT.Sin).then_inc(sem("pa"), 1)

        def prep_dve_scalars(dve):
            def own(ins):
                ins.then_inc(sem("pd"), 1)
                chain[0] += 1
                dve.wait_ge(sem("pd"), chain[0])

            def tt(out, a, b, op):
                own(dve.tensor_tensor(out, a, b, op))

            def cmul(outr, outi, ar, ai, br, bi, t1, t2):
                tt(t1, ar, br, ALU.mult)
                tt(t2, ai, bi, ALU.mult)
                tt(outr, t1, t2, ALU.subtract)
                tt(t1, ar, bi, ALU.mult)
                tt(t2, ai, br, ALU.mult)
                tt(outi, t1, t2, ALU.add)

            dve.wait_ge(sem("x_out"), 16)
            dve.wait_ge(sem("par_made"), 1)
            dve.wait_ge(sem("pa"), 1)
            tt(S_lrs, par[:, 1, :], S_step, ALU.mult)
            dve.tensor_tensor(S_ang, par[:, 2, :], S_step, ALU.mult).then_inc(sem("pd_exp"), 1)
            dve.wait_ge(sem("pd_exp"), 1)
            own(dve.tensor_scalar(S_k, S_ang, 1.0 / TWO_PI, MAGIC, ALU.mult, ALU.add))
            own(dve.tensor_scalar(S_k, S_k, MAGIC, None, ALU.subtract))
            own(dve.scalar_tensor_tensor(S_r, S_k, -TURN[0], S_ang, ALU.mult, ALU.add))
            own(dve.scalar_tensor_tensor(S_r, S_k, -TURN[1], S_r, ALU.mult, ALU.add))
            own(dve.scalar_tensor_tensor(S_r, S_k, -TURN[2], S_r, ALU.mult, ALU.add))
            own(dve.tensor_scalar(S_r, S_r, 3.1415925, -3.1415925, ALU.min, ALU.max))
            own(dve.scalar_tensor_tensor(S_rc, S_r, -1.0, S_r, ALU.mult, ALU.max))
            dve.tensor_scalar(S_rc, S_rc, -1.0, TWO_PI / 4, ALU.mult, ALU.add).then_inc(sem("pd_ang"), 1)
            dve.wait_ge(sem("pa"), 5)
            own(dve.memset(pc[:, 0, :, 0], 1.0))
            own(dve.memset(pc[:, 1, :, 0], 0.0))
            tt(pc[:, 0, :, 1], S_mag, S_cos, ALU.mult)
            tt(pc[:, 1, :, 1], S_mag, S_sin, ALU.mult)
            for k in (1, 2, 4):
                b = [pc[:, r, :, k:k + 1].to_broadcast([P, GP, k]) for r in range(2)]
                cmul(pc[:, 0, :, k + 1:2 * k + 1], pc[:, 1, :, k + 1:2 * k + 1], pc[:, 0, :, 1:k + 1], pc[:, 1, :, 1:k + 1],
                     b[0], b[1], t1[:, 0:GP * k].rearrange("p (j k) -> p j k", k=k), t2[:, 0:GP * k].rearrange("p (j k) -> p j k", k=k))
            for s in range(L):
                own(dve.tensor_copy(pb[:, :, :, s], pc[:, :, :, L - 1 - s]))
            lr, li = par[:, 1, :], par[:, 2, :]
            tt(S_a, lr, lr, ALU.mult)
            tt(S_b, li, li, ALU.mult)
            tt(S_a, S_a, S_b, ALU.add)
            own(dve.reciprocal(S_a, S_a))
            own(dve.tensor_scalar(S_nr, pc[:, 0, :, 1], 1.0, None, ALU.subtract))
            tt(S_b, S_nr, lr, ALU.mult)
            tt(S_c, pc[:, 1, :, 1], li, ALU.mult)
            tt(S_b, S_b, S_c, ALU.add)
            tt(S_cor, S_b, S_a, ALU.mult)
            tt(S_b, pc[:, 1, :, 1], lr, ALU.mult)
            tt(S_c, S_nr, li, ALU.mult)
            tt(S_b, S_b, S_c, ALU.subtract)
            tt(S_coi, S_b, S_a, ALU.mult)
            dve.wait_ge(sem("b_loaded"), 32)
            w = GP * 16
            co = [v.unsqueeze(2).to_broadcast([P, GP, 16]) for v in (S_cor, S_coi)]
            v1, v2, v3 = (t[:, o:o + w].rearrange("p (j c) -> p j c", c=16) for t, o in ((t1, 0), (t2, 0), (t1, w)))
            tt(v1, bb[:, 0], co[0], ALU.mult)
            tt(v2, bb[:, 1], co[1], ALU.mult)
            tt(v1, v1, v2, ALU.subtract)
            tt(v2, bb[:, 0], co[1], ALU.mult)
            tt(v3, bb[:, 1], co[0], ALU.mult)
            tt(bb[:, 1], v2, v3, ALU.add)
            own(dve.tensor_copy(bb[:, 0], v1))
            own(dve.tensor_copy(pp[:, 0:2, :], par[:, 3:5, :]))
            cmul(pp[:, 2, :], pp[:, 3, :], pc[:, 0, :, 8], pc[:, 1, :, 8], pp[:, 0, :], pp[:, 1, :], S_a, S_b)
            src = (S_cos, S_sin)
            for m in range(10):
                dst = (S_e[m % 2], S_f[m % 2]) if m < 3 else (ek[:, 0, :, m - 3], ek[:, 1, :, m - 3])
                if m:
                    cmul(dst[0], dst[1], src[0], src[1], src[0], src[1], S_a, S_b)
                else:
                    own(dve.tensor_copy(dst[0], src[0]))
                    own(dve.tensor_copy(dst[1], src[1]))
                unit(dve, own, dst[0], dst[1], S_a, S_b)
                src = dst
            dve.tensor_copy(S_c, S_a).then_inc(sem("pp_made"), 1)
            dve.wait_ge(sem("pp_made"), 1)

        def unit(dve, own, re, im, a, b):
            own(dve.tensor_tensor(a, re, re, ALU.mult))
            own(dve.tensor_tensor(b, im, im, ALU.mult))
            own(dve.tensor_tensor(a, a, b, ALU.add))
            own(dve.tensor_scalar(a, a, -0.5, 1.5, ALU.mult, ALU.add))
            own(dve.tensor_tensor(re, re, a, ALU.mult))
            own(dve.tensor_tensor(im, im, a, ALU.mult))

        chain = [0]

        def prep_dve_block(dve, n):
            blk, kind = divmod(n, 3)
            j0 = 8 * blk

            def own(ins):
                ins.then_inc(sem("pd"), 1)
                chain[0] += 1
                dve.wait_ge(sem("pd"), chain[0])

            def tt(out, a, b, op):
                own(dve.tensor_tensor(out, a, b, op))

            if n >= 3:
                dve.wait_ge(sem(f"prep_out{kind}"), 16 * blk)
            if kind == 0:
                own(dve.memset(eb[:, 0, :, 0:1], 1.0))
                own(dve.memset(eb[:, 1, :, 0:1], 0.0))
                for m in range(7):
                    k = 1 << m
                    er_, ei_ = eb[:, 0, :, 0:k], eb[:, 1, :, 0:k]
                    br_, bi_ = (ek[:, r, j0:j0 + 8, m:m + 1].to_broadcast([P, 8, k]) for r in range(2))
                    v1, v2 = (t[:, 0:8 * k].rearrange("p (j k) -> p j k", k=k) for t in (t1, t2))
                    tt(v1, er_, br_, ALU.mult)
                    tt(v2, ei_, bi_, ALU.mult)
                    tt(eb[:, 0, :, k:2 * k], v1, v2, ALU.subtract)
                    tt(v1, er_, bi_, ALU.mult)
                    tt(v2, ei_, br_, ALU.mult)
                    tt(eb[:, 1, :, k:2 * k], v1, v2, ALU.add)
                v1, v2 = (t[:, 0:8 * P].rearrange("p (j k) -> p j k", k=P) for t in (t1, t2))
                unit(dve, own, eb[:, 0, :, 0:P], eb[:, 1, :, 0:P], v1, v2)
                for r in range(2):
                    own(dve.tensor_copy(eb[:, r, :, P:NCH], eb[:, r, :, 0:NCH - P]))
                own(dve.tensor_copy(eb[:, 2, :, :], S_r8[:, j0:j0 + 8].unsqueeze(2).to_broadcast([P, 8, NCH])))
                own(dve.memset(eb[:, 2, :, 0:1], 0.0))
                dve.memset(eb[:, 2, :, P:P + 1], 0.0).then_inc(sem("prep_made"), 1)
            elif kind == 1:
                sh = [P, 8, L, 16]
                p_ = [pb[:, r, j0:j0 + 8, :].unsqueeze(3).to_broadcast(sh) for r in range(2)]
                b_ = [bb[:, r, j0:j0 + 8, :].unsqueeze(2).to_broadcast(sh) for r in range(2)]
                o_ = [bo[:, :, r, :].rearrange("p j (s c) -> p j s c", c=16) for r in range(2)]
                v1, v2 = (t[:, 0:8 * P].rearrange("p (j s c) -> p j s c", s=L, c=16) for t in (t1, t2))
                tt(v1, p_[0], b_[0], ALU.mult)
                tt(v2, p_[1], b_[1], ALU.mult)
                tt(o_[0], v1, v2, ALU.subtract)
                tt(v1, p_[0], b_[1], ALU.mult)
                tt(v2, p_[1], b_[0], ALU.mult)
                dve.tensor_tensor(o_[1], v1, v2, ALU.add).then_inc(sem("prep_made"), 1)
            else:
                sh = [P, 8, L + 1, 16]
                p_ = [pc[:, r, j0:j0 + 8, :].unsqueeze(3).to_broadcast(sh) for r in range(2)]
                c_ = [ct[:, r, j0:j0 + 8, :].unsqueeze(2).to_broadcast(sh) for r in range(2)]
                o_ = [co_[:, :, r, :].rearrange("p j (s c) -> p j s c", c=16) for r in range(2)]
                v1, v2 = (t[:, 0:8 * CW].rearrange("p (j s c) -> p j s c", s=L + 1, c=16) for t in (t1, t2))
                tt(v1, p_[0], c_[0], ALU.mult)
                tt(v2, p_[1], c_[1], ALU.mult)
                tt(o_[0], v1, v2, ALU.subtract)
                tt(v1, p_[0], c_[1], ALU.mult)
                tt(v2, p_[1], c_[0], ALU.mult)
                tt(v1, v1, v2, ALU.add)
                dve.tensor_scalar(o_[1], v1, -1.0, None, ALU.mult).then_inc(sem("prep_made"), 1)
            dve.wait_ge(sem("prep_made"), n + 1)

        def prep_pool_block(pool, n):
            blk, kind = divmod(n, 3)
            j0 = 8 * blk
            pool.wait_ge(sem("prep_made"), n + 1)
            if kind == 0:
                pool.dma_start(dE[:, :, j0:j0 + 8, :], eb[:]).then_inc(sem(f"prep_out{kind}"), 16)
            elif kind == 1:
                pool.dma_start(dB[:, j0:j0 + 8, :, :], bo[:]).then_inc(sem(f"prep_out{kind}"), 16)
            else:
                pool.dma_start(dC[:, j0:j0 + 8, :, :], co_[:]).then_inc(sem(f"prep_out{kind}"), 16)

        NF = KD

        def s5_sp(sp):
            sp.wait_ge(sem("n_f"), n_units(2))
            sp.dma_start(xs, x[:]).then_inc(sem("x_out"), 16)
            sp.wait_ge(sem("x_out"), 32)
            sp.wait_ge(sem("p_out"), 16)
            sp.dma_start(p4[:], dP).then_inc(sem("p4_loaded"), 16)

            def load(f):
                if f >= 1:
                    sp.wait_ge(sem("e_BT"), 2 * f)
                    sp.wait_ge(sem("s_K"), f)
                    sp.wait_ge(sem("s_rot"), f)
                if f >= 2:
                    sp.wait_ge(sem("s_Y"), f - 1)
                js = slice(4 * f, 4 * f + 4)
                sp.dma_start(br[:], dB[:, js, :, :]).then_inc(sem("br_loaded"), 16)
                sp.dma_start(ca[:, f % 2], dC[:, js, :, :]).then_inc(sem(f"ca_loaded{f % 2}"), 16)
                sp.dma_start(e3[:], dE[:, :, js, :]).then_inc(sem("e3_loaded"), 16)

            load(0)
            for f in range(NF):
                sp.wait_ge(sem("e_K"), 2 * f + 2)
                if f >= 2:
                    sp.wait_ge(sem("s_Y"), f - 1)
                sp.wait_ge(sem("t_zero"), 1)
                for s in range(L):
                    sp.dma_start(tm[16 * s:16 * s + 16, f % 2, :, 16 * s:P], kt[0:16, :, 0:P - 16 * s]).then_inc(sem(f"t_made{f % 2}"), 16)
                if f + 1 < NF:
                    load(f + 1)
            sp.wait_ge(sem("y_f"), 3 * NF)
            sp.dma_start(x[:], xs).then_inc(sem("x_back"), 16)
            sp.wait_ge(sem("fin_t"), 1)
            for q, o in enumerate(("re_p", "im_p", "re_s", "im_s")):
                sp.dma_start(O[o].rearrange("o b g p -> (o b g p)").rearrange("(j q) -> j q", q=P), fout[0:GP, q, :]).then_inc(sem("fin_out"), 16)

        def s5_pe(pe):
            def first(f):
                h0 = f * T
                if f:
                    pe.wait_ge(sem("e_BT"), 2 * f)
                    pe.wait_ge(sem("e_K"), 2 * f)
                else:
                    pe.wait_ge(sem("n_f"), n_units(2))
                for s in range(L):
                    b, o = s // 4, (s % 4) * P
                    pe.transpose(ps[:, b, o:o + P], hp[:, h0 + s:h0 + SEQ:L], ident[:])
                for s in range(L):
                    b, o = s // 4, (s % 4) * P
                    mm = pe.transpose(ps[0:8, 2 + b, o:o + P], hp[:, h0 + SEQ + s:h0 + T:L], ident[:])
                mm.then_inc(sem("s_R"), 1)
                pe.wait_ge(sem("e_R"), 2 * f + 2)
                pe.wait_ge(sem("e_Rs"), 2 * f + 2)
                if f:
                    pe.wait_ge(sem("e_X"), 3 * f)
                for g in range(8):
                    b, o = 4 + g // 3, (g % 3) * NCH
                    pe.transpose(ps[:, b, o:o + P], rr[:, g, :], ident[:])
                    mm = pe.transpose(ps[:, b, o + P:o + NCH], rs[0:8, g, :], ident[0:8, 0:8])
                mm.then_inc(sem("s_U"), 1)
                pe.wait_ge(sem("br_loaded"), 16 * (f + 1))
                for q in range(8):
                    mm = pe.transpose(ps[:, q // 4, (q % 4) * P:(q % 4 + 1) * P], br[:, q // 2, q % 2, :], ident[:])
                mm.then_inc(sem("s_B"), 1)
                pe.wait_ge(sem(f"ca_loaded{f % 2}"), 16 * (f // 2 + 1))
                for g in range(8):
                    j, a = divmod(g, 2)
                    r = slice(64 * a, 64 * a + 64)
                    for q in range(2):
                        mm = pe.matmul(ps[0:16, 2 + a, j * P:(j + 1) * P], br[r, j, q, P - 16:P], ca[r, f % 2, j, q, 0:P],
                                       start=q == 0, stop=q == 1)
                mm.then_inc(sem("s_K"), 1)
                pe.wait_ge(sem("e_U"), 3 * f + 3)
                pe.wait_ge(sem("e_BT"), 2 * f + 2)
                for q in range(2):
                    for j in range(4):
                        n = 4 * q + j
                        for a in range(2):
                            mm = pe.matmul(ps[64 * a:64 * a + 64, 4 + n // 3, (n % 3) * NCH:(n % 3 + 1) * NCH],
                                           bt[:, j, q, 64 * a:64 * a + 64], u[:, f % 2, 2 * j + a, :], start=True, stop=True,
                                           skip_group_check=True)
                mm.then_inc(sem("s_X"), 1)

            def second(f):
                pe.wait_ge(sem(f"t_made{f % 2}"), 16 * L * (f // 2 + 1))
                pe.wait_ge(sem("s_sh"), 2 * f + 2)
                nxt = min(f + 1, NF - 1)
                pe.wait_ge(sem("e_BT"), 2 * nxt + 2)
                pe.wait_ge(sem("e_K"), 2 * nxt + 2)
                for g in range(8):
                    j, a = divmod(g, 2)
                    r = slice(64 * a, 64 * a + 64)
                    out = ps[:, 2 * a + j // 2, (j % 2) * NCH:(j % 2 + 1) * NCH]
                    pe.matmul(out, tm[:, f % 2, g, :], u[:, f % 2, g, :], start=True, stop=False)
                    for q in range(2):
                        mm = pe.matmul(out, ca[r, f % 2, j, q, 16:CW], sh[r, f % 2, q, j, :], start=False, stop=q == 1)
                mm.then_inc(sem("s_Y"), 1)
                pe.wait_ge(sem("e_Y"), 4 * f + 4)
                pe.wait_ge(sem("e_X"), 3 * nxt + 3)
                for g in range(8):
                    b, o = g // 4, (g % 4) * P
                    pe.transpose(ps[:, 4 + b, o:o + P], yy[:, g, 0:P], ident[:])
                    mm = pe.transpose(ps[0:8, 6 + b, o:o + P], yy[:, g, P:NCH], ident[:])
                mm.then_inc(sem("s_Q"), 1)
                pe.wait_ge(sem("e_Q"), 2 * f + 2)
                pe.wait_ge(sem("e_Qs"), 2 * f + 2)
                for t in range(L):
                    pe.transpose(ps[:, t // 4, (t % 4) * P:(t % 4 + 1) * P], rp[:, t, :], ident[:])
                    mm = pe.transpose(ps[:, 3, 8 * t:8 * t + 8], rps[0:8, t, :], ident[0:8, 0:8])
                mm.then_inc(sem("s_Z"), 1)
                pe.wait_ge(sem("y_f"), 3 * f + 3)

            for f in range(NF + 1):
                if f < NF:
                    first(f)
                if f:
                    second(f - 1)
            pe.wait_ge(sem("fin_made"), 4 * NF)
            for q in range(4):
                mm = pe.transpose(ps[0:GP, 4, q * P:(q + 1) * P], fin[:, q, :], ident[:])
            mm.then_inc(sem("fin_mm"), 1)

        def s5_act(act):
            def first(f):
                act.wait_ge(sem("s_R"), f + 1)
                if f:
                    act.wait_ge(sem("s_U"), f)
                for b in range(2):
                    act.activation(rr[:].rearrange("p g (s c) -> p s g c", c=16)[:, 4 * b:4 * b + 4],
                                   ps[:, b, :].rearrange("p (s g c) -> p s g c", s=4, c=16), ACT.Copy).then_inc(sem("e_R"), 1)
                act.wait_ge(sem("s_U"), f + 1)
                if f >= 2:
                    act.wait_ge(sem("s_Y"), f - 1)
                for b in range(3):
                    n = 3 if b < 2 else 2
                    act.activation(u[:, f % 2, 3 * b:3 * b + n, :], ps[:, 4 + b, 0:n * NCH].rearrange("p (g n) -> p g n", g=n), ACT.Copy
                                   ).then_inc(sem("e_U"), 1)
                act.wait_ge(sem("s_B"), f + 1)
                if f:
                    act.wait_ge(sem("s_X"), f)
                for b in range(2):
                    act.activation(bt[:, 2 * b:2 * b + 2, :, :], ps[:, b, :].rearrange("p (j q n) -> p j q n", j=2, q=2), ACT.Copy
                                   ).then_inc(sem("e_BT"), 1)
                act.wait_ge(sem("s_X"), f + 1)
                if f:
                    act.wait_ge(sem("s_rot"), f)
                for b in range(3):
                    n = 3 if b < 2 else 2
                    act.activation(xx[:, 3 * b * NCH:(3 * b + n) * NCH], ps[:, 4 + b, 0:n * NCH], ACT.Copy).then_inc(sem("e_X"), 1)

            def second(f):
                act.wait_ge(sem("s_Y"), f + 1)
                if f:
                    act.wait_ge(sem("s_Q"), f)
                for b in range(4):
                    act.activation(yy[:].rearrange("p (h l a) n -> p a h l n", l=2, a=2)[:, b // 2, b % 2],
                                   ps[:, b, 0:2 * NCH].rearrange("p (l n) -> p l n", l=2), ACT.Copy).then_inc(sem("e_Y"), 1)
                act.wait_ge(sem("s_Q"), f + 1)
                if f:
                    act.wait_ge(sem("s_Z"), f)
                for b in range(2):
                    act.activation(rp[:].rearrange("p t (g c) -> p g t c", c=16)[:, 4 * b:4 * b + 4],
                                   ps[:, 4 + b, :].rearrange("p (g t c) -> p g t c", g=4, c=16), ACT.Copy).then_inc(sem("e_Q"), 1)
                act.wait_ge(sem("y_f"), 3 * f + 3)
                yt = yp[:, f * T:(f + 1) * T]
                act.activation(yt, yt, GELU).then_inc(sem("y_g"), 1)

            for f in range(NF + 1):
                if f < NF:
                    first(f)
                if f:
                    second(f - 1)

        def s5_dve(dve):
            def own(ins):
                ins.then_inc(sem("sd"), 1)
                chain[1] += 1
                dve.wait_ge(sem("sd"), chain[1])

            def tt(out, a, b, op):
                own(dve.tensor_tensor(out, a, b, op))

            chain.append(0)
            W4 = 4 * NCH
            xr, xi = xx[:, 0:W4], xx[:, W4:2 * W4]
            er_, ei_, r8_ = (e3[:, q].rearrange("p j n -> p (j n)") for q in range(3))

            def first(f):
                dve.wait_ge(sem("s_R"), f + 1)
                if f:
                    dve.wait_ge(sem("s_U"), f)
                for b in range(2):
                    dve.tensor_copy(rs[0:8].rearrange("p g (s c) -> p s g c", c=16)[:, 4 * b:4 * b + 4],
                                    ps[0:8, 2 + b, :].rearrange("p (s g c) -> p s g c", s=4, c=16)).then_inc(sem("e_Rs"), 1)
                dve.wait_ge(sem("s_K"), f + 1)
                if f:
                    dve.wait_ge(sem(f"t_made{(f - 1) % 2}"), 16 * L * ((f - 1) // 2 + 1))
                for b in range(2):
                    dve.tensor_copy(kt[0:16].rearrange("p (j a) n -> p a j n", a=2)[:, b], ps[0:16, 2 + b, :].rearrange("p (j n) -> p j n", j=4)).then_inc(sem("e_K"), 1)

            def scan(f):
                dve.wait_ge(sem("e_X"), 3 * f + 3)
                dve.wait_ge(sem("e3_loaded"), 16 * (f + 1))
                for q in range(2):
                    v = xx[:, q * W4:(q + 1) * W4].rearrange("p (j n) -> p j n", j=4)[:, :, P:P + 1]
                    own(dve.tensor_tensor(v, v, p4[:, 2 + q, 4 * f:4 * f + 4].unsqueeze(2), ALU.add))
                tt(v1, xr, er_, ALU.mult)
                tt(v2, xi, ei_, ALU.mult)
                tt(v1, v1, v2, ALU.add)
                tt(v2, xi, er_, ALU.mult)
                tt(v3, xr, ei_, ALU.mult)
                tt(v2, v2, v3, ALU.subtract)
                own(dve.tensor_tensor_scan(w1, r8_, v1, 0.0, ALU.mult, ALU.add))
                own(dve.tensor_tensor_scan(w2, r8_, v2, 0.0, ALU.mult, ALU.add))
                tt(v1, w1, er_, ALU.mult)
                tt(v2, w2, ei_, ALU.mult)
                tt(v1, v1, v2, ALU.subtract)
                tt(v2, w1, ei_, ALU.mult)
                tt(v3, w2, er_, ALU.mult)
                dve.tensor_tensor(v2, v2, v3, ALU.add).then_inc(sem("s_rot"), 1)
                dve.wait_ge(sem("s_rot"), f + 1)
                if f >= 2:
                    dve.wait_ge(sem("s_Y"), f - 1)
                for q, v in enumerate((v1, v2)):
                    v = v.rearrange("p (j n) -> p j n", j=4)
                    o = sh[:, f % 2, q, :, :]
                    for r, n in ((0, P - 1), (2, NCH - 1)):
                        dve.tensor_copy(fin[:, q + r, 4 * f:4 * f + 4], v[:, :, n]).then_inc(sem("fin_made"), 1)
                    own(dve.tensor_copy(o[:, :, 1:NCH], v[:, :, 0:NCH - 1]))
                    own(dve.memset(o[:, :, 0:1], 0.0))
                    dve.tensor_copy(o[:, :, P:P + 1], p4[:, q, 4 * f:4 * f + 4].unsqueeze(2)).then_inc(sem("s_sh"), 1)
                dve.wait_ge(sem("s_sh"), 2 * f + 2)

            def second(f):
                dve.wait_ge(sem("s_Q"), f + 1)
                if f:
                    dve.wait_ge(sem("s_Z"), f)
                for b in range(2):
                    dve.tensor_copy(rps[0:8].rearrange("p t (g c) -> p g t c", c=16)[:, 4 * b:4 * b + 4],
                                    ps[0:8, 6 + b, :].rearrange("p (g t c) -> p g t c", g=4, c=16)).then_inc(sem("e_Qs"), 1)
                dve.wait_ge(sem("s_Z"), f + 1)
                d = cols[:, 40 + f:41 + f]
                yt, ht = yp[:, f * T:(f + 1) * T], hp[:, f * T:(f + 1) * T]
                for b in range(3):
                    if b < 2:
                        o, h = (v[:, 0:SEQ].rearrange("p (n s) -> p s n", s=L)[:, 4 * b:4 * b + 4, :] for v in (yt, ht))
                        z = ps[:, b, :].rearrange("p (s n) -> p s n", s=4)
                    else:
                        o, h = (v[:, SEQ:T].rearrange("p (n s) -> p s n", s=L) for v in (yt, ht))
                        z = ps[:, 3, 0:DEC].rearrange("p (s n) -> p s n", s=L)
                    dve.scalar_tensor_tensor(o, h, d, z, ALU.mult, ALU.add).then_inc(sem("y_f"), 1)

            dve.wait_ge(sem("p4_loaded"), 16)
            for f in range(NF + 1):
                if f < NF:
                    first(f)
                    scan(f)
                if f:
                    second(f - 1)
            dve.wait_ge(sem("fin_mm"), 1)
            dve.tensor_copy(fout[0:GP].rearrange("p q n -> p (q n)"), ps[0:GP, 4, :]).then_inc(sem("fin_t"), 1)

        def y_split_act(act):
            for c, (s, n) in enumerate(CHUNKS):
                for f in range(KD):
                    o = f * T + s
                    act.wait_ge(sem("y_g"), NF)
                    act.activation(hhi[:, o:o + n], yp[:, o:o + n], ACT.Copy).then_inc(sem("ys_hi"), 1)

        def y_split_pool(pool):
            for c, (s, n) in enumerate(CHUNKS):
                for f in range(KD):
                    o = f * T + s
                    pool.wait_ge(sem("ys_hi"), c * KD + f + 1)
                    pool.tensor_tensor(hlo[:, o:o + n], yp[:, o:o + n], hhi[:, o:o + n].bitcast(F32), ALU.subtract).then_inc(sem("ys_lo"), 1)

        def glu_slab(t):
            m, half = divmod(t - SLAB_GLU, 2)
            return w_glu[:, :, half * D + m * P:half * D + (m + 1) * P]

        def glu_pe(pe):
            for q in range(KD):
                pe_pair(pe, SLAB_GLU + 2 * q, PAIR_GLU + NC * q, ready=(lambda c: pe.wait_ge(sem("ys_lo"), KD * (c + 1))) if q == 0 else None)

        def glu_act(act):
            for q in range(KD):
                for j in range(2):
                    if q < 2:
                        slab_hi(act, SLAB_GLU + 2 * q + 2 + j)
                    else:
                        slab_hi(act, SLAB_GLU + 2 * q + 2 + j, "pair_ready", PAIR_GLU + NC * (q - 1))
                for c, (s, n) in enumerate(CHUNKS):
                    v = PAIR_GLU + NC * q + c
                    act.wait_ge(sem("pair_ready"), v + 1)
                    act.wait_ge(sem("pair_used"), v - 1)
                    act.activation(abuf[:, v % 2, 0:n], ps[:, 2 * (v % 2) + 1, 0:n], ACT.Sigmoid).then_inc(sem("pair_act"), 1)

        def glu_dve(dve):
            dve.wait_ge(sem("x_back"), 32)
            for q in range(KD):
                for c, (s, n) in enumerate(CHUNKS):
                    r = NC * q + c
                    v = PAIR_GLU + r
                    dve.wait_ge(sem("pair_act"), v + 1)
                    if r >= 2:
                        dve.wait_ge(sem("glu_res"), r - 1)
                    dve.tensor_tensor(fbuf[:, v % 2, 0:n], ps[:, 2 * (v % 2), 0:n], abuf[:, v % 2, 0:n], ALU.mult).then_inc(sem("pair_used"), 1)
                    dve.wait_ge(sem("pair_used"), v + 1)
                    xo = x[:, q * T + s:q * T + s + n]
                    dve.tensor_tensor(xo, xo, fbuf[:, v % 2, 0:n], ALU.add).then_inc(sem("glu_res"), 1)

        def out_pe(pe):
            for tt, (s, n) in enumerate(TILES):
                pe.wait_ge(sem("n_f"), n_units(4, KD * (tt // 3 + 1)))
                for b in range(2):
                    if tt >= 2:
                        pe.wait_ge(sem(("yo_v", "yo_a")[b]), tt - 1)
                    for f in range(4):
                        o = (4 * b + f) * T + s
                        mm = pe.transpose(ps[0:n, 4 + (2 * tt + b) % 4, f * P:(f + 1) * P], yf[:, o:o + n], ident[:])
                    mm.then_inc(sem("yo_mm"), 1)

        def out_take(eng, b, copy):
            for tt, (s, n) in enumerate(TILES):
                eng.wait_ge(sem("yo_mm"), 2 * tt + b + 1)
                if tt >= 2:
                    eng.wait_ge(sem(f"y_out{tt % 2}"), 16 * (tt // 2))
                copy(yo[0:n, tt % 2, 512 * b:512 * b + 512], ps[0:n, 4 + (2 * tt + b) % 4, :]).then_inc(sem(("yo_v", "yo_a")[b]), 1)

        def out_sp(sp):
            for tt, (s, n) in enumerate(TILES):
                sp.wait_ge(sem("yo_v"), tt + 1)
                sp.wait_ge(sem("yo_a"), tt + 1)
                sp.dma_start(y_new[0][s:s + n, :] if tt < 8 else y_new[1], yo[0:n, tt % 2, :]).then_inc(sem(f"y_out{tt % 2}"), 16)


        POOL0 = 2
        block = ctx.enter_context(nc.Block())

        @block.sync
        def _(sp):
            for tt, (s, n) in enumerate(TILES):
                if tt >= 2:
                    sp.wait_ge(sem("xt_mm"), 2 * (tt - 1))
                src = xp[s:s + n, :] if tt < 8 else xd
                sp.dma_start(xin[0:n, tt % 2, :], src).then_inc(sem(f"x_loaded{tt % 2}"), 16)
                if tt == 0:
                    for j, w in enumerate((A["norm_mix"][0], A["norm_mix"][1], A["norm_ffn"][0], A["norm_ffn"][1],
                                           A["norm_final"], A["ssm_d"][0])):
                        sp.dma_start(nrow[8 * j:8 * j + 8, :], w.rearrange("(f p) -> f p", p=P)).then_inc(sem("n_loaded"), 16)
                if tt in (2, 3):
                    load_slab(sp, tt - 2, w_in[:, :, (tt - 2) * P:(tt - 1) * P])
            prep_sp(sp)
            for t in range(2, 4):
                load_slab(sp, t, w_in[:, :, t * P:(t + 1) * P])
            sp.wait_ge(sem("n_f"), n_units(0))
            sp.dma_start(xs, x[:]).then_inc(sem("x_out"), 16)
            with sp.Fori(0, 4) as i:
                for t in range(4, 8):
                    load_slab(sp, t, w_in[:, :, bass.ds(i * (4 * P) + t * P, P)], i, 4)
            for t in range(2):
                load_slab(sp, SLAB_OUT + t, w_out[:, :, t * P:(t + 1) * P])
            tr_sp(sp)
            at_sp(sp)
            for t in range(2, 8):
                load_slab(sp, SLAB_OUT + t, w_out[:, :, t * P:(t + 1) * P])
            ffn_sp(sp, F[0])
            ffn_sp(sp, F[0], 1)
            for t in range(2):
                load_slab(sp, SLAB_GLU + t, glu_slab(SLAB_GLU + t))
            s5_sp(sp)
            for t in range(2, 2 * KD):
                load_slab(sp, SLAB_GLU + t, glu_slab(SLAB_GLU + t))
            ffn_sp(sp, F[1])
            ffn_sp(sp, F[1], 1)
            out_sp(sp)
            sp.wait_ge(sem("y_out0"), 16 * 5)
            sp.wait_ge(sem("y_out1"), 16 * 4)
            sp.wait_ge(sem("fin_out"), 16 * 4)

        @block.gpsimd
        def _(pool):
            pool.memset(ident[:], 0.0).then_inc(sem("pool"), 1)
            pool.memset(cols[:, 48:49], EPS).then_inc(sem("pool"), 1)
            pool.wait_ge(sem("pool"), 2)
            pool.memset(ones[:], 1.0).then_inc(sem("consts"), 1)
            pool.affine_select(out=ident[:], in_=ident[:], compare_op=ALU.not_equal, fill=1.0, base=0, pattern=[[-1, P]],
                               channel_multiplier=1).then_inc(sem("ident_made"), 1)
            for t in range(2):
                slab_lo(pool, t)
            norm_pool(pool, 0)

            def store(t, i=None, b=0):
                pool.wait_ge(sem("acc_used"), step(NC * (t + 1), i, NC * b))
                r = step(t * P, i, b * P)
                pool.dma_start(zT[bass.ds(r, P), :] if i is not None else zT[r:r + P, :], zst[:, t % 2, :]
                               ).then_inc(sem(f"z_stored{t % 2}"), 16)

            for t in range(IN_TILES):
                slab_lo(pool, t + 2)
                store(t)
                if t == 1:
                    pool.wait_ge(sem("pp_made"), 1)
                    pool.dma_start(dP, pp[:]).then_inc(sem("p_out"), 16)
                if 2 <= t < 14:
                    prep_pool_block(pool, t - 2)
            tr_pool(pool)
            at_pool_make(pool)
            at_pool(pool)
            for t in range(8):
                slab_lo(pool, SLAB_OUT + t + 2)
            norm_pool(pool, 1)
            ffn_pool(pool, F[0])
            pool.wait_ge(sem("n_f"), n_units(2))
            pool.memset(tm[:], 0.0).then_inc(sem("t_zero"), 1)
            y_split_pool(pool)
            for q in range(KD):
                for j in range(2):
                    slab_lo(pool, SLAB_GLU + 2 * q + 2 + j)
            norm_pool(pool, 3)
            ffn_pool(pool, F[1])

        @block.scalar
        def _(act):
            for tt, (s, n) in enumerate(TILES):
                act.wait_ge(sem("xt_mm"), 2 * tt + 2)
                act.activation(x3[:, 4:8, s:s + n], ps[:, (2 * tt + 1) % 4, :].rearrange("p (f n) -> p f n", f=4)[:, :, 0:n], ACT.Copy
                               ).then_inc(sem("xt_a"), 1)
                if tt in (4, 5):
                    slab_hi(act, tt - 4)

            def x_in(eng, c):
                last = (3, 6, 9)[c]
                eng.wait_ge(sem("xt_a"), last)
                eng.wait_ge(sem("xt_v"), last)

            act.wait_ge(sem("consts"), 1)
            norm_act(act, 0, x_in, True)
            for t in range(IN_TILES):
                slab_hi(act, t + 2, "acc_ready" if t >= 2 else None, NC * (t - 1))
                if t == 1:
                    prep_act_scalars(act)
            tr_act(act)
            at_act(act)
            act.wait_ge(sem("o_lo"), 12)
            for t in range(8):
                slab_hi(act, SLAB_OUT + t + 2, "acc_ready" if t >= 2 else None, ACC_OUT + NC * (t - 1))
            norm_act(act, 1, lambda e, c: e.wait_ge(sem("acc_used"), ACC_FF0 - NC + c + 1), True)
            ffn_act(act, F[0], "acc_ready", ACC_FF0)
            norm_act(act, 2, lambda e, c: e.wait_ge(sem("acc_used"), ACC_FF1 - KD * (2 - c)), False)
            s5_act(act)
            y_split_act(act)
            glu_act(act)
            act.wait_ge(sem("fin_out"), 16 * 4)
            norm_act(act, 3, lambda e, c: e.wait_ge(sem("glu_res"), NC * KD), True)
            ffn_act(act, F[1], "pair_ready", PAIR_FF1)
            norm_act(act, 4, lambda e, c: e.wait_ge(sem("acc_used"), ACC_FF1 + PARTS * KD * NC - KD * (2 - c)), False)
            out_take(act, 1, lambda o, i: act.activation(o, i, ACT.Copy))

        @block.vector
        def _(dve):
            dve.wait_ge(sem("cols_mm"), 1)
            dve.tensor_copy(cols[:, 0:48], ps[:, 4, 0:48]).then_inc(sem("cols_made"), 1)
            for tt, (s, n) in enumerate(TILES):
                dve.wait_ge(sem("xt_mm"), 2 * tt + 1)
                dve.tensor_copy(x3[:, 0:4, s:s + n], ps[:, (2 * tt) % 4, :].rearrange("p (f n) -> p f n", f=4)[:, :, 0:n]
                                ).then_inc(sem("xt_v"), 1)
            dve.wait_ge(sem("cols_made"), 1)
            prep_dve_in(dve)
            norm_dve(dve, 0, 0)

            def stage(t, i=None, b=0):
                if t >= 2:
                    dve.wait_ge(sem(f"z_stored{t % 2}"), step(16 * (t // 2), i, 8 * b))
                for c, (s, n) in enumerate(CHUNKS):
                    v = NC * t + c
                    dve.wait_ge(sem("acc_ready"), step(v + 1, i, NC * b))
                    dve.tensor_copy(zst[:, t % 2, s:s + n], acc(v)[:, 0:n]).then_inc(sem("acc_used"), 1)

            for t in range(IN_TILES):
                stage(t)
                if t == 1:
                    prep_dve_scalars(dve)
                if 2 <= t < 14:
                    prep_dve_block(dve, t - 2)
            tr_dve(dve)
            dve.wait_ge(sem("at_made"), 2)
            at_dve(dve)
            dve.wait_ge(sem("x_back"), 16)
            for m in range(KD):
                for c, (s, n) in enumerate(CHUNKS):
                    v = ACC_OUT + m * NC + c
                    dve.wait_ge(sem("acc_ready"), v + 1)
                    xo = x[:, m * T + s:m * T + s + n]
                    dve.tensor_tensor(xo, acc(v)[:, 0:n], xo, ALU.add).then_inc(sem("acc_used"), 1)
            norm_dve(dve, 1, 16)
            ffn_dve(dve, F[0])
            norm_dve(dve, 2, 8, plain=hp)
            s5_dve(dve)
            glu_dve(dve)
            norm_dve(dve, 3, 24)
            ffn_dve(dve, F[1])
            norm_dve(dve, 4, 32, plain=yf)
            out_take(dve, 0, dve.tensor_copy)

        @block.tensor
        def _(pe):
            pe.wait_ge(sem("ident_made"), 1)
            pe.wait_ge(sem("n_loaded"), 16 * 6)
            pe.transpose(ps[:, 4, 0:48], nrow[0:48, :], ident[0:48, 0:48]).then_inc(sem("cols_mm"), 1)
            for tt, (s, n) in enumerate(TILES):
                pe.wait_ge(sem(f"x_loaded{tt % 2}"), 16 * (tt // 2 + 1))
                for b in range(2):
                    if tt >= 2:
                        pe.wait_ge(sem(("xt_v", "xt_a")[b]), tt - 1)
                    for f in range(4):
                        mm = pe.transpose(ps[:, (2 * tt + b) % 4, f * P:f * P + n], xin[0:n, tt % 2, (4 * b + f) * P:(4 * b + f + 1) * P],
                                          ident[0:n, 0:n])
                    mm.then_inc(sem("xt_mm"), 1)
            pe.wait_ge(sem("cols_made"), 1)
            prep_pe(pe)
            pe.wait_ge(sem("par_made"), 1)
            pe.wait_ge(sem("ct_made"), 8)
            pe.wait_ge(sem("xt_v"), 9)
            pe.wait_ge(sem("xt_a"), 9)
            norm_pe(pe, 0)
            for t in range(4):
                pe_single(pe, t, ready=h_ready(0)(pe) if t == 0 else None)
            with pe.Fori(0, 4) as i:
                for t in range(4, 8):
                    pe_single(pe, t, i, 4)
            tr_pe(pe)
            at_pe(pe)
            pe.wait_ge(sem("o_lo"), 12)
            pe.wait_ge(sem("mix_lo"), 4 * NC)
            for t in range(8):
                pe_single(pe, SLAB_OUT + t)
            norm_pe(pe, 1)
            ffn_pe(pe, F[0])
            norm_pe(pe, 2)
            s5_pe(pe)
            glu_pe(pe)
            pe.wait_ge(sem("glu_res"), NC * KD)
            norm_pe(pe, 3)
            ffn_pe(pe, F[1])
            norm_pe(pe, 4)
            out_pe(pe)


_INS = ["x_prompt", "x_sample", "cache_sb_k", "cache_sb_v", "state_ssm_re", "state_ssm_im", "norm_mix", "norm_ffn",
        "norm_final", "ab_w_in", "sgu_w", "sgu_b", "ab_w_out", "ssm_lam_re", "ssm_lam_im", "ssm_log_step", "ssm_b_re",
        "ssm_b_im", "ssm_c_re", "ssm_c_im", "ssm_d", "ssm_w_glu", "ffn_w_gate", "ffn_w_up", "ffn_w_down"]
_OUTS = {"y_p": (1, 1024, 1024), "y_s": (1, 64, 1024), "k_p": (1, 1, 1024, 8, 64), "v_p": (1, 1, 1024, 8, 64),
         "k_s": (1, 1, 64, 8, 64), "v_s": (1, 1, 64, 8, 64), "g_s": (1, 1, 64, 512), "re_p": (1, 1, 64, 64),
         "im_p": (1, 1, 64, 64), "re_s": (1, 1, 64, 64), "im_s": (1, 1, 64, 64)}


def kernel(**inputs):
    import numpy as np
    from concourse import bacc
    from concourse.bass_utils import run_bass_kernel_spmd

    nc = bacc.Bacc("TRN2", target_bir_lowering=False, num_devices=1)
    arrays, ins = {}, {}
    for name in _INS:
        a = np.ascontiguousarray(inputs[name])
        arrays[f"in_{name}"] = a
        ins[name] = nc.dram_tensor(f"in_{name}", a.shape, F32, kind="ExternalInput").ap()
    outs = {name: nc.dram_tensor(f"out_{name}", shape, F32, kind="ExternalOutput").ap() for name, shape in _OUTS.items()}
    build(nc, ins, outs)
    r = run_bass_kernel_spmd(nc, [arrays], core_ids=[0])
    return tuple(r.results[0][f"out_{name}"] for name in _OUTS)
```

```python
from contextlib import ExitStack

import concourse.bass as bass
from concourse import mybir
from concourse.alu_op_type import AluOpType as ALU

F32 = mybir.dt.float32
F32R = mybir.dt.float32r
ACT = mybir.ActivationFunctionType

P = 128
D = 1024
KD = D // P
SEQ, DEC = 1024, 64
T = SEQ + DEC
TILES = [(i * P, min(P, T - i * P)) for i in range((T + P - 1) // P)]
CHUNKS = [(0, 384), (384, 384), (768, 320)]
NC = len(CHUNKS)
HD = 64
HEADS = 8
SB = HEADS * HD
PAST = 512
QT, KT, VT, UT, GT = 0, 4, 8, 12, 16
IN_TILES = 20
FF = 2816
PARTS = FF // (2 * P)
EPS = 1e-6
NEG = -1.0e30
GELU = ACT.Gelu_apprx_tanh
L = 8
NCH = T // L
CW = (L + 1) * 16
GP = 32
TWO_PI = 6.283185307179586
TURN = (6.28125, 0.0019350051879882812, 3.019916050e-07)
MAGIC = 12582912.0

SLAB_OUT = IN_TILES
SLAB_FF0 = SLAB_OUT + KD
PART_SLABS = 6
SLAB_GLU = SLAB_FF0 + PARTS * PART_SLABS
SLAB_FF1 = SLAB_GLU + 2 * KD
SLAB_END = SLAB_FF1 + PARTS * PART_SLABS
ACC_OUT = IN_TILES * NC
ACC_FF0 = ACC_OUT + KD * NC
ACC_FF1 = ACC_FF0 + PARTS * KD * NC
PAIR_GLU = 2 * PARTS * NC
PAIR_FF1 = PAIR_GLU + KD * NC


def slot(t):
    return t % 4 if t < SLAB_FF0 else (t - SLAB_FF0 + 4) % 6


def step(c, i, b):
    return c if i is None else c + i * b


def build(nc, A, O):
    with ExitStack() as ctx:
        sems = {}

        def sem(name):
            if name not in sems:
                sems[name] = ctx.enter_context(nc.semaphore(name))
            return sems[name]

        SIZE = 53200 * 4
        ctx.enter_context(nc.sbuf_tensor("arena", [P, SIZE // 4], F32))
        base = nc.sbuf_base - SIZE

        def plan(off, *specs):
            got = []
            for name, shape, dt in specs:
                n = 4
                for s in shape[1:]:
                    n *= s
                assert off + n <= SIZE, (name, off + n)
                got.append(nc.alloc_sbuf_tensor_at(name, shape, dt, offset=base + off))
                off += n
            return got + [off]

        ident, ones, cols, off = plan(0, ("ident", [P, P], F32), ("ones", [P, P], F32), ("cols", [P, 64], F32))
        off_a = off
        abuf, fbuf, rms, off = plan(off, ("abuf", [P, 2, 384], F32), ("fbuf", [P, 2, 384], F32), ("rms", [P, 2, 384], F32))
        raw, off_w = plan(off, ("raw", [P, 2, D], F32))
        whi, wlo, off_h = plan(off_w, ("whi", [P, 6, D], F32R), ("wlo", [P, 6, D], F32R))
        hhi, hlo, off_x = plan(off_h, ("hhi", [P, KD * T], F32R), ("hlo", [P, KD * T], F32R))
        x, off_g = plan(off_x, ("x", [P, KD * T], F32))
        gh, gl, off_end = plan(off_g, ("gh", [P, 4 * T], F32R), ("gl", [P, 4 * T], F32R))
        xin, nrow, _ = plan(off_g, ("xin", [P, 2, D], F32), ("nrow", [P, P], F32))
        zst, _ = plan(off_g, ("zst", [P, 2, T], F32))
        zt, tok, wsr, wsT, bT, ug, mg, tri0, _ = plan(
            off_x, ("zt", [P, 2, T], F32), ("tok", [P, 2, 9, P], F32), ("wsr", [P, 8, P], F32), ("wsT", [P, 8, P], F32),
            ("bT", [P, 4, P], F32), ("ug", [P, 2, T], F32), ("mg", [P, 2, 384], F32), ("tri0", [P, P], F32))
        KCOL = T + 64 + PAST
        kS, qS, kst, oa = plan(
            off_x, ("kS", [P, 4, KCOL], F32R),
            ("qS", [P, 4, 2, T], F32R),
            ("kst", [P, T + PAST], F32))
        assert oa <= off_end
        tri, comp, qst, oa = plan(off_a, ("tri", [P, P], F32R), ("comp", [P, P], F32R), ("qst", [P, T], F32))
        assert oa <= off_a + 2 * 3072
        off_raw = off_w - 2 * D * 4
        esp, tz, sphi, vv, oa = plan(off_raw, ("esp", [P, 4, 2, 512], F32), ("tz", [P, 4, 2, 512], F32),
                                     ("sphi", [P, 2, 2, 512], F32R), ("vv", [P, 2, 13, P], F32))
        assert oa <= off_h
        splo, _ = plan(off_raw, ("splo", [P, 4, 2, 512], F32R))

        eb, bo, co_, pb, _ = plan(off_x, ("eb", [P, 3, 8, NCH], F32), ("bo", [P, 8, 2, P], F32), ("co", [P, 8, 2, CW], F32),
                                  ("pb", [P, 2, GP, L], F32))
        assert _ <= off_g
        ct, bb, pc, sc, ek, par, pp, off_t, = plan(
            off_g + 2 * T * 4, ("ct", [P, 2, GP, 16], F32), ("bb", [P, 2, GP, 16], F32), ("pc", [P, 2, GP, L + 1], F32),
            ("sc", [P, 20, GP], F32), ("ek", [P, 2, GP, 7], F32), ("par", [P, 5, GP], F32), ("pp", [P, 4, GP], F32))
        t1, t2, _ = plan(off_t, ("t1", [P, 8 * CW], F32), ("t2", [P, 8 * CW], F32))
        assert _ <= off_end
        lt, craw, lstep, _ = plan(off_t, ("lt", [P, 5, P], F32), ("craw", [P, 2, 8, 64], F32), ("lstep", [P, 2], F32))
        (S_step, S_mag, S_lrs, S_r8, S_sin, S_cos, S_ang, S_k, S_r, S_rc, S_a, S_b, S_c, S_nr, S_cor, S_coi, *S_ef) = (
            sc[:, n, :] for n in range(20))
        S_e, S_f = S_ef[0:2], S_ef[2:4]
        br, bt, _ = plan(off_w, ("br", [P, 4, 2, P], F32), ("bt", [P, 4, 2, P], F32))
        tm, kt, p4, _ = plan(off_w + 6 * D * 4, ("tm", [P, 2, 8, P], F32), ("kt", [P, 8, P], F32), ("p4", [P, 4, GP], F32))
        u, ca, sh, zb1, oa = plan(off_h, ("u", [P, 2, 8, NCH], F32), ("ca", [P, 2, 4, 2, CW], F32), ("sh", [P, 2, 2, 4, NCH], F32),
                                  ("zb1", [P, T], F32))
        assert oa <= off_h + KD * T * 4
        yp, _ = plan(off_h + KD * T * 4, ("yp", [P, KD * T], F32))
        e3, xx, v1, v2, v3, w1, w2, yy, zb0, oa = plan(
            off_x, ("e3", [P, 3, 4, NCH], F32), ("xx", [P, 8 * NCH], F32), ("v1", [P, 4 * NCH], F32), ("v2", [P, 4 * NCH], F32),
            ("v3", [P, 4 * NCH], F32), ("w1", [P, 4 * NCH], F32), ("w2", [P, 4 * NCH], F32), ("yy", [P, 2, 8, NCH], F32),
            ("zb0", [P, T], F32))
        assert oa <= off_g
        zb = [zb0, zb1]
        v1, v2, v3, w1, w2 = v1[:], v2[:], v3[:], w1[:], w2[:]
        hp, _ = plan(off_g, ("hp", [P, KD * T], F32))
        fin, fout, _ = plan(off_w - 2 * D * 4 - 3072, ("fin", [P, 4, GP], F32), ("fout", [P, 4, P], F32))
        yf, _ = plan(off_h, ("yf", [P, KD * T], F32))
        yo, _ = plan(off_g, ("yo", [P, 2, D], F32))

        ps = ctx.enter_context(nc.psum_tensor("ps", [P, 8, 512], F32))

        zT = nc.dram_tensor("zT", [IN_TILES * P, T], F32).ap()
        kcT = nc.dram_tensor("kcT", [SB, PAST], F32).ap()
        dE = nc.dram_tensor("dE", [P, 3, GP, NCH], F32).ap()
        dB = nc.dram_tensor("dB", [P, GP, 2, P], F32).ap()
        dC = nc.dram_tensor("dC", [P, GP, 2, CW], F32).ap()
        dP = nc.dram_tensor("dP", [P, 4, GP], F32).ap()
        dU = nc.dram_tensor("dU", [KD * P, T], F32).ap()
        dY = nc.dram_tensor("dY", [KD * P, T], F32).ap()
        xs = nc.dram_tensor("xs", [P, KD * T], F32).ap()

        xp = A["x_prompt"].rearrange("b t d -> (b t) d")
        xd = A["x_sample"].rearrange("b t d -> (b t) d")

        x3 = x[:].rearrange("p (f t) -> p f t", f=KD)
        epsb = cols[:, 48:49]
        dneg = rms[:, 1, 0:P]

        def kview(w):
            return w.rearrange("(k p) n -> p k n", p=P)

        w_in, w_out = kview(A["ab_w_in"][0]), kview(A["ab_w_out"][0])
        w_gate = [kview(A["ffn_w_gate"][l]) for l in range(2)]
        w_up = [kview(A["ffn_w_up"][l]) for l in range(2)]
        w_down = [A["ffn_w_down"][l] for l in range(2)]
        w_glu = kview(A["ssm_w_glu"][0])
        k_new = [O["k_p"].rearrange("a b t h d -> (a b t) (h d)"), O["k_s"].rearrange("a b t h d -> (a b t) (h d)")]
        v_new = [O["v_p"].rearrange("a b t h d -> (a b t) (h d)"), O["v_s"].rearrange("a b t h d -> (a b t) (h d)")]
        g_new = O["g_s"].rearrange("a b t d -> (a b t) d")
        y_new = [O["y_p"].rearrange("b t d -> (b t) d"), O["y_s"].rearrange("b t d -> (b t) d")]
        ck = A["cache_sb_k"].rearrange("a b t h d -> (a b t) (h d)")
        cv = A["cache_sb_v"].rearrange("a b t h d -> (a b t) (h d)")

        def xcol(m, c, buf=x):
            s, n = CHUNKS[c]
            return buf[:, bass.ds(m * T + s, n)]

        def load_slab(sp, t, src, i=None, b=0):
            if t >= 2:
                sp.wait_ge(sem("w_lo"), step(t - 1, i, b))
            dst = raw[:, t % 2, :]
            if len(src.shape) == 3:
                dst = dst.rearrange("p (k n) -> p k n", k=KD)
            sp.dma_start(dst, src).then_inc(sem(f"raw_loaded{t % 2}"), 16)

        def slab_hi(act, t, left=None, count=0, i=None, b=0, per=0):
            act.wait_ge(sem(f"raw_loaded{t % 2}"), step(16 * (t // 2 + 1), i, 8 * b))
            if left:
                act.wait_ge(sem(left), step(count, i, per))
            act.activation(whi[:, slot(t), :], raw[:, t % 2, :], ACT.Copy).then_inc(sem("w_hi"), 1)

        def slab_lo(pool, t, i=None, b=0):
            pool.wait_ge(sem("w_hi"), step(t + 1, i, b))
            pool.tensor_tensor(wlo[:, slot(t), :], raw[:, t % 2, :], whi[:, slot(t), :].bitcast(F32),
                               ALU.subtract).then_inc(sem("w_lo"), 1)

        def three(pe, out, s, col, rh, rl, first, last):
            wh, wl = whi[:, s, col:col + P], wlo[:, s, col:col + P]
            pe.matmul(out, wh, rh, start=first, stop=False)
            pe.matmul(out, wh, rl, start=False, stop=False)
            return pe.matmul(out, wl, rh, start=False, stop=last)

        def eight(pe, out, s, c):
            s0, n = CHUNKS[c]
            for k in range(KD):
                o = k * T + s0
                mm = three(pe, out[:, 0:n], s, k * P, hhi[:, o:o + n], hlo[:, o:o + n], k == 0, k == KD - 1)
            return mm

        def acc(v):
            return ps[:, 4 + v % 4, :]

        def pe_single(pe, t, i=None, b=0, ready=None):
            pe.wait_ge(sem("w_lo"), step(t + 1, i, b))
            for c in range(NC):
                v = NC * t + c
                if ready:
                    ready(c)
                if v >= 4:
                    pe.wait_ge(sem("acc_used"), step(v - 3, i, NC * b))
                eight(pe, acc(v), slot(t), c).then_inc(sem("acc_ready"), 1)

        def pe_pair(pe, t, v0, i=None, b=0, per=0, ready=None):
            pe.wait_ge(sem("w_lo"), step(t + 2, i, b))
            for c in range(NC):
                v = v0 + c
                if ready:
                    ready(c)
                if v >= 2:
                    pe.wait_ge(sem("pair_used"), step(v - 1, i, per))
                eight(pe, ps[:, 2 * (v % 2), :], slot(t), c)
                eight(pe, ps[:, 2 * (v % 2) + 1, :], slot(t + 1), c).then_inc(sem("pair_ready"), 1)

        SPLIT = {0: 0, 1: 1, 3: 2}

        def n_units(k, e=NC * KD):
            return NC * KD * k + e

        def n_split(k, e=NC * KD):
            return NC * KD * SPLIT[k] + e

        def norm_act(act, k, xin_ready, split, hlast=None):
            def squares(c):
                s, n = CHUNKS[c]
                xin_ready(act, c)
                for f in range(KD):
                    e = c * KD + f
                    if e >= 2:
                        act.wait_ge(sem("n_sum"), n_units(k, e - 1))
                    act.activation(abuf[:, e % 2, 0:n], x[:, f * T + s:f * T + s + n], ACT.Square).then_inc(sem("n_sq"), 1)

            def root(c):
                n = CHUNKS[c][1]
                act.wait_ge(sem("n_sum"), n_units(k, KD * (c + 1)))
                if c >= 2:
                    act.wait_ge(sem("n_f"), n_units(k, KD * (c - 1)))
                act.activation(rms[:, c % 2, 0:n], ps[:, c, 0:n], ACT.Sqrt, bias=epsb[:, 0:1], scale=1.0 / D).then_inc(sem("n_rt"), 1)

            def his(c):
                s, n = CHUNKS[c]
                for f in range(KD):
                    e = c * KD + f
                    act.wait_ge(sem("n_f"), n_units(k, e + 1))
                    act.activation(hhi[:, f * T + s:f * T + s + n], fbuf[:, e % 2, 0:n], ACT.Copy).then_inc(sem("n_hi"), 1)

            squares(0)
            root(0)
            squares(1)
            root(1)
            squares(2)
            if split:
                his(0)
            root(2)
            if split:
                his(1)
                his(2)

        def norm_pe(pe, k):
            pe.wait_ge(sem("consts"), 1)
            for c, (s, n) in enumerate(CHUNKS):
                for f in range(KD):
                    pe.wait_ge(sem("n_sq"), n_units(k, c * KD + f + 1))
                    pe.matmul(ps[:, c, 0:n], ones[:], abuf[:, (c * KD + f) % 2, 0:n], start=f == 0,
                              stop=f == KD - 1).then_inc(sem("n_sum"), 1)

        def norm_dve(dve, k, row, plain=None, by_chunk=False):
            for c, (s, n) in enumerate(CHUNKS):
                dve.wait_ge(sem("n_rt"), NC * k + c + 1)
                dve.reciprocal(rms[:, c % 2, 0:n], rms[:, c % 2, 0:n]).then_inc(sem("n_rr"), 1)
                dve.wait_ge(sem("n_rr"), NC * k + c + 1)
                for f in range(KD):
                    e = c * KD + f
                    out = fbuf[:, e % 2, 0:n]
                    if plain is not None:
                        out = plain[:, f * T + s:f * T + s + n]
                    elif e >= 2:
                        dve.wait_ge(sem("n_lo"), n_split(k, e - 1))
                    xf, rf = x[:, f * T + s:f * T + s + n], rms[:, c % 2, 0:n]
                    if by_chunk:
                        out = plain[:, f * T:(f + 1) * T].rearrange("p (s n) -> p n s", s=L)[:, s // L:(s + n) // L, :]
                        xf, rf = (v.rearrange("p (n s) -> p n s", s=L) for v in (xf, rf))
                    dve.scalar_tensor_tensor(out, xf, cols[:, row + f:row + f + 1], rf, ALU.mult, ALU.mult).then_inc(sem("n_f"), 1)

        def norm_pool(pool, k):
            for c, (s, n) in enumerate(CHUNKS):
                for f in range(KD):
                    e = c * KD + f
                    o = f * T + s
                    pool.wait_ge(sem("n_hi"), n_split(k, e + 1))
                    pool.tensor_tensor(hlo[:, o:o + n], fbuf[:, e % 2, 0:n], hhi[:, o:o + n].bitcast(F32),
                                       ALU.subtract).then_inc(sem("n_lo"), 1)

        def h_ready(k):
            return lambda eng: (lambda c: eng.wait_ge(sem("n_lo"), n_split(k, KD * (c + 1))))

        class Ffn:
            def __init__(self, layer):
                self.l = layer
                self.slab = (SLAB_FF0, SLAB_FF1)[layer]
                self.pair = (0, PAIR_FF1)[layer]
                self.acc = (ACC_FF0, ACC_FF1)[layer]
                self.hid = (0, 2 * PARTS * NC)[layer]
                self.norm = (1, 3)[layer]

        F = [Ffn(0), Ffn(1)]

        def ffn_sp(sp, f, skip=0):
            def gu(tile, t, i=None):
                o = step(tile * P, i, 2 * P)
                for w, tt in ((w_gate[f.l], t), (w_up[f.l], t + 1)):
                    load_slab(sp, tt, w[:, :, bass.ds(o, P)] if i is not None else w[:, :, o:o + P], i, 6)

            def down(tile, t, i=None):
                for j in range(2):
                    o = step((tile + j) * P, i, 2 * P)
                    load_slab(sp, t + j, w_down[f.l][bass.ds(o, P), :] if i is not None else w_down[f.l][o:o + P, :], i, 6)

            if not skip:
                gu(0, f.slab)
                return
            gu(1, f.slab + 2)
            with sp.Fori(0, PARTS - 1) as i:
                gu(2, f.slab + 4, i)
                gu(3, f.slab + 6, i)
                down(0, f.slab + 8, i)
            down(2 * PARTS - 2, f.slab + 64)

        def ffn_act(act, f, start_sem, start_count):
            def silu(v0, i=None):
                for c, (s, n) in enumerate(CHUNKS):
                    v = v0 + c
                    act.wait_ge(sem("pair_ready"), step(v + 1, i, 6))
                    if v >= 2:
                        act.wait_ge(sem("pair_used"), step(v - 1, i, 6))
                    act.activation(abuf[:, v % 2, 0:n], ps[:, 2 * (v % 2), 0:n], ACT.Silu).then_inc(sem("pair_act"), 1)

            for q in range(2):
                for j in range(2):
                    slab_hi(act, f.slab + 2 * q + 2 + j, start_sem, start_count)
                silu(f.pair + NC * q)
            with act.Fori(0, PARTS - 1) as i:
                t = f.slab + 4
                for j in range(2):
                    slab_hi(act, t + 2 + j, "pair_ready", f.pair + 2 * NC, i, 6, 6)
                silu(f.pair + 2 * NC, i)
                for j in range(2):
                    slab_hi(act, t + 4 + j, "acc_ready", f.acc, i, 6, KD * NC)
                silu(f.pair + 3 * NC, i)
                for j in range(2):
                    slab_hi(act, t + 6 + j, "pair_ready", f.pair + 3 * NC, i, 6, 6)
            if f.l == 0:
                for j in range(2):
                    slab_hi(act, SLAB_GLU + j, "pair_ready", PAIR_GLU)

        def ffn_pool(pool, f):
            def lo(v0, half, i=None):
                for c, (s, n) in enumerate(CHUNKS):
                    v, h = v0 + c, f.hid + v0 - f.pair + c
                    o = (half if i is None else ((i + 1) % 2) * (2 * T) + half) + s
                    pool.wait_ge(sem("hid_hi"), step(h + 1, i, 6))
                    pool.tensor_tensor(gl[:, bass.ds(o, n)], fbuf[:, v % 2, 0:n], gh[:, bass.ds(o, n)].bitcast(F32),
                                       ALU.subtract).then_inc(sem("hid_lo"), 1)

            for q in range(2):
                for j in range(2):
                    slab_lo(pool, f.slab + 2 * q + 2 + j)
                lo(f.pair + NC * q, q * T)
            with pool.Fori(0, PARTS - 1) as i:
                t = f.slab + 4
                for q in range(2):
                    for j in range(2):
                        slab_lo(pool, t + 2 * q + 2 + j, i, 6)
                    lo(f.pair + (2 + q) * NC, q * T, i)
                for j in range(2):
                    slab_lo(pool, t + 6 + j, i, 6)
            if f.l == 0:
                for j in range(2):
                    slab_lo(pool, SLAB_GLU + j)

        def ffn_pe(pe, f):
            def down(t, v0, h0, i=None, buf=None):
                buf = (i % 2) * (2 * T) if buf is None else buf
                pe.wait_ge(sem("w_lo"), step(t + 2, i, 6))
                for c, (s, n) in enumerate(CHUNKS):
                    pe.wait_ge(sem("hid_lo"), step(h0 + c + 1, i, 6))
                    for m in range(KD):
                        v = v0 + c * KD + m
                        pe.wait_ge(sem("acc_used"), step(v - 3, i, KD * NC))
                        for j in range(2):
                            o = buf + j * T + s
                            mm = three(pe, acc(v)[:, 0:n], slot(t + j), m * P, gh[:, bass.ds(o, n)], gl[:, bass.ds(o, n)],
                                       j == 0, j == 1)
                        mm.then_inc(sem("acc_ready"), 1)

            pe_pair(pe, f.slab, f.pair, ready=h_ready(f.norm)(pe))
            pe_pair(pe, f.slab + 2, f.pair + NC)
            with pe.Fori(0, PARTS - 1) as i:
                pe_pair(pe, f.slab + 4, f.pair + 2 * NC, i, 6, 6)
                pe_pair(pe, f.slab + 6, f.pair + 3 * NC, i, 6, 6)
                down(f.slab + 8, f.acc, f.hid + NC, i)
            down(f.slab + 64, f.acc + (PARTS - 1) * KD * NC, f.hid + NC * (2 * PARTS - 1), buf=((PARTS - 1) % 2) * 2 * T)

        def ffn_dve(dve, f):
            def hidden(v0, half, i=None):
                for c, (s, n) in enumerate(CHUNKS):
                    v, h = v0 + c, f.hid + v0 - f.pair + c
                    o = (half if i is None else ((i + 1) % 2) * (2 * T) + half) + s
                    dve.wait_ge(sem("pair_act"), step(v + 1, i, 6))
                    if h >= 2:
                        dve.wait_ge(sem("hid_lo"), step(h - 1, i, 6))
                    dve.tensor_tensor(fbuf[:, v % 2, 0:n], ps[:, 2 * (v % 2) + 1, 0:n], abuf[:, v % 2, 0:n],
                                      ALU.mult).then_inc(sem("pair_used"), 1)
                    dve.wait_ge(sem("pair_used"), step(v + 1, i, 6))
                    dve.tensor_copy(gh[:, bass.ds(o, n)], fbuf[:, v % 2, 0:n]).then_inc(sem("hid_hi"), 1)

            def residual(v0, i=None):
                for c, (s, n) in enumerate(CHUNKS):
                    for m in range(KD):
                        v = v0 + c * KD + m
                        dve.wait_ge(sem("acc_ready"), step(v + 1, i, KD * NC))
                        xo = x[:, m * T + s:m * T + s + n]
                        dve.tensor_tensor(xo, acc(v)[:, 0:n], xo, ALU.add).then_inc(sem("acc_used"), 1)

            dve.wait_ge(sem("n_lo"), n_split(f.norm))
            hidden(f.pair, 0)
            hidden(f.pair + NC, T)
            with dve.Fori(0, PARTS - 1) as i:
                hidden(f.pair + 2 * NC, 0, i)
                hidden(f.pair + 3 * NC, T, i)
                residual(f.acc, i)
            residual(f.acc + (PARTS - 1) * KD * NC)

        def zrow(n):
            return (KT + n if n < 8 else GT + n - 12) * P

        tp_units = [(n, b) for n in range(16) for b in range(1 if 8 <= n < 12 else NC)]
        tp_no = {nb: u for u, nb in enumerate(tp_units)}
        TP_V = sum(n < 12 for n, _ in tp_units)

        def tp_taken(eng, u):
            if u < TP_V:
                eng.wait_ge(sem("tp_used_v"), u + 1)
            else:
                eng.wait_ge(sem("tp_used_a"), u + 1 - TP_V)

        def tr_sp(sp):
            for n in range(3):
                sp.wait_ge(sem(f"prep_out{n}"), 64)
            sp.wait_ge(sem("z_stored0"), 16 * IN_TILES // 2)
            sp.wait_ge(sem("z_stored1"), 16 * IN_TILES // 2)
            sp.dma_start(wsr[:], A["sgu_w"][0].rearrange("g t s -> t g s")).then_inc(sem("ws_loaded"), 16)
            for j in range(4):
                for a in range(2):
                    sp.dma_start(bT[64 * a:64 * a + 64, j, :], A["sgu_b"][0, 2 * j + a:2 * j + a + 1, :].to_broadcast([64, P])
                                 ).then_inc(sem("bT_loaded"), 16)
            for n in range(17):
                if n < 16:
                    if n >= 2:
                        sp.wait_ge(sem("tp_mm"), tp_no[(n - 1, 0)])
                    if 8 <= n < 12:
                        sp.dma_start(zt[:, n % 2, 0:512].rearrange("p (b n) -> p b n", b=4),
                                     ck[:, (n - 8) * P:(n - 7) * P].rearrange("(b p) n -> p b n", p=P)).then_inc(sem(f"zt_loaded{n % 2}"), 16)
                    else:
                        sp.dma_start(zt[:, n % 2, :], zT[zrow(n):zrow(n) + P, :]).then_inc(sem(f"zt_loaded{n % 2}"), 16)
                    if n >= 12:
                        j = n - 12
                        if j >= 2:
                            sp.wait_ge(sem("mix_f"), 2 * NC * (j - 1))
                        sp.dma_start(ug[:, j % 2, :], zT[(UT + j) * P:(UT + j + 1) * P, :]).then_inc(sem(f"ug_loaded{j % 2}"), 16)
                if n >= 1:
                    m = n - 1
                    tp_taken(sp, tp_no[(m, 0 if 8 <= m < 12 else 2)])
                    cs = slice((m % 4) * P, (m % 4 + 1) * P)
                    if m < 8:
                        dst = (k_new, v_new)[m // 4]
                        sp.dma_start(dst[0][:, cs].rearrange("(t p) n -> p t n", p=P), tok[:, m % 2, 0:8, :]).then_inc(sem(f"tok_out{m % 2}"), 16)
                        sp.dma_start(dst[1][:, cs], tok[0:DEC, m % 2, 8, :]).then_inc(sem(f"tok_out{m % 2}"), 16)
                    elif m < 12:
                        sp.dma_start(kcT[cs, :], tok[:, m % 2, 0:4, :].rearrange("p b n -> p (b n)")).then_inc(sem(f"tok_out{m % 2}"), 16)
                    else:
                        sp.dma_start(g_new[:, cs], tok[0:DEC, m % 2, 8, :]).then_inc(sem(f"tok_out{m % 2}"), 16)

        def tok_free(eng, n):
            if n >= 2:
                done = sum((32 if m < 8 else 16) for m in range(n - 1) if m % 2 == n % 2)
                eng.wait_ge(sem(f"tok_out{n % 2}"), done)
            if n >= 14:
                eng.wait_ge(sem("mix_mm"), NC * (n - 13))

        def tr_pe(pe):
            pe.wait_ge(sem("ws_loaded"), 16)
            pe.wait_ge(sem("acc_used"), NC * IN_TILES)
            for g in range(8):
                mm = pe.transpose(ps[:, 6 + g // 4, (g % 4) * P:(g % 4 + 1) * P], wsr[:, g, :], ident[:])
            mm.then_inc(sem("ws_mm"), 1)
            for u, (n, b) in enumerate(tp_units):
                if b == 0:
                    pe.wait_ge(sem(f"zt_loaded{n % 2}"), 16 * (n // 2 + 1))
                if u >= 6:
                    tp_taken(pe, u - 6)
                for r in range(4 if 8 <= n < 12 else 3):
                    if 8 <= n < 12:
                        mm = pe.transpose(ps[:, u % 6, r * P:(r + 1) * P], zt[:, n % 2, r * P:(r + 1) * P], ident[:])
                    else:
                        s, w = TILES[3 * b + r]
                        mm = pe.transpose(ps[0:w, u % 6, r * P:(r + 1) * P], zt[:, n % 2, s:s + w], ident[:])
                mm.then_inc(sem("tp_mm"), 1)
                if n >= 12 and b == 2:
                    gate_pe(pe, n - 12)

        def gate_pe(pe, j):
            tp_taken(pe, tp_no[(12 + j, 2)])
            pe.wait_ge(sem("ws_t"), 8)
            for c in range(NC):
                s = NC * j + c
                if s >= 2:
                    pe.wait_ge(sem("mix_f"), 2 * (s - 1) - 1)
                for r in range(3):
                    w = TILES[3 * c + r][1]
                    for a in range(2):
                        mm = pe.matmul(ps[64 * a:64 * a + 64, 6 + s % 2, r * P:r * P + w],
                                       tok[0:w, (12 + j) % 2, 3 * c + r, 64 * a:64 * a + 64], wsT[0:w, 2 * j + a, 0:w],
                                       start=True, stop=True, skip_group_check=True)
                mm.then_inc(sem("mix_mm"), 1)

        def tr_dve(dve):
            dve.wait_ge(sem("ws_mm"), 1)
            dve.wait_ge(sem("tri0_made"), 1)
            for g in range(8):
                dve.tensor_tensor(wsT[:, g, :], ps[:, 6 + g // 4, (g % 4) * P:(g % 4 + 1) * P], tri0[:], ALU.mult).then_inc(sem("ws_t"), 1)
            for u, (n, b) in enumerate(tp_units[:TP_V]):
                if b == 0:
                    tok_free(dve, n)
                dve.wait_ge(sem("tp_mm"), u + 1)
                if 8 <= n < 12:
                    dve.tensor_copy(tok[:, n % 2, 0:4, :], ps[:, u % 6, 0:512].rearrange("p (b n) -> p b n", b=4)).then_inc(sem("tp_used_v"), 1)
                elif b < 2:
                    dve.tensor_copy(tok[:, n % 2, 3 * b:3 * b + 3, :], ps[:, u % 6, 0:384].rearrange("p (b n) -> p b n", b=3)
                                    ).then_inc(sem("tp_used_v"), 1)
                else:
                    dve.tensor_copy(tok[0:DEC, n % 2, 8, :], ps[0:DEC, u % 6, 256:384]).then_inc(sem("tp_part"), 1)
                    dve.wait_ge(sem("tp_part"), sum(1 for m, bb in tp_units[:u + 1] if bb == 2))
                    dve.tensor_copy(tok[:, n % 2, 6:8, :], ps[:, u % 6, 0:256].rearrange("p (b n) -> p b n", b=2)).then_inc(sem("tp_used_v"), 1)
            dve.wait_ge(sem("bT_loaded"), 16 * 8)
            for s in range(4 * NC):
                j, c = divmod(s, NC)
                s0, n = CHUNKS[c]
                dve.wait_ge(sem("mix_mm"), s + 1)
                if s >= 2:
                    dve.wait_ge(sem("mix_lo"), s - 1)
                for r in range(3):
                    w = TILES[3 * c + r][1]
                    ins = dve.tensor_tensor(mg[:, s % 2, r * P:r * P + w], ps[:, 6 + s % 2, r * P:r * P + w], bT[:, j, 0:w], ALU.add)
                    ins.then_inc(sem("mix_f" if r == 2 else "mix_part"), 1)
                dve.wait_ge(sem("mix_f"), 2 * s + 1)
                dve.wait_ge(sem("mix_part"), 2 * s + 2)
                dve.wait_ge(sem("ug_act"), j + 1)
                dve.tensor_tensor(mg[:, s % 2, 0:n], mg[:, s % 2, 0:n], ug[:, j % 2, s0:s0 + n], ALU.mult).then_inc(sem("mix_f"), 1)

        def tr_act(act):
            for j in range(4):
                n = 12 + j
                act.wait_ge(sem(f"ug_loaded{j % 2}"), 16 * (j // 2 + 1))
                act.activation(ug[:, j % 2, :], ug[:, j % 2, :], GELU).then_inc(sem("ug_act"), 1)
                tok_free(act, n)
                for b in range(NC):
                    u = tp_no[(n, b)]
                    act.wait_ge(sem("tp_mm"), u + 1)
                    if b < 2:
                        act.activation(tok[:, n % 2, 3 * b:3 * b + 3, :], ps[:, u % 6, 0:384].rearrange("p (b n) -> p b n", b=3), GELU
                                       ).then_inc(sem("tp_used_a"), 1)
                    else:
                        act.activation(tok[0:DEC, n % 2, 8, :], ps[0:DEC, u % 6, 256:384], GELU).then_inc(sem("tp_part_a"), 1)
                        act.wait_ge(sem("tp_part_a"), j + 1)
                        act.activation(tok[:, n % 2, 6:8, :], ps[:, u % 6, 0:256].rearrange("p (b n) -> p b n", b=2), GELU
                                       ).then_inc(sem("tp_used_a"), 1)
                for c in range(NC):
                    s = NC * j + c
                    s0, w = CHUNKS[c]
                    act.wait_ge(sem("mix_f"), 2 * s + 2)
                    o = (4 + j) * T + s0
                    act.activation(hhi[:, o:o + w], mg[:, s % 2, 0:w], ACT.Copy).then_inc(sem("mix_hi"), 1)

        def tr_pool(pool):
            for n in range(3):
                pool.wait_ge(sem(f"prep_out{n}"), 64)
            pool.wait_ge(sem("p_out"), 16)
            pool.wait_ge(sem("z_stored0"), 16 * IN_TILES // 2)
            pool.wait_ge(sem("z_stored1"), 16 * IN_TILES // 2)
            pool.memset(tri0[:], 1.0).then_inc(sem("pool"), 1)
            pool.wait_ge(sem("pool"), POOL0 + 1)
            pool.affine_select(out=tri0[:], in_=tri0[:], compare_op=ALU.is_ge, fill=0.0, base=0, pattern=[[1, P]],
                               channel_multiplier=-1).then_inc(sem("tri0_made"), 1)
            for s in range(4 * NC):
                j, c = divmod(s, NC)
                s0, w = CHUNKS[c]
                o = (4 + j) * T + s0
                pool.wait_ge(sem("mix_hi"), s + 1)
                pool.tensor_tensor(hlo[:, o:o + w], mg[:, s % 2, 0:w], hhi[:, o:o + w].bitcast(F32), ALU.subtract).then_inc(sem("mix_lo"), 1)

        units = []
        for pr in range(HEADS // 2):
            for q0, w, blocks in ((0, 512, range(3, -1, -1)), (512, 512, range(7, -1, -1)), (SEQ, DEC, range(4, -1, -1))):
                blocks = list(blocks)
                for b in blocks:
                    if q0 < SEQ:
                        off = max(0, b * P - q0)
                        units.append(dict(pr=pr, q0=q0, off=off, w=w - off, kc=b * P, vb=b, diag=b * P >= q0))
                    else:
                        units.append(dict(pr=pr, q0=q0, off=0, w=w, kc=SEQ if b == 4 else T + 64 + b * P,
                                          vb=8 if b == 4 else 9 + b, diag=b == 4))
                    units[-1].update(first=b == blocks[0], last=b == blocks[-1], total=w)
        NU = len(units)
        PAIR_U = NU // (HEADS // 2)
        GROUPS = sum(v["last"] for v in units)
        LEAD = 3
        group_no = {i: sum(v["last"] for v in units[:i]) for i in range(NU)}
        diags = [sum(v["diag"] for v in units[:i]) for i in range(NU + 1)]
        prep_at = {PAIR_U * (g // 2 - 1) + 7 * (g % 2) + 3 * s + 1: (g, s) for g in range(2, HEADS) for s in range(2)}

        def copied(i):
            return i + 1 + diags[i + 1]

        def sums_used(eng, i):
            if units[i]["last"]:
                eng.wait_ge(sem("u_tri"), i + 1)
            else:
                eng.wait_ge(sem("u_rest"), i + 1 - group_no[i])

        def at_sp(sp):
            sp.wait_ge(sem("mix_lo"), 4 * NC)
            sp.wait_ge(sem("tok_out0"), sum((32 if m < 8 else 16) for m in range(0, 16, 2)))
            sp.wait_ge(sem("tok_out1"), sum((32 if m < 8 else 16) for m in range(1, 16, 2)))
            sp.wait_ge(sem("at_made"), 2)
            for g in range(HEADS):
                if g:
                    sp.wait_ge(sem("k_lo"), 2 * g)
                kr = slice((KT * P + g * HD), (KT * P + g * HD + HD))
                for a in range(2):
                    sp.dma_start(kst[64 * a:64 * a + 64, 0:T], zT[kr, :]).then_inc(sem("k_loaded"), 16)
                    sp.dma_start(kst[64 * a:64 * a + 64, T:T + PAST], kcT[g * HD:g * HD + HD, :]).then_inc(sem("k_loaded"), 16)
                if g:
                    sp.wait_ge(sem("q_lo"), 2 * g)
                for a in range(2):
                    sp.dma_start(qst[64 * a:64 * a + 64, :], zT[g * HD:g * HD + HD, :]).then_inc(sem("q_loaded"), 16)
                if g % 2 == 0:
                    pr = g // 2
                    if pr >= 2:
                        sp.wait_ge(sem("u_pv"), PAIR_U * (pr - 1))
                    cs = slice(pr * P, pr * P + P)
                    sp.dma_start(vv[:, pr % 2, 0:8, :], v_new[0][:, cs].rearrange("(t p) n -> p t n", p=P)).then_inc(sem("v_loaded"), 16)
                    sp.dma_start(vv[0:DEC, pr % 2, 8, :], v_new[1][:, cs]).then_inc(sem("v_loaded"), 16)
                    sp.dma_start(vv[:, pr % 2, 9:13, :], cv[:, cs].rearrange("(t p) n -> p t n", p=P)).then_inc(sem("v_loaded"), 16)
            sp.wait_ge(sem("u_pv"), NU)
            sp.wait_ge(sem("o_lo"), GROUPS)
            sp.dma_start(x[:], xs).then_inc(sem("x_back"), 16)

        def at_pool_make(pool):
            pool.wait_ge(sem("mix_lo"), 4 * NC)
            pool.wait_ge(sem("tok_out0"), sum((32 if m < 8 else 16) for m in range(0, 16, 2)))
            pool.wait_ge(sem("tok_out1"), sum((32 if m < 8 else 16) for m in range(1, 16, 2)))
            pool.memset(vv[:, :, 8, :], 0.0).then_inc(sem("pool"), 1)
            pool.memset(kS[:, :, T:T + 64].bitcast(F32), 0.0).then_inc(sem("pool"), 1)
            pool.memset(dneg, 0.0).then_inc(sem("pool"), 1)
            pool.memset(esp[:, 0, 0, 0:P], 1.0).then_inc(sem("pool"), 1)
            pool.memset(esp[:, 0, 1, 0:P], 1.0).then_inc(sem("pool"), 1)
            pool.wait_ge(sem("pool"), POOL0 + 6)
            pool.affine_select(out=dneg, in_=dneg, compare_op=ALU.is_gt, fill=NEG, base=0, pattern=[[1, P]],
                               channel_multiplier=-1).then_inc(sem("pool"), 1)
            pool.affine_select(out=esp[:, 0, 0, 0:P], in_=esp[:, 0, 0, 0:P], compare_op=ALU.is_ge, fill=0.0, base=0,
                               pattern=[[-1, P]], channel_multiplier=1).then_inc(sem("pool"), 1)
            pool.affine_select(out=esp[:, 0, 1, 0:P], in_=esp[:, 0, 1, 0:P], compare_op=ALU.is_gt, fill=0.0, base=0,
                               pattern=[[1, P]], channel_multiplier=-1).then_inc(sem("pool"), 1)
            pool.wait_ge(sem("pool"), POOL0 + 9)
            pool.tensor_copy(tri[:], esp[:, 0, 0, 0:P]).then_inc(sem("at_made"), 1)
            pool.tensor_copy(comp[:], esp[:, 0, 1, 0:P]).then_inc(sem("at_made"), 1)

        def pair_start(i):
            return i < NU and i % PAIR_U == 0

        def at_act(act):
            act.wait_ge(sem("at_made"), 2)
            nc.scalar.preload_act_table_set("natural_log_exp_and_others")

            def prepare(g, s):
                if s == 0:
                    act.wait_ge(sem("k_loaded"), 64 * (g + 1))
                    act.activation(kS[:, g % 4, 0:T], kst[:, 0:T], ACT.Copy).then_inc(sem("k_hi"), 1)
                    act.activation(kS[:, g % 4, T + 64:KCOL], kst[:, T:T + PAST], ACT.Copy).then_inc(sem("k_hi"), 1)
                else:
                    act.wait_ge(sem("q_loaded"), 32 * (g + 1))
                    for v in range(2):
                        act.activation(qS[:, g % 4, v, :], qst[:], ACT.Copy).then_inc(sem("q_hi"), 1)

            for g in range(2):
                for s in range(2):
                    prepare(g, s)
            for i in range(-LEAD, NU + 2):
                if 0 <= i < NU:
                    act.wait_ge(sem("u_t"), i + 1)
                    tb = tz[:, i % 4, :, 0:units[i]["w"]]
                    act.activation(tb, tb, ACT.Exp).then_inc(sem("u_w"), 1)
                if i >= 2 and units[i - 2]["last"]:
                    u, g = units[i - 2], group_no[i - 2]
                    act.wait_ge(sem("u_pv"), i - 1)
                    o = u["pr"] * T + u["q0"]
                    act.activation(hhi[:, o:o + u["total"]], ps[:, 6 + g % 2, 0:u["total"]], ACT.Copy).then_inc(sem("o_hi"), 1)
                n = i + LEAD
                if n < NU:
                    w = units[n]["w"]
                    e = esp[:, n % 4, :, 0:w]
                    act.wait_ge(sem("u_c"), copied(n))
                    if n >= 4:
                        sums_used(act, n - 4)
                    act.activation(e, tz[:, n % 4, :, 0:w], ACT.Abs).then_inc(sem("u_e"), 1)
                    act.wait_ge(sem("u_e"), 3 * n + 1)
                    act.activation(e, e, ACT.Exp, scale=-1.0).then_inc(sem("u_e"), 1)
                    act.wait_ge(sem("u_e"), 3 * n + 2)
                    act.activation(e, e, ACT.Ln, bias=1.0).then_inc(sem("u_e"), 1)
                if i in prep_at:
                    prepare(*prep_at[i])

        def at_dve(dve):
            for i in range(-LEAD, NU + 2):
                if 0 <= i < NU:
                    u, w = units[i], units[i]["w"]
                    tb = tz[:, i % 4, :, 0:w]
                    dve.wait_ge(sem("u_tri"), i + 1)
                    dve.tensor_tensor(tb, tb, ps[:, 4:6, u["off"]:u["off"] + w], ALU.subtract).then_inc(sem("u_t"), 1)
                n = i + 2
                if 0 <= n < NU:
                    w = units[n]["w"]
                    e = esp[:, n % 4, :, 0:w]
                    dve.wait_ge(sem("u_e"), 3 * n + 3)
                    dve.scalar_tensor_tensor(e, tz[:, n % 4, :, 0:w], 0.0, e, ALU.max, ALU.add).then_inc(sem("u_sp"), 1)
                c = i + LEAD
                if c < NU:
                    u, w = units[c], units[c]["w"]
                    tb = tz[:, c % 4, :, 0:w]
                    dve.wait_ge(sem("u_z"), c + 1)
                    if c >= 4:
                        dve.wait_ge(sem("u_pv"), c - 3)
                    b = 2 * (c % 2)
                    dve.tensor_scalar(tb, ps[:, b:b + 2, 0:w], HD ** -0.5, None, ALU.mult).then_inc(sem("u_c"), 1)
                    if u["diag"]:
                        dve.wait_ge(sem("u_c"), c + 1 + diags[c])
                        dw = min(P, w)
                        tb = tz[:, c % 4, :, 0:dw]
                        dve.tensor_tensor(tb, tb, dneg[:, 0:dw].unsqueeze(1).to_broadcast([P, 2, dw]), ALU.add).then_inc(sem("u_c"), 1)
                if 0 <= n < NU:
                    dve.wait_ge(sem("u_sp"), n + 1)
                    if n >= 2:
                        sums_used(dve, n - 2)
                    w = units[n]["w"]
                    dve.tensor_copy(sphi[:, n % 2, :, 0:w], esp[:, n % 4, :, 0:w]).then_inc(sem("u_sphi"), 1)
                if i >= 2 and units[i - 2]["last"]:
                    u, g = units[i - 2], group_no[i - 2]
                    dve.wait_ge(sem("o_hi"), g + 1)
                    o, m = u["pr"] * T + u["q0"], u["total"]
                    dve.tensor_tensor(hlo[:, o:o + m], ps[:, 6 + g % 2, 0:m], hhi[:, o:o + m].bitcast(F32), ALU.subtract
                                      ).then_inc(sem("o_lo"), 1)

        def at_pool(pool):
            def prepare(g, s):
                if s == 0:
                    pool.wait_ge(sem("k_hi"), 2 * g + 2)
                    for d0, s0, n in ((0, 0, T), (T + 64, T, PAST)):
                        kl = kS[64:P, g % 4, d0:d0 + n]
                        pool.tensor_tensor(kl, kst[64:P, s0:s0 + n], kl.bitcast(F32), ALU.subtract).then_inc(sem("k_lo"), 1)
                    pool.wait_ge(sem("k_lo"), 2 * g + 2)
                else:
                    pool.wait_ge(sem("q_hi"), 2 * g + 2)
                    for v in range(2):
                        r = slice(64, P) if v == 0 else slice(0, 64)
                        ql = qS[r, g % 4, v, :]
                        pool.tensor_tensor(ql, qst[r, :], ql.bitcast(F32), ALU.subtract).then_inc(sem("q_lo"), 1)
                        pool.wait_ge(sem("q_lo"), 2 * g + v + 1)

            for g in range(2):
                for s in range(2):
                    prepare(g, s)
            for i in range(-LEAD, NU):
                n = i + 2
                if 0 <= n < NU:
                    w = units[n]["w"]
                    pool.wait_ge(sem("u_sphi"), n + 1)
                    pool.tensor_tensor(splo[:, n % 4, :, 0:w], esp[:, n % 4, :, 0:w], sphi[:, n % 2, :, 0:w].bitcast(F32),
                                       ALU.subtract).then_inc(sem("u_splo"), 1)
                if i in prep_at:
                    pool.wait_ge(sem("u_splo"), n + 1)
                    prepare(*prep_at[i])

        def at_pe(pe):
            def scores(i):
                u = units[i]
                if i >= 2:
                    pe.wait_ge(sem("u_c"), copied(i - 2))
                if pair_start(i):
                    pe.wait_ge(sem("k_lo"), 4 * (u["pr"] + 1))
                    pe.wait_ge(sem("q_lo"), 4 * (u["pr"] + 1))
                h = 2 * (u["pr"] % 2)
                for a in range(2):
                    q = u["q0"] + u["off"]
                    out = ps[:, 2 * (i % 2) + a, 0:u["w"]]
                    pe.matmul(out, kS[:, h + a, u["kc"]:u["kc"] + P], qS[:, h + a, 0, q:q + u["w"]], start=True, stop=False)
                    mm = pe.matmul(out, kS[:, h + a, u["kc"]:u["kc"] + P], qS[:, h + a, 1, q:q + u["w"]], start=False, stop=True)
                mm.then_inc(sem("u_z"), 1)

            def sums(i, mat):
                u, w = units[i], units[i]["w"]
                for a in range(2):
                    out = ps[:, 4 + a, u["off"]:u["off"] + w]
                    for j, r in enumerate((sphi[:, i % 2, a, 0:w], splo[:, i % 4, a, 0:w])):
                        mm = pe.matmul(out, mat[:], r, start=mat is tri and u["first"] and j == 0, stop=True, skip_group_check=True)
                return mm

            def values(i):
                u, g = units[i], group_no[i]
                pe.wait_ge(sem("u_w"), i + 1)
                if u["first"] and g >= 2:
                    pe.wait_ge(sem("o_lo"), g - 1)
                if pair_start(i):
                    pe.wait_ge(sem("v_loaded"), 48 * (u["pr"] + 1))
                for a in range(2):
                    out = ps[64 * a:64 * a + 64, 6 + g % 2, u["off"]:u["off"] + u["w"]]
                    mm = pe.matmul(out, vv[:, u["pr"] % 2, u["vb"], 64 * a:64 * a + 64], tz[:, i % 4, a, 0:u["w"]],
                                   start=u["first"], stop=True, skip_group_check=True)
                mm.then_inc(sem("u_pv"), 1)

            pe.wait_ge(sem("at_made"), 2)
            pe.wait_ge(sem("mix_f"), 8 * NC)
            for i in range(-LEAD, NU + 1):
                if 0 <= i < NU:
                    pe.wait_ge(sem("u_splo"), i + 1)
                    if units[i]["first"] and i:
                        pe.wait_ge(sem("u_t"), i)
                    sums(i, tri).then_inc(sem("u_tri"), 1)
                if i + LEAD < NU:
                    scores(i + LEAD)
                if i >= 1:
                    values(i - 1)
                if 0 <= i < NU and not units[i]["last"]:
                    pe.wait_ge(sem("u_t"), i + 1)
                    sums(i, comp).then_inc(sem("u_rest"), 1)

        def prep_sp(sp):
            for j, (src, n) in enumerate((("ssm_lam_re", 1), ("ssm_lam_im", 2), ("state_ssm_re", 3), ("state_ssm_im", 4))):
                v = A[src].rearrange("o g p -> (o g p)" if src[0:3] == "ssm" else "o b g p -> (o b g p)")
                sp.dma_start(lt[0:GP, n, :], v.rearrange("(j q) -> j q", q=P)).then_inc(sem("par_loaded"), 16)
            sp.dma_start(lstep[0:GP, :], A["ssm_log_step"].rearrange("o (j a) -> (o j) a", a=2)).then_inc(sem("step_loaded"), 16)
            for r, src in enumerate(("ssm_c_re", "ssm_c_im")):
                sp.dma_start(craw[:, r, :, :], A[src].rearrange("o g c p -> (o g c) p").rearrange("(t q) p -> q t p", q=P)
                             ).then_inc(sem("c_loaded"), 16)
            for r, src in enumerate(("ssm_b_re", "ssm_b_im")):
                sp.dma_start(bb[:, r, :, :], A[src].rearrange("o (j a) p c -> (o a p) j c", a=2)).then_inc(sem("b_loaded"), 16)

        def prep_pe(pe):
            pe.wait_ge(sem("par_loaded"), 16 * 4)
            pe.wait_ge(sem("step_spread"), 1)
            for n in range(5):
                mm = pe.transpose(ps[:, 4, 64 + n * GP:64 + (n + 1) * GP], lt[0:GP, n, :], ident[0:GP, 0:GP])
            mm.then_inc(sem("par_mm"), 1)
            pe.wait_ge(sem("c_loaded"), 32)
            for q in range(4):
                if q == 3:
                    pe.wait_ge(sem("ct_made"), 2)
                for t in range(4):
                    mm = pe.transpose(ps[0:64, 5 + q % 3, t * P:(t + 1) * P], craw[:, q // 2, 4 * (q % 2) + t, :], ident[:])
                mm.then_inc(sem("c_mm"), 1)

        def prep_dve_in(dve):
            dve.wait_ge(sem("step_loaded"), 16)
            dve.tensor_copy(lt[0:GP, 0, :].rearrange("j (a p) -> j a p", a=2), lstep[0:GP, :].unsqueeze(2).to_broadcast([GP, 2, 64])
                            ).then_inc(sem("step_spread"), 1)
            dve.wait_ge(sem("par_mm"), 1)
            dve.tensor_copy(par[:], ps[:, 4, 64:64 + 5 * GP].rearrange("p (n j) -> p n j", n=5)).then_inc(sem("par_made"), 1)
            for q in range(4):
                dve.wait_ge(sem("c_mm"), q + 1)
                v = ps[0:64, 5 + q % 3, :].rearrange("p (j a c) -> p j a c", a=2, c=16)
                for a in range(2):
                    dve.tensor_copy(ct[64 * a:64 * a + 64, q // 2, 16 * (q % 2):16 * (q % 2) + 16, :], v[:, :, a, :]
                                    ).then_inc(sem("ct_made"), 1)

        def prep_act_scalars(act):
            act.wait_ge(sem("par_made"), 1)
            act.activation(S_step, par[:, 0, :], ACT.Exp).then_inc(sem("pa"), 1)
            act.wait_ge(sem("pd_exp"), 1)
            act.activation(S_mag, S_lrs, ACT.Exp).then_inc(sem("pa"), 1)
            act.activation(S_r8, S_lrs, ACT.Exp, scale=float(L)).then_inc(sem("pa"), 1)
            act.wait_ge(sem("pd_ang"), 1)
            act.activation(S_sin, S_r, ACT.Sin).then_inc(sem("pa"), 1)
            act.activation(S_cos, S_rc, ACT.Sin).then_inc(sem("pa"), 1)

        def prep_dve_scalars(dve):
            def own(ins):
                ins.then_inc(sem("pd"), 1)
                chain[0] += 1
                dve.wait_ge(sem("pd"), chain[0])

            def tt(out, a, b, op):
                own(dve.tensor_tensor(out, a, b, op))

            def cmul(outr, outi, ar, ai, br, bi, t1, t2):
                tt(t1, ar, br, ALU.mult)
                tt(t2, ai, bi, ALU.mult)
                tt(outr, t1, t2, ALU.subtract)
                tt(t1, ar, bi, ALU.mult)
                tt(t2, ai, br, ALU.mult)
                tt(outi, t1, t2, ALU.add)

            dve.wait_ge(sem("x_out"), 16)
            dve.wait_ge(sem("par_made"), 1)
            dve.wait_ge(sem("pa"), 1)
            tt(S_lrs, par[:, 1, :], S_step, ALU.mult)
            dve.tensor_tensor(S_ang, par[:, 2, :], S_step, ALU.mult).then_inc(sem("pd_exp"), 1)
            dve.wait_ge(sem("pd_exp"), 1)
            own(dve.tensor_scalar(S_k, S_ang, 1.0 / TWO_PI, MAGIC, ALU.mult, ALU.add))
            own(dve.tensor_scalar(S_k, S_k, MAGIC, None, ALU.subtract))
            own(dve.scalar_tensor_tensor(S_r, S_k, -TURN[0], S_ang, ALU.mult, ALU.add))
            own(dve.scalar_tensor_tensor(S_r, S_k, -TURN[1], S_r, ALU.mult, ALU.add))
            own(dve.scalar_tensor_tensor(S_r, S_k, -TURN[2], S_r, ALU.mult, ALU.add))
            own(dve.tensor_scalar(S_r, S_r, 3.1415925, -3.1415925, ALU.min, ALU.max))
            own(dve.scalar_tensor_tensor(S_rc, S_r, -1.0, S_r, ALU.mult, ALU.max))
            dve.tensor_scalar(S_rc, S_rc, -1.0, TWO_PI / 4, ALU.mult, ALU.add).then_inc(sem("pd_ang"), 1)
            dve.wait_ge(sem("pa"), 5)
            own(dve.memset(pc[:, 0, :, 0], 1.0))
            own(dve.memset(pc[:, 1, :, 0], 0.0))
            tt(pc[:, 0, :, 1], S_mag, S_cos, ALU.mult)
            tt(pc[:, 1, :, 1], S_mag, S_sin, ALU.mult)
            for k in (1, 2, 4):
                b = [pc[:, r, :, k:k + 1].to_broadcast([P, GP, k]) for r in range(2)]
                cmul(pc[:, 0, :, k + 1:2 * k + 1], pc[:, 1, :, k + 1:2 * k + 1], pc[:, 0, :, 1:k + 1], pc[:, 1, :, 1:k + 1],
                     b[0], b[1], t1[:, 0:GP * k].rearrange("p (j k) -> p j k", k=k), t2[:, 0:GP * k].rearrange("p (j k) -> p j k", k=k))
            for s in range(L):
                own(dve.tensor_copy(pb[:, :, :, s], pc[:, :, :, L - 1 - s]))
            lr, li = par[:, 1, :], par[:, 2, :]
            tt(S_a, lr, lr, ALU.mult)
            tt(S_b, li, li, ALU.mult)
            tt(S_a, S_a, S_b, ALU.add)
            own(dve.reciprocal(S_a, S_a))
            own(dve.tensor_scalar(S_nr, pc[:, 0, :, 1], 1.0, None, ALU.subtract))
            tt(S_b, S_nr, lr, ALU.mult)
            tt(S_c, pc[:, 1, :, 1], li, ALU.mult)
            tt(S_b, S_b, S_c, ALU.add)
            tt(S_cor, S_b, S_a, ALU.mult)
            tt(S_b, pc[:, 1, :, 1], lr, ALU.mult)
            tt(S_c, S_nr, li, ALU.mult)
            tt(S_b, S_b, S_c, ALU.subtract)
            tt(S_coi, S_b, S_a, ALU.mult)
            dve.wait_ge(sem("b_loaded"), 32)
            w = GP * 16
            co = [v.unsqueeze(2).to_broadcast([P, GP, 16]) for v in (S_cor, S_coi)]
            v1, v2, v3 = (t[:, o:o + w].rearrange("p (j c) -> p j c", c=16) for t, o in ((t1, 0), (t2, 0), (t1, w)))
            tt(v1, bb[:, 0], co[0], ALU.mult)
            tt(v2, bb[:, 1], co[1], ALU.mult)
            tt(v1, v1, v2, ALU.subtract)
            tt(v2, bb[:, 0], co[1], ALU.mult)
            tt(v3, bb[:, 1], co[0], ALU.mult)
            tt(bb[:, 1], v2, v3, ALU.add)
            own(dve.tensor_copy(bb[:, 0], v1))
            own(dve.tensor_copy(pp[:, 0:2, :], par[:, 3:5, :]))
            cmul(pp[:, 2, :], pp[:, 3, :], pc[:, 0, :, 8], pc[:, 1, :, 8], pp[:, 0, :], pp[:, 1, :], S_a, S_b)
            src = (S_cos, S_sin)
            for m in range(10):
                dst = (S_e[m % 2], S_f[m % 2]) if m < 3 else (ek[:, 0, :, m - 3], ek[:, 1, :, m - 3])
                if m:
                    cmul(dst[0], dst[1], src[0], src[1], src[0], src[1], S_a, S_b)
                else:
                    own(dve.tensor_copy(dst[0], src[0]))
                    own(dve.tensor_copy(dst[1], src[1]))
                unit(dve, own, dst[0], dst[1], S_a, S_b)
                src = dst
            dve.tensor_copy(S_c, S_a).then_inc(sem("pp_made"), 1)
            dve.wait_ge(sem("pp_made"), 1)

        def unit(dve, own, re, im, a, b):
            own(dve.tensor_tensor(a, re, re, ALU.mult))
            own(dve.tensor_tensor(b, im, im, ALU.mult))
            own(dve.tensor_tensor(a, a, b, ALU.add))
            own(dve.tensor_scalar(a, a, -0.5, 1.5, ALU.mult, ALU.add))
            own(dve.tensor_tensor(re, re, a, ALU.mult))
            own(dve.tensor_tensor(im, im, a, ALU.mult))

        chain = [0]

        def prep_dve_block(dve, n):
            blk, kind = divmod(n, 3)
            j0 = 8 * blk

            def own(ins):
                ins.then_inc(sem("pd"), 1)
                chain[0] += 1
                dve.wait_ge(sem("pd"), chain[0])

            def tt(out, a, b, op):
                own(dve.tensor_tensor(out, a, b, op))

            if n >= 3:
                dve.wait_ge(sem(f"prep_out{kind}"), 16 * blk)
            if kind == 0:
                own(dve.memset(eb[:, 0, :, 0:1], 1.0))
                own(dve.memset(eb[:, 1, :, 0:1], 0.0))
                for m in range(7):
                    k = 1 << m
                    er_, ei_ = eb[:, 0, :, 0:k], eb[:, 1, :, 0:k]
                    br_, bi_ = (ek[:, r, j0:j0 + 8, m:m + 1].to_broadcast([P, 8, k]) for r in range(2))
                    v1, v2 = (t[:, 0:8 * k].rearrange("p (j k) -> p j k", k=k) for t in (t1, t2))
                    tt(v1, er_, br_, ALU.mult)
                    tt(v2, ei_, bi_, ALU.mult)
                    tt(eb[:, 0, :, k:2 * k], v1, v2, ALU.subtract)
                    tt(v1, er_, bi_, ALU.mult)
                    tt(v2, ei_, br_, ALU.mult)
                    tt(eb[:, 1, :, k:2 * k], v1, v2, ALU.add)
                v1, v2 = (t[:, 0:8 * P].rearrange("p (j k) -> p j k", k=P) for t in (t1, t2))
                unit(dve, own, eb[:, 0, :, 0:P], eb[:, 1, :, 0:P], v1, v2)
                for r in range(2):
                    own(dve.tensor_copy(eb[:, r, :, P:NCH], eb[:, r, :, 0:NCH - P]))
                own(dve.tensor_copy(eb[:, 2, :, :], S_r8[:, j0:j0 + 8].unsqueeze(2).to_broadcast([P, 8, NCH])))
                own(dve.memset(eb[:, 2, :, 0:1], 0.0))
                dve.memset(eb[:, 2, :, P:P + 1], 0.0).then_inc(sem("prep_made"), 1)
            elif kind == 1:
                sh = [P, 8, L, 16]
                p_ = [pb[:, r, j0:j0 + 8, :].unsqueeze(3).to_broadcast(sh) for r in range(2)]
                b_ = [bb[:, r, j0:j0 + 8, :].unsqueeze(2).to_broadcast(sh) for r in range(2)]
                o_ = [bo[:, :, r, :].rearrange("p j (s c) -> p j s c", c=16) for r in range(2)]
                v1, v2 = (t[:, 0:8 * P].rearrange("p (j s c) -> p j s c", s=L, c=16) for t in (t1, t2))
                tt(v1, p_[0], b_[0], ALU.mult)
                tt(v2, p_[1], b_[1], ALU.mult)
                tt(o_[0], v1, v2, ALU.subtract)
                tt(v1, p_[0], b_[1], ALU.mult)
                tt(v2, p_[1], b_[0], ALU.mult)
                dve.tensor_tensor(o_[1], v1, v2, ALU.add).then_inc(sem("prep_made"), 1)
            else:
                sh = [P, 8, L + 1, 16]
                p_ = [pc[:, r, j0:j0 + 8, :].unsqueeze(3).to_broadcast(sh) for r in range(2)]
                c_ = [ct[:, r, j0:j0 + 8, :].unsqueeze(2).to_broadcast(sh) for r in range(2)]
                o_ = [co_[:, :, r, :].rearrange("p j (s c) -> p j s c", c=16) for r in range(2)]
                v1, v2 = (t[:, 0:8 * CW].rearrange("p (j s c) -> p j s c", s=L + 1, c=16) for t in (t1, t2))
                tt(v1, p_[0], c_[0], ALU.mult)
                tt(v2, p_[1], c_[1], ALU.mult)
                tt(o_[0], v1, v2, ALU.subtract)
                tt(v1, p_[0], c_[1], ALU.mult)
                tt(v2, p_[1], c_[0], ALU.mult)
                tt(v1, v1, v2, ALU.add)
                dve.tensor_scalar(o_[1], v1, -1.0, None, ALU.mult).then_inc(sem("prep_made"), 1)
            dve.wait_ge(sem("prep_made"), n + 1)

        def prep_pool_block(pool, n):
            blk, kind = divmod(n, 3)
            j0 = 8 * blk
            pool.wait_ge(sem("prep_made"), n + 1)
            if kind == 0:
                pool.dma_start(dE[:, :, j0:j0 + 8, :], eb[:]).then_inc(sem(f"prep_out{kind}"), 16)
            elif kind == 1:
                pool.dma_start(dB[:, j0:j0 + 8, :, :], bo[:]).then_inc(sem(f"prep_out{kind}"), 16)
            else:
                pool.dma_start(dC[:, j0:j0 + 8, :, :], co_[:]).then_inc(sem(f"prep_out{kind}"), 16)

        NF = KD

        def s5_sp(sp):
            sp.wait_ge(sem("acc_used"), ACC_FF1)
            sp.dma_start(xs, x[:]).then_inc(sem("x_out"), 16)
            sp.wait_ge(sem("p_out"), 16)
            sp.dma_start(p4[:], dP).then_inc(sem("p4_loaded"), 16)

            def store_h(f):
                sp.wait_ge(sem("n_f"), n_units(2, 2 * KD + f + 1))
                sp.dma_start(dU[f * P:(f + 1) * P, :], hp[:, f * T:(f + 1) * T]).then_inc(sem(f"u_out{f % 2}"), 16)

            def load(f):
                if f >= 1:
                    sp.wait_ge(sem("e_BT"), 2 * f)
                    sp.wait_ge(sem("s_K"), f)
                if f >= 2:
                    sp.wait_ge(sem("s_Y"), f - 1)
                js = slice(4 * f, 4 * f + 4)
                sp.dma_start(br[:], dB[:, js, :, :]).then_inc(sem("br_loaded"), 16)
                sp.dma_start(ca[:, f % 2], dC[:, js, :, :]).then_inc(sem(f"ca_loaded{f % 2}"), 16)
                sp.wait_ge(sem(f"u_out{f % 2}"), 16 * (f // 2 + 1))
                if f + 2 < NF:
                    store_h(f + 2)
                for s in range(L):
                    sp.dma_start(u[16 * s:16 * s + 16, f % 2, :, :],
                                 dU[f * P:(f + 1) * P, s * NCH:(s + 1) * NCH].rearrange("(g c) n -> c g n", c=16)
                                 ).then_inc(sem(f"u_loaded{f % 2}"), 16)
                if f >= 1:
                    sp.wait_ge(sem("s_rot"), f)
                else:
                    sp.wait_ge(sem("x_out"), 32)
                sp.dma_start(e3[:], dE[:, :, js, :]).then_inc(sem("e3_loaded"), 16)

            store_h(0)
            store_h(1)
            load(0)
            for f in range(NF + 1):
                if f < NF:
                    sp.wait_ge(sem("e_K"), 2 * f + 2)
                    if f >= 2:
                        sp.wait_ge(sem("s_Y"), f - 1)
                    sp.wait_ge(sem("t_zero"), 1)
                    for s in range(L):
                        sp.dma_start(tm[16 * s:16 * s + 16, f % 2, :, 16 * s:P], kt[0:16, :, 0:P - 16 * s]).then_inc(sem(f"t_made{f % 2}"), 16)
                if f + 1 < NF:
                    load(f + 1)
                if f:
                    g = f - 1
                    sp.wait_ge(sem("e_Y"), 4 * g + 4)
                    if g >= 2:
                        sp.wait_ge(sem(f"z_loaded{g % 2}"), 16 * (g // 2))
                    for t in range(L):
                        sp.dma_start(dY[g * P:(g + 1) * P, t * NCH:(t + 1) * NCH].rearrange("(g c) n -> c g n", c=16),
                                     yy[16 * t:16 * t + 16, g % 2, :, :]).then_inc(sem(f"y_stored{g % 2}"), 16)
            sp.wait_ge(sem("y_f"), NF)
            sp.dma_start(x[:], xs).then_inc(sem("x_back"), 16)
            sp.wait_ge(sem("fin_t"), 1)
            for q, o in enumerate(("re_p", "im_p", "re_s", "im_s")):
                sp.dma_start(O[o].rearrange("o b g p -> (o b g p)").rearrange("(j q) -> j q", q=P), fout[0:GP, q, :]).then_inc(sem("fin_out"), 16)

        def s5_pe(pe):
            def first(f):
                if f >= 2:
                    pe.wait_ge(sem("e_Y"), 4 * (f - 1))
                elif f == 0:
                    pe.wait_ge(sem("n_f"), n_units(2))
                pe.wait_ge(sem("br_loaded"), 16 * (f + 1))
                for q in range(8):
                    mm = pe.transpose(ps[:, q // 4, (q % 4) * P:(q % 4 + 1) * P], br[:, q // 2, q % 2, :], ident[:])
                mm.then_inc(sem("s_B"), 1)
                pe.wait_ge(sem(f"ca_loaded{f % 2}"), 16 * (f // 2 + 1))
                for g in range(8):
                    j, a = divmod(g, 2)
                    r = slice(64 * a, 64 * a + 64)
                    for q in range(2):
                        mm = pe.matmul(ps[0:16, 2 + a, j * P:(j + 1) * P], br[r, j, q, P - 16:P], ca[r, f % 2, j, q, 0:P],
                                       start=q == 0, stop=q == 1)
                mm.then_inc(sem("s_K"), 1)
                pe.wait_ge(sem(f"u_loaded{f % 2}"), 16 * L * (f // 2 + 1))
                pe.wait_ge(sem("e_BT"), 2 * f + 2)
                if f:
                    pe.wait_ge(sem("e_X"), 3 * f)
                for q in range(2):
                    for j in range(4):
                        n = 4 * q + j
                        for a in range(2):
                            mm = pe.matmul(ps[64 * a:64 * a + 64, 4 + n // 3, (n % 3) * NCH:(n % 3 + 1) * NCH],
                                           bt[:, j, q, 64 * a:64 * a + 64], u[:, f % 2, 2 * j + a, :], start=True, stop=True,
                                           skip_group_check=True)
                mm.then_inc(sem("s_X"), 1)

            def second(f):
                pe.wait_ge(sem(f"t_made{f % 2}"), 16 * L * (f // 2 + 1))
                pe.wait_ge(sem("s_sh"), 2 * f + 2)
                if f:
                    pe.wait_ge(sem("e_Y"), 4 * f)
                nxt = min(f + 1, NF - 1)
                pe.wait_ge(sem("e_BT"), 2 * nxt + 2)
                pe.wait_ge(sem("e_K"), 2 * nxt + 2)
                for g in range(8):
                    j, a = divmod(g, 2)
                    r = slice(64 * a, 64 * a + 64)
                    out = ps[:, 2 * a + j // 2, (j % 2) * NCH:(j % 2 + 1) * NCH]
                    pe.matmul(out, tm[:, f % 2, g, :], u[:, f % 2, g, :], start=True, stop=False)
                    for q in range(2):
                        mm = pe.matmul(out, ca[r, f % 2, j, q, 16:CW], sh[r, f % 2, q, j, :], start=False, stop=q == 1)
                mm.then_inc(sem("s_Y"), 1)
            for f in range(NF + 1):
                if f < NF:
                    first(f)
                if f:
                    second(f - 1)
            pe.wait_ge(sem("fin_made"), 4 * NF)
            for q in range(4):
                mm = pe.transpose(ps[0:GP, 4, q * P:(q + 1) * P], fin[:, q, :], ident[:])
            mm.then_inc(sem("fin_mm"), 1)

        def s5_act(act):
            def first(f):
                act.wait_ge(sem("s_B"), f + 1)
                if f:
                    act.wait_ge(sem("s_X"), f)
                for b in range(2):
                    act.activation(bt[:, 2 * b:2 * b + 2, :, :], ps[:, b, :].rearrange("p (j q n) -> p j q n", j=2, q=2), ACT.Copy
                                   ).then_inc(sem("e_BT"), 1)
                act.wait_ge(sem("s_X"), f + 1)
                if f:
                    act.wait_ge(sem("s_rot"), f)
                for b in range(3):
                    n = 3 if b < 2 else 2
                    act.activation(xx[:, 3 * b * NCH:(3 * b + n) * NCH], ps[:, 4 + b, 0:n * NCH], ACT.Copy).then_inc(sem("e_X"), 1)

            def second(f):
                act.wait_ge(sem("s_Y"), f + 1)
                if f >= 2:
                    act.wait_ge(sem(f"y_stored{f % 2}"), 16 * L * (f // 2))
                for b in range(4):
                    act.activation(yy[:, f % 2].rearrange("p (h l a) n -> p a h l n", l=2, a=2)[:, b // 2, b % 2],
                                   ps[:, b, 0:2 * NCH].rearrange("p (l n) -> p l n", l=2), ACT.Copy).then_inc(sem("e_Y"), 1)

            def third(f):
                act.wait_ge(sem("y_f"), f + 1)
                yt = yp[:, f * T:(f + 1) * T]
                act.activation(yt, yt, GELU).then_inc(sem("y_g"), 1)

            for f in range(NF + 2):
                if f < NF:
                    first(f)
                if 1 <= f <= NF:
                    second(f - 1)
                if f >= 2:
                    third(f - 2)

        def s5_pool(pool):
            for f in range(NF):
                pool.wait_ge(sem(f"y_stored{f % 2}"), 16 * L * (f // 2 + 1))
                if f >= 2:
                    pool.wait_ge(sem("y_f"), f - 1)
                pool.dma_start(zb[f % 2][:], dY[f * P:(f + 1) * P, :]).then_inc(sem(f"z_loaded{f % 2}"), 16)

        def s5_dve(dve):
            def own(ins):
                ins.then_inc(sem("sd"), 1)
                chain[1] += 1
                dve.wait_ge(sem("sd"), chain[1])

            def tt(out, a, b, op):
                own(dve.tensor_tensor(out, a, b, op))

            chain.append(0)
            W4 = 4 * NCH
            xr, xi = xx[:, 0:W4], xx[:, W4:2 * W4]
            er_, ei_, r8_ = (e3[:, q].rearrange("p j n -> p (j n)") for q in range(3))

            def first(f):
                dve.wait_ge(sem("s_K"), f + 1)
                if f:
                    dve.wait_ge(sem(f"t_made{(f - 1) % 2}"), 16 * L * ((f - 1) // 2 + 1))
                for b in range(2):
                    dve.tensor_copy(kt[0:16].rearrange("p (j a) n -> p a j n", a=2)[:, b], ps[0:16, 2 + b, :].rearrange("p (j n) -> p j n", j=4)).then_inc(sem("e_K"), 1)

            def scan(f):
                dve.wait_ge(sem("e_X"), 3 * f + 3)
                dve.wait_ge(sem("e3_loaded"), 16 * (f + 1))
                for q in range(2):
                    v = xx[:, q * W4:(q + 1) * W4].rearrange("p (j n) -> p j n", j=4)[:, :, P:P + 1]
                    own(dve.tensor_tensor(v, v, p4[:, 2 + q, 4 * f:4 * f + 4].unsqueeze(2), ALU.add))
                tt(v1, xr, er_, ALU.mult)
                tt(v2, xi, ei_, ALU.mult)
                tt(v1, v1, v2, ALU.add)
                tt(v2, xi, er_, ALU.mult)
                tt(v3, xr, ei_, ALU.mult)
                tt(v2, v2, v3, ALU.subtract)
                own(dve.tensor_tensor_scan(w1, r8_, v1, 0.0, ALU.mult, ALU.add))
                own(dve.tensor_tensor_scan(w2, r8_, v2, 0.0, ALU.mult, ALU.add))
                tt(v1, w1, er_, ALU.mult)
                tt(v2, w2, ei_, ALU.mult)
                tt(v1, v1, v2, ALU.subtract)
                tt(v2, w1, ei_, ALU.mult)
                tt(v3, w2, er_, ALU.mult)
                dve.tensor_tensor(v2, v2, v3, ALU.add).then_inc(sem("s_rot"), 1)
                dve.wait_ge(sem("s_rot"), f + 1)
                if f >= 2:
                    dve.wait_ge(sem("s_Y"), f - 1)
                for q, v in enumerate((v1, v2)):
                    v = v.rearrange("p (j n) -> p j n", j=4)
                    o = sh[:, f % 2, q, :, :]
                    for r, n in ((0, P - 1), (2, NCH - 1)):
                        dve.tensor_copy(fin[:, q + r, 4 * f:4 * f + 4], v[:, :, n]).then_inc(sem("fin_made"), 1)
                    own(dve.tensor_copy(o[:, :, 1:NCH], v[:, :, 0:NCH - 1]))
                    own(dve.memset(o[:, :, 0:1], 0.0))
                    dve.tensor_copy(o[:, :, P:P + 1], p4[:, q, 4 * f:4 * f + 4].unsqueeze(2)).then_inc(sem("s_sh"), 1)
                dve.wait_ge(sem("s_sh"), 2 * f + 2)

            def second(f):
                dve.wait_ge(sem(f"z_loaded{f % 2}"), 16 * (f // 2 + 1))
                dve.scalar_tensor_tensor(yp[:, f * T:(f + 1) * T].rearrange("p (n s) -> p s n", s=L),
                                         hp[:, f * T:(f + 1) * T].rearrange("p (s n) -> p s n", s=L), cols[:, 40 + f:41 + f],
                                         zb[f % 2][:].rearrange("p (s n) -> p s n", s=L), ALU.mult, ALU.add).then_inc(sem("y_f"), 1)

            dve.wait_ge(sem("p4_loaded"), 16)
            for f in range(NF + 2):
                if f < NF:
                    first(f)
                    scan(f)
                if f >= 2:
                    second(f - 2)
            dve.wait_ge(sem("fin_mm"), 1)
            dve.tensor_copy(fout[0:GP].rearrange("p q n -> p (q n)"), ps[0:GP, 4, :]).then_inc(sem("fin_t"), 1)

        def y_split_act(act):
            for c, (s, n) in enumerate(CHUNKS):
                for f in range(KD):
                    o = f * T + s
                    act.wait_ge(sem("y_g"), NF)
                    act.activation(hhi[:, o:o + n], yp[:, o:o + n], ACT.Copy).then_inc(sem("ys_hi"), 1)

        def y_split_pool(pool):
            for c, (s, n) in enumerate(CHUNKS):
                for f in range(KD):
                    o = f * T + s
                    pool.wait_ge(sem("ys_hi"), c * KD + f + 1)
                    pool.tensor_tensor(hlo[:, o:o + n], yp[:, o:o + n], hhi[:, o:o + n].bitcast(F32), ALU.subtract).then_inc(sem("ys_lo"), 1)

        def glu_slab(t):
            m, half = divmod(t - SLAB_GLU, 2)
            return w_glu[:, :, half * D + m * P:half * D + (m + 1) * P]

        def glu_pe(pe):
            for q in range(KD):
                pe_pair(pe, SLAB_GLU + 2 * q, PAIR_GLU + NC * q, ready=(lambda c: pe.wait_ge(sem("ys_lo"), KD * (c + 1))) if q == 0 else None)

        def glu_act(act):
            for q in range(KD):
                for j in range(2):
                    if q < 2:
                        slab_hi(act, SLAB_GLU + 2 * q + 2 + j)
                    else:
                        slab_hi(act, SLAB_GLU + 2 * q + 2 + j, "pair_ready", PAIR_GLU + NC * (q - 1))
                for c, (s, n) in enumerate(CHUNKS):
                    v = PAIR_GLU + NC * q + c
                    act.wait_ge(sem("pair_ready"), v + 1)
                    act.wait_ge(sem("pair_used"), v - 1)
                    act.activation(abuf[:, v % 2, 0:n], ps[:, 2 * (v % 2) + 1, 0:n], ACT.Sigmoid).then_inc(sem("pair_act"), 1)

        def glu_dve(dve):
            dve.wait_ge(sem("x_back"), 32)
            for q in range(KD):
                for c, (s, n) in enumerate(CHUNKS):
                    r = NC * q + c
                    v = PAIR_GLU + r
                    dve.wait_ge(sem("pair_act"), v + 1)
                    if r >= 2:
                        dve.wait_ge(sem("glu_res"), r - 1)
                    dve.tensor_tensor(fbuf[:, v % 2, 0:n], ps[:, 2 * (v % 2), 0:n], abuf[:, v % 2, 0:n], ALU.mult).then_inc(sem("pair_used"), 1)
                    dve.wait_ge(sem("pair_used"), v + 1)
                    xo = x[:, q * T + s:q * T + s + n]
                    dve.tensor_tensor(xo, xo, fbuf[:, v % 2, 0:n], ALU.add).then_inc(sem("glu_res"), 1)

        def out_pe(pe):
            for tt, (s, n) in enumerate(TILES):
                pe.wait_ge(sem("n_f"), n_units(4, KD * (tt // 3 + 1)))
                for b in range(2):
                    if tt >= 2:
                        pe.wait_ge(sem(("yo_v", "yo_a")[b]), tt - 1)
                    for f in range(4):
                        o = (4 * b + f) * T + s
                        mm = pe.transpose(ps[0:n, 4 + (2 * tt + b) % 4, f * P:(f + 1) * P], yf[:, o:o + n], ident[:])
                    mm.then_inc(sem("yo_mm"), 1)

        def out_take(eng, b, copy):
            for tt, (s, n) in enumerate(TILES):
                eng.wait_ge(sem("yo_mm"), 2 * tt + b + 1)
                if tt >= 2:
                    eng.wait_ge(sem(f"y_out{tt % 2}"), 16 * (tt // 2))
                copy(yo[0:n, tt % 2, 512 * b:512 * b + 512], ps[0:n, 4 + (2 * tt + b) % 4, :]).then_inc(sem(("yo_v", "yo_a")[b]), 1)

        def out_sp(sp):
            for tt, (s, n) in enumerate(TILES):
                sp.wait_ge(sem("yo_v"), tt + 1)
                sp.wait_ge(sem("yo_a"), tt + 1)
                sp.dma_start(y_new[0][s:s + n, :] if tt < 8 else y_new[1], yo[0:n, tt % 2, :]).then_inc(sem(f"y_out{tt % 2}"), 16)


        POOL0 = 2
        block = ctx.enter_context(nc.Block())

        @block.sync
        def _(sp):
            for tt, (s, n) in enumerate(TILES):
                if tt >= 2:
                    sp.wait_ge(sem("xt_mm"), 2 * (tt - 1))
                src = xp[s:s + n, :] if tt < 8 else xd
                sp.dma_start(xin[0:n, tt % 2, :], src).then_inc(sem(f"x_loaded{tt % 2}"), 16)
                if tt == 0:
                    for j, w in enumerate((A["norm_mix"][0], A["norm_mix"][1], A["norm_ffn"][0], A["norm_ffn"][1],
                                           A["norm_final"], A["ssm_d"][0])):
                        sp.dma_start(nrow[8 * j:8 * j + 8, :], w.rearrange("(f p) -> f p", p=P)).then_inc(sem("n_loaded"), 16)
                if tt in (2, 3):
                    load_slab(sp, tt - 2, w_in[:, :, (tt - 2) * P:(tt - 1) * P])
            prep_sp(sp)
            for t in range(2, 4):
                load_slab(sp, t, w_in[:, :, t * P:(t + 1) * P])
            sp.wait_ge(sem("n_f"), n_units(0))
            sp.dma_start(xs, x[:]).then_inc(sem("x_out"), 16)
            with sp.Fori(0, 4) as i:
                for t in range(4, 8):
                    load_slab(sp, t, w_in[:, :, bass.ds(i * (4 * P) + t * P, P)], i, 4)
            tr_sp(sp)
            at_sp(sp)
            for t in range(8):
                load_slab(sp, SLAB_OUT + t, w_out[:, :, t * P:(t + 1) * P])
            ffn_sp(sp, F[0])
            ffn_sp(sp, F[0], 1)
            for t in range(2):
                load_slab(sp, SLAB_GLU + t, glu_slab(SLAB_GLU + t))
            s5_sp(sp)
            for t in range(2, 2 * KD):
                load_slab(sp, SLAB_GLU + t, glu_slab(SLAB_GLU + t))
            ffn_sp(sp, F[1])
            ffn_sp(sp, F[1], 1)
            out_sp(sp)
            sp.wait_ge(sem("y_out0"), 16 * 5)
            sp.wait_ge(sem("y_out1"), 16 * 4)
            sp.wait_ge(sem("fin_out"), 16 * 4)

        @block.gpsimd
        def _(pool):
            pool.memset(ident[:], 0.0).then_inc(sem("pool"), 1)
            pool.memset(cols[:, 48:49], EPS).then_inc(sem("pool"), 1)
            pool.wait_ge(sem("pool"), 2)
            pool.memset(ones[:], 1.0).then_inc(sem("consts"), 1)
            pool.affine_select(out=ident[:], in_=ident[:], compare_op=ALU.not_equal, fill=1.0, base=0, pattern=[[-1, P]],
                               channel_multiplier=1).then_inc(sem("ident_made"), 1)
            for t in range(2):
                slab_lo(pool, t)
            norm_pool(pool, 0)

            def store(t, i=None, b=0):
                pool.wait_ge(sem("acc_used"), step(NC * (t + 1), i, NC * b))
                r = step(t * P, i, b * P)
                pool.dma_start(zT[bass.ds(r, P), :] if i is not None else zT[r:r + P, :], zst[:, t % 2, :]
                               ).then_inc(sem(f"z_stored{t % 2}"), 16)

            for t in range(IN_TILES):
                if t + 2 < IN_TILES:
                    slab_lo(pool, t + 2)
                store(t)
                if t == 1:
                    pool.wait_ge(sem("pp_made"), 1)
                    pool.dma_start(dP, pp[:]).then_inc(sem("p_out"), 16)
                if 2 <= t < 14:
                    prep_pool_block(pool, t - 2)
            tr_pool(pool)
            at_pool_make(pool)
            at_pool(pool)
            for t in range(-2, 8):
                slab_lo(pool, SLAB_OUT + t + 2)
            norm_pool(pool, 1)
            ffn_pool(pool, F[0])
            pool.wait_ge(sem("n_f"), n_units(2))
            pool.memset(tm[:], 0.0).then_inc(sem("t_zero"), 1)
            s5_pool(pool)
            y_split_pool(pool)
            for q in range(KD):
                for j in range(2):
                    slab_lo(pool, SLAB_GLU + 2 * q + 2 + j)
            norm_pool(pool, 3)
            ffn_pool(pool, F[1])

        @block.scalar
        def _(act):
            for tt, (s, n) in enumerate(TILES):
                act.wait_ge(sem("xt_mm"), 2 * tt + 2)
                act.activation(x3[:, 4:8, s:s + n], ps[:, (2 * tt + 1) % 4, :].rearrange("p (f n) -> p f n", f=4)[:, :, 0:n], ACT.Copy
                               ).then_inc(sem("xt_a"), 1)
                if tt in (4, 5):
                    slab_hi(act, tt - 4)

            def x_in(eng, c):
                last = (3, 6, 9)[c]
                eng.wait_ge(sem("xt_a"), last)
                eng.wait_ge(sem("xt_v"), last)

            act.wait_ge(sem("consts"), 1)
            norm_act(act, 0, x_in, True)
            for t in range(IN_TILES):
                if t + 2 < IN_TILES:
                    slab_hi(act, t + 2, "acc_ready" if t >= 2 else None, NC * (t - 1))
                if t == 1:
                    prep_act_scalars(act)
            tr_act(act)
            at_act(act)
            act.wait_ge(sem("o_lo"), GROUPS)
            for t in range(-2, 8):
                slab_hi(act, SLAB_OUT + t + 2, "acc_ready" if t >= 2 else None, ACC_OUT + NC * (t - 1))
            norm_act(act, 1, lambda e, c: e.wait_ge(sem("acc_used"), ACC_FF0 - NC + c + 1), True)
            ffn_act(act, F[0], "acc_ready", ACC_FF0)
            norm_act(act, 2, lambda e, c: e.wait_ge(sem("acc_used"), ACC_FF1 - KD * (2 - c)), False)
            s5_act(act)
            y_split_act(act)
            glu_act(act)
            act.wait_ge(sem("fin_out"), 16 * 4)
            norm_act(act, 3, lambda e, c: e.wait_ge(sem("glu_res"), NC * KD), True)
            ffn_act(act, F[1], "pair_ready", PAIR_FF1)
            norm_act(act, 4, lambda e, c: e.wait_ge(sem("acc_used"), ACC_FF1 + PARTS * KD * NC - KD * (2 - c)), False)
            out_take(act, 1, lambda o, i: act.activation(o, i, ACT.Copy))

        @block.vector
        def _(dve):
            dve.wait_ge(sem("cols_mm"), 1)
            dve.tensor_copy(cols[:, 0:48], ps[:, 4, 0:48]).then_inc(sem("cols_made"), 1)
            for tt, (s, n) in enumerate(TILES):
                dve.wait_ge(sem("xt_mm"), 2 * tt + 1)
                dve.tensor_copy(x3[:, 0:4, s:s + n], ps[:, (2 * tt) % 4, :].rearrange("p (f n) -> p f n", f=4)[:, :, 0:n]
                                ).then_inc(sem("xt_v"), 1)
            dve.wait_ge(sem("cols_made"), 1)
            prep_dve_in(dve)
            norm_dve(dve, 0, 0)

            def stage(t, i=None, b=0):
                if t >= 2:
                    dve.wait_ge(sem(f"z_stored{t % 2}"), step(16 * (t // 2), i, 8 * b))
                for c, (s, n) in enumerate(CHUNKS):
                    v = NC * t + c
                    dve.wait_ge(sem("acc_ready"), step(v + 1, i, NC * b))
                    dve.tensor_copy(zst[:, t % 2, s:s + n], acc(v)[:, 0:n]).then_inc(sem("acc_used"), 1)

            for t in range(IN_TILES):
                stage(t)
                if t == 1:
                    prep_dve_scalars(dve)
                if 2 <= t < 14:
                    prep_dve_block(dve, t - 2)
            tr_dve(dve)
            dve.wait_ge(sem("at_made"), 2)
            at_dve(dve)
            dve.wait_ge(sem("x_back"), 16)
            for m in range(KD):
                for c, (s, n) in enumerate(CHUNKS):
                    v = ACC_OUT + m * NC + c
                    dve.wait_ge(sem("acc_ready"), v + 1)
                    xo = x[:, m * T + s:m * T + s + n]
                    dve.tensor_tensor(xo, acc(v)[:, 0:n], xo, ALU.add).then_inc(sem("acc_used"), 1)
            norm_dve(dve, 1, 16)
            ffn_dve(dve, F[0])
            norm_dve(dve, 2, 8, plain=hp, by_chunk=True)
            s5_dve(dve)
            glu_dve(dve)
            norm_dve(dve, 3, 24)
            ffn_dve(dve, F[1])
            norm_dve(dve, 4, 32, plain=yf)
            out_take(dve, 0, dve.tensor_copy)

        @block.tensor
        def _(pe):
            pe.wait_ge(sem("ident_made"), 1)
            pe.wait_ge(sem("n_loaded"), 16 * 6)
            pe.transpose(ps[:, 4, 0:48], nrow[0:48, :], ident[0:48, 0:48]).then_inc(sem("cols_mm"), 1)
            for tt, (s, n) in enumerate(TILES):
                pe.wait_ge(sem(f"x_loaded{tt % 2}"), 16 * (tt // 2 + 1))
                for b in range(2):
                    if tt >= 2:
                        pe.wait_ge(sem(("xt_v", "xt_a")[b]), tt - 1)
                    for f in range(4):
                        mm = pe.transpose(ps[:, (2 * tt + b) % 4, f * P:f * P + n], xin[0:n, tt % 2, (4 * b + f) * P:(4 * b + f + 1) * P],
                                          ident[0:n, 0:n])
                    mm.then_inc(sem("xt_mm"), 1)
            pe.wait_ge(sem("cols_made"), 1)
            prep_pe(pe)
            pe.wait_ge(sem("par_made"), 1)
            pe.wait_ge(sem("ct_made"), 8)
            pe.wait_ge(sem("xt_v"), 9)
            pe.wait_ge(sem("xt_a"), 9)
            norm_pe(pe, 0)
            for t in range(4):
                pe_single(pe, t, ready=h_ready(0)(pe) if t == 0 else None)
            with pe.Fori(0, 4) as i:
                for t in range(4, 8):
                    pe_single(pe, t, i, 4)
            tr_pe(pe)
            at_pe(pe)
            pe.wait_ge(sem("o_lo"), GROUPS)
            pe.wait_ge(sem("mix_lo"), 4 * NC)
            for t in range(8):
                pe_single(pe, SLAB_OUT + t)
            norm_pe(pe, 1)
            ffn_pe(pe, F[0])
            norm_pe(pe, 2)
            s5_pe(pe)
            glu_pe(pe)
            pe.wait_ge(sem("glu_res"), NC * KD)
            norm_pe(pe, 3)
            ffn_pe(pe, F[1])
            norm_pe(pe, 4)
            out_pe(pe)


_INS = ["x_prompt", "x_sample", "cache_sb_k", "cache_sb_v", "state_ssm_re", "state_ssm_im", "norm_mix", "norm_ffn",
        "norm_final", "ab_w_in", "sgu_w", "sgu_b", "ab_w_out", "ssm_lam_re", "ssm_lam_im", "ssm_log_step", "ssm_b_re",
        "ssm_b_im", "ssm_c_re", "ssm_c_im", "ssm_d", "ssm_w_glu", "ffn_w_gate", "ffn_w_up", "ffn_w_down"]
_OUTS = {"y_p": (1, 1024, 1024), "y_s": (1, 64, 1024), "k_p": (1, 1, 1024, 8, 64), "v_p": (1, 1, 1024, 8, 64),
         "k_s": (1, 1, 64, 8, 64), "v_s": (1, 1, 64, 8, 64), "g_s": (1, 1, 64, 512), "re_p": (1, 1, 64, 64),
         "im_p": (1, 1, 64, 64), "re_s": (1, 1, 64, 64), "im_s": (1, 1, 64, 64)}


def kernel(**inputs):
    import numpy as np
    from concourse import bacc
    from concourse.bass_utils import run_bass_kernel_spmd

    nc = bacc.Bacc("TRN2", target_bir_lowering=False, num_devices=1)
    arrays, ins = {}, {}
    for name in _INS:
        a = np.ascontiguousarray(inputs[name])
        arrays[f"in_{name}"] = a
        ins[name] = nc.dram_tensor(f"in_{name}", a.shape, F32, kind="ExternalInput").ap()
    outs = {name: nc.dram_tensor(f"out_{name}", shape, F32, kind="ExternalOutput").ap() for name, shape in _OUTS.items()}
    build(nc, ins, outs)
    r = run_bass_kernel_spmd(nc, [arrays], core_ids=[0])
    return tuple(r.results[0][f"out_{name}"] for name in _OUTS)
```

```python
from contextlib import ExitStack

import concourse.bass as bass
from concourse import mybir
from concourse.alu_op_type import AluOpType as ALU

F32 = mybir.dt.float32
F32R = mybir.dt.float32r
ACT = mybir.ActivationFunctionType

P = 128
D = 1024
KD = D // P
SEQ, DEC = 1024, 64
T = SEQ + DEC
TILES = [(i * P, min(P, T - i * P)) for i in range((T + P - 1) // P)]
CHUNKS = [(0, 384), (384, 384), (768, 320)]
NC = len(CHUNKS)
HD = 64
HEADS = 8
SB = HEADS * HD
PAST = 512
QT, KT, VT, UT, GT = 0, 4, 8, 12, 16
IN_TILES = 20
FF = 2816
PARTS = FF // (2 * P)
EPS = 1e-6
NEG = -1.0e30
GELU = ACT.Gelu_apprx_tanh
L = 8
NCH = T // L
CW = (L + 1) * 16
GP = 32
TWO_PI = 6.283185307179586
TURN = (6.28125, 0.0019350051879882812, 3.019916050e-07)
MAGIC = 12582912.0

SLAB_OUT = IN_TILES
SLAB_FF0 = SLAB_OUT + KD
PART_SLABS = 6
SLAB_GLU = SLAB_FF0 + PARTS * PART_SLABS
SLAB_FF1 = SLAB_GLU + 2 * KD
ACC_OUT = IN_TILES * NC
ACC_FF0 = ACC_OUT + KD * NC
ACC_FF1 = ACC_FF0 + PARTS * KD * NC
PAIR_GLU = 2 * PARTS * NC
PAIR_FF1 = PAIR_GLU + KD * NC


def slot(t):
    return t % 4 if t < SLAB_FF0 else (t - SLAB_FF0 + 4) % 6


def step(c, i, b):
    return c if i is None else c + i * b


def build(nc, A, O):
    with ExitStack() as ctx:
        sems = {}

        def sem(name):
            if name not in sems:
                sems[name] = ctx.enter_context(nc.semaphore(name))
            return sems[name]

        SIZE = 53200 * 4
        ctx.enter_context(nc.sbuf_tensor("arena", [P, SIZE // 4], F32))
        base = nc.sbuf_base - SIZE

        def plan(off, *specs):
            got = []
            for name, shape, dt in specs:
                n = 4
                for s in shape[1:]:
                    n *= s
                assert off + n <= SIZE, (name, off + n)
                got.append(nc.alloc_sbuf_tensor_at(name, shape, dt, offset=base + off))
                off += n
            return got + [off]

        ident, ones, cols, off = plan(0, ("ident", [P, P], F32), ("ones", [P, P], F32), ("cols", [P, 64], F32))
        off_a = off
        abuf, fbuf, rms, off = plan(off, ("abuf", [P, 2, 384], F32), ("fbuf", [P, 2, 384], F32), ("rms", [P, 2, 384], F32))
        raw, off_w = plan(off, ("raw", [P, 2, D], F32))
        whi, wlo, off_h = plan(off_w, ("whi", [P, 6, D], F32R), ("wlo", [P, 6, D], F32R))
        hhi, hlo, off_x = plan(off_h, ("hhi", [P, KD * T], F32R), ("hlo", [P, KD * T], F32R))
        x, off_g = plan(off_x, ("x", [P, KD * T], F32))
        gh, gl, off_end = plan(off_g, ("gh", [P, 4 * T], F32R), ("gl", [P, 4 * T], F32R))
        xin, nrow, _ = plan(off_g, ("xin", [P, 2, D], F32), ("nrow", [P, P], F32))
        zst, _ = plan(off_g, ("zst", [P, 2, T], F32))
        tokkv, oa = plan(off_a, ("tokkv", [P, 2, 9, P], F32))
        assert oa <= off_a + 3 * 3072
        zt, tok, wsr, wsT, bT, ug, mg, tri0, _ = plan(
            off_x, ("zt", [P, 2, T], F32), ("tok", [P, 2, 9, P], F32), ("wsr", [P, 8, P], F32), ("wsT", [P, 8, P], F32),
            ("bT", [P, 4, P], F32), ("ug", [P, 2, T], F32), ("mg", [P, 2, 384], F32), ("tri0", [P, P], F32))
        KCOL = T + 64 + PAST
        kS, qS, kst, oa = plan(
            off_x, ("kS", [P, 4, KCOL], F32R),
            ("qS", [P, 4, 2, T], F32R),
            ("kst", [P, T + PAST], F32))
        assert oa <= off_end
        tri, comp, qst, oa = plan(off_a, ("tri", [P, P], F32R), ("comp", [P, P], F32R), ("qst", [P, T], F32))
        assert oa <= off_a + 2 * 3072
        off_raw = off_w - 2 * D * 4
        esp, tz, sphi, vv, oa = plan(off_raw, ("esp", [P, 4, 2, 512], F32), ("tz", [P, 4, 2, 512], F32),
                                     ("sphi", [P, 2, 2, 512], F32R), ("vv", [P, 2, 13, P], F32))
        assert oa <= off_h
        splo, _ = plan(off_raw, ("splo", [P, 4, 2, 512], F32R))

        eb, bo, co_, pb, _ = plan(off_x, ("eb", [P, 3, 8, NCH], F32), ("bo", [P, 8, 2, P], F32), ("co", [P, 8, 2, CW], F32),
                                  ("pb", [P, 2, GP, L], F32))
        assert _ <= off_g
        ct, bb, pc, sc, ek, par, pp, off_t, = plan(
            off_g + 2 * T * 4, ("ct", [P, 2, GP, 16], F32), ("bb", [P, 2, GP, 16], F32), ("pc", [P, 2, GP, L + 1], F32),
            ("sc", [P, 20, GP], F32), ("ek", [P, 2, GP, 7], F32), ("par", [P, 5, GP], F32), ("pp", [P, 4, GP], F32))
        t1, t2, _ = plan(off_t, ("t1", [P, 8 * CW], F32), ("t2", [P, 8 * CW], F32))
        assert _ <= off_end
        lt, craw, lstep, _ = plan(off_t, ("lt", [P, 5, P], F32), ("craw", [P, 2, 8, 64], F32), ("lstep", [P, 2], F32))
        (S_step, S_mag, S_lrs, S_r8, S_sin, S_cos, S_ang, S_k, S_r, S_rc, S_a, S_b, S_c, S_nr, S_cor, S_coi, *S_ef) = (
            sc[:, n, :] for n in range(20))
        S_e, S_f = S_ef[0:2], S_ef[2:4]
        br, bt, zb1, oa = plan(off_w, ("br", [P, 4, 2, P], F32), ("bt", [P, 4, 2, P], F32), ("zb1", [P, T], F32))
        assert oa <= off_w + 4 * D * 4
        tm, kt, p4, _ = plan(off_w + 6 * D * 4, ("tm", [P, 2, 8, P], F32), ("kt", [P, 8, P], F32), ("p4", [P, 4, GP], F32))
        u, ca, sh, oa = plan(off_h, ("u", [P, 2, 8, NCH], F32), ("ca", [P, 3, 4, 2, CW], F32), ("sh", [P, 2, 2, 4, NCH], F32))
        assert oa <= off_h + KD * T * 4
        yp, _ = plan(off_h + KD * T * 4, ("yp", [P, KD * T], F32))
        e3, xx, v1, v2, v3, w1, w2, yy, zb0, oa = plan(
            off_x, ("e3", [P, 3, 4, NCH], F32), ("xx", [P, 8 * NCH], F32), ("v1", [P, 4 * NCH], F32), ("v2", [P, 4 * NCH], F32),
            ("v3", [P, 4 * NCH], F32), ("w1", [P, 4 * NCH], F32), ("w2", [P, 4 * NCH], F32), ("yy", [P, 2, 8, NCH], F32),
            ("zb0", [P, T], F32))
        assert oa <= off_g
        zb = [zb0, zb1]
        v1, v2, v3, w1, w2 = v1[:], v2[:], v3[:], w1[:], w2[:]
        hp, _ = plan(off_g, ("hp", [P, KD * T], F32))
        fin, fout, _ = plan(off_w - 2 * D * 4 - 3072, ("fin", [P, 4, GP], F32), ("fout", [P, 4, P], F32))
        sq, _ = plan(off_g, ("sq", [P, 6, 384], F32))
        ssum, _ = plan(off_end, ("ssum", [P, NC, 384], F32))
        yf, _ = plan(off_h, ("yf", [P, KD * T], F32))
        yo, _ = plan(off_g, ("yo", [P, 2, D], F32))

        ps = ctx.enter_context(nc.psum_tensor("ps", [P, 8, 512], F32))

        zT = nc.dram_tensor("zT", [IN_TILES * P, T], F32).ap()
        kcT = nc.dram_tensor("kcT", [SB, PAST], F32).ap()
        dE = nc.dram_tensor("dE", [P, 3, GP, NCH], F32).ap()
        dB = nc.dram_tensor("dB", [P, GP, 2, P], F32).ap()
        dC = nc.dram_tensor("dC", [P, GP, 2, CW], F32).ap()
        dP = nc.dram_tensor("dP", [P, 4, GP], F32).ap()
        dU = nc.dram_tensor("dU", [KD * P, T], F32).ap()
        dY = nc.dram_tensor("dY", [KD * P, T], F32).ap()
        xs = nc.dram_tensor("xs", [P, KD * T], F32).ap()

        xp = A["x_prompt"].rearrange("b t d -> (b t) d")
        xd = A["x_sample"].rearrange("b t d -> (b t) d")

        x3 = x[:].rearrange("p (f t) -> p f t", f=KD)
        epsb = cols[:, 48:49]
        dneg = rms[:, 1, 0:P]

        def kview(w):
            return w.rearrange("(k p) n -> p k n", p=P)

        w_in, w_out = kview(A["ab_w_in"][0]), kview(A["ab_w_out"][0])
        w_gate = [kview(A["ffn_w_gate"][l]) for l in range(2)]
        w_up = [kview(A["ffn_w_up"][l]) for l in range(2)]
        w_down = [A["ffn_w_down"][l] for l in range(2)]
        w_glu = kview(A["ssm_w_glu"][0])
        k_new = [O["k_p"].rearrange("a b t h d -> (a b t) (h d)"), O["k_s"].rearrange("a b t h d -> (a b t) (h d)")]
        v_new = [O["v_p"].rearrange("a b t h d -> (a b t) (h d)"), O["v_s"].rearrange("a b t h d -> (a b t) (h d)")]
        g_new = O["g_s"].rearrange("a b t d -> (a b t) d")
        y_new = [O["y_p"].rearrange("b t d -> (b t) d"), O["y_s"].rearrange("b t d -> (b t) d")]
        ck = A["cache_sb_k"].rearrange("a b t h d -> (a b t) (h d)")
        cv = A["cache_sb_v"].rearrange("a b t h d -> (a b t) (h d)")

        def load_slab(sp, t, src, i=None, b=0):
            if t >= 2:
                sp.wait_ge(sem("w_lo"), step(t - 1, i, b))
            dst = raw[:, t % 2, :]
            if len(src.shape) == 3:
                dst = dst.rearrange("p (k n) -> p k n", k=KD)
            sp.dma_start(dst, src).then_inc(sem(f"raw_loaded{t % 2}"), 16)

        def slab_hi(act, t, left=None, count=0, i=None, b=0, per=0):
            act.wait_ge(sem(f"raw_loaded{t % 2}"), step(16 * (t // 2 + 1), i, 8 * b))
            if left:
                act.wait_ge(sem(left), step(count, i, per))
            act.activation(whi[:, slot(t), :], raw[:, t % 2, :], ACT.Copy).then_inc(sem("w_hi"), 1)

        def slab_lo(pool, t, i=None, b=0):
            pool.wait_ge(sem("w_hi"), step(t + 1, i, b))
            pool.tensor_tensor(wlo[:, slot(t), :], raw[:, t % 2, :], whi[:, slot(t), :].bitcast(F32),
                               ALU.subtract).then_inc(sem("w_lo"), 1)

        def three(pe, out, s, col, rh, rl, first, last):
            wh, wl = whi[:, s, col:col + P], wlo[:, s, col:col + P]
            pe.matmul(out, wh, rh, start=first, stop=False)
            pe.matmul(out, wh, rl, start=False, stop=False)
            return pe.matmul(out, wl, rh, start=False, stop=last)

        def eight(pe, out, s, c, ready=None):
            s0, n = CHUNKS[c]
            for k in range(KD):
                if ready:
                    ready(c, k)
                o = k * T + s0
                mm = three(pe, out[:, 0:n], s, k * P, hhi[:, o:o + n], hlo[:, o:o + n], k == 0, k == KD - 1)
            return mm

        def acc(v):
            return ps[:, 4 + v % 4, :]

        def pe_single(pe, t, i=None, b=0, ready=None):
            pe.wait_ge(sem("w_lo"), step(t + 1, i, b))
            for c in range(NC):
                v = NC * t + c
                if v >= 4:
                    pe.wait_ge(sem("acc_used"), step(v - 3, i, NC * b))
                eight(pe, acc(v), slot(t), c, ready).then_inc(sem("acc_ready"), 1)

        def pe_pair(pe, t, v0, i=None, b=0, per=0, ready=None):
            pe.wait_ge(sem("w_lo"), step(t + 2, i, b))
            for c in range(NC):
                v = v0 + c
                if v >= 2:
                    pe.wait_ge(sem("pair_used"), step(v - 1, i, per))
                if ready:
                    s0, n = CHUNKS[c]
                    for k in range(KD):
                        ready(c, k)
                        o = k * T + s0
                        for j in range(2):
                            mm = three(pe, ps[:, 2 * (v % 2) + j, 0:n], slot(t + j), k * P, hhi[:, o:o + n], hlo[:, o:o + n],
                                       k == 0, k == KD - 1)
                    mm.then_inc(sem("pair_ready"), 1)
                else:
                    eight(pe, ps[:, 2 * (v % 2), :], slot(t), c)
                    eight(pe, ps[:, 2 * (v % 2) + 1, :], slot(t + 1), c).then_inc(sem("pair_ready"), 1)

        SPLIT = {0: 0, 1: 1, 3: 2}

        def n_units(k, e=NC * KD):
            return NC * KD * k + e

        def n_split(k, e=NC * KD):
            return NC * KD * SPLIT[k] + e

        def order(k, c, f, tiles=KD):
            return f * NC + c if k in (1, 3) else c * tiles + f

        def n_adds(k, a=NC * (KD - 1)):
            return NC * (KD - 1) * (k - 1) + a

        def sqbuf(k, a):
            return sq[:, a % 6, :] if k in (1, 3) else abuf[:, a % 2, :]

        def square(act, k, c, f):
            s, n = CHUNKS[c]
            if k == 0:
                e = order(0, c, f)
                if e >= 2:
                    act.wait_ge(sem("sq_read"), e - 1)
                out = abuf[:, e % 2, 0:n]
            elif f == 0:
                if k >= 2:
                    act.wait_ge(sem("n_sum"), NC * (k - 2) + c + 1)
                out = ssum[:, c, 0:n]
            else:
                a = order(k, c, f - 1, KD - 1)
                ring = 6 if k in (1, 3) else 2
                if n_adds(k, a) >= ring:
                    act.wait_ge(sem("n_add"), n_adds(k, a + 1 - min(ring, a + 1)))
                out = sqbuf(k, a)[:, 0:n]
            act.activation(out, x[:, f * T + s:f * T + s + n], ACT.Square).then_inc(sem("n_sq"), 1)

        def add_square(pool, k, c, f):
            if f == 0:
                return
            n = CHUNKS[c][1]
            a = order(k, c, f - 1, KD - 1)
            pool.wait_ge(sem("n_sq"), n_units(k, order(k, c, f) + 1))
            if n_adds(k, a):
                pool.wait_ge(sem("n_add"), n_adds(k, a))
            pool.tensor_tensor(ssum[:, c, 0:n], ssum[:, c, 0:n], sqbuf(k, a)[:, 0:n], ALU.add).then_inc(sem("n_add"), 1)

        def sbank(k, c):
            return 4 + c if k == 3 else c

        def sum_pe0(pe, c):
            n = CHUNKS[c][1]
            for f in range(KD):
                e = order(0, c, f)
                pe.wait_ge(sem("n_sq"), e + 1)
                mm = pe.matmul(ps[:, c, 0:n], ones[:], abuf[:, e % 2, 0:n], start=f == 0, stop=f == KD - 1)
                mm.then_inc(sem("sq_read"), 1)

        def sum_pe(pe, k, c):
            n = CHUNKS[c][1]
            pe.wait_ge(sem("n_add"), n_adds(k, order(k, c, KD - 2, KD - 1) + 1))
            pe.matmul(ps[:, sbank(k, c), 0:n], ones[:], ssum[:, c, 0:n], start=True, stop=True).then_inc(sem("n_sum"), 1)

        def x_in(eng, c):
            last = (3, 6, 9)[c]
            eng.wait_ge(sem("xt_a"), last)
            eng.wait_ge(sem("xt_v"), last)

        def norm_act(act, k, split):
            def root(c):
                n = CHUNKS[c][1]
                if k:
                    act.wait_ge(sem("n_sum"), NC * (k - 1) + c + 1)
                else:
                    act.wait_ge(sem("sq_read"), KD * (c + 1))
                if c >= 2:
                    act.wait_ge(sem("n_f"), n_units(k, KD * (c - 1)))
                act.activation(rms[:, c % 2, 0:n], ps[:, sbank(k, c), 0:n], ACT.Sqrt, bias=epsb[:, 0:1], scale=1.0 / D
                               ).then_inc(sem("n_rt"), 1)

            def his(c, tiles=range(KD)):
                s, n = CHUNKS[c]
                for f in tiles:
                    e = c * KD + f
                    act.wait_ge(sem("n_f"), n_units(k, e + 1))
                    act.activation(hhi[:, f * T + s:f * T + s + n], fbuf[:, e % 2, 0:n], ACT.Copy).then_inc(sem("n_hi"), 1)

            if k == 0:
                for c in range(NC):
                    x_in(act, c)
                    for f in range(KD):
                        square(act, k, c, f)
                        if c:
                            his(c - 1, (f,))
                    root(c)
            else:
                root(0)
                root(1)
                if split:
                    his(0)
                root(2)
            if split:
                if k:
                    his(1)
                his(2)

        def norm_dve(dve, k, row, plain=None, by_chunk=False):
            for c, (s, n) in enumerate(CHUNKS):
                dve.wait_ge(sem("n_rt"), NC * k + c + 1)
                dve.reciprocal(rms[:, c % 2, 0:n], rms[:, c % 2, 0:n]).then_inc(sem("n_rr"), 1)
                dve.wait_ge(sem("n_rr"), NC * k + c + 1)
                for f in range(KD):
                    e = c * KD + f
                    out = fbuf[:, e % 2, 0:n]
                    if plain is not None:
                        out = plain[:, f * T + s:f * T + s + n]
                    elif e >= 2:
                        dve.wait_ge(sem("n_lo"), n_split(k, e - 1))
                    xf, rf = x[:, f * T + s:f * T + s + n], rms[:, c % 2, 0:n]
                    if by_chunk:
                        out = plain[:, f * T:(f + 1) * T].rearrange("p (s n) -> p n s", s=L)[:, s // L:(s + n) // L, :]
                        xf, rf = (v.rearrange("p (n s) -> p n s", s=L) for v in (xf, rf))
                    dve.scalar_tensor_tensor(out, xf, cols[:, row + f:row + f + 1], rf, ALU.mult, ALU.mult).then_inc(sem("n_f"), 1)

        def norm_pool(pool, k):
            for c, (s, n) in enumerate(CHUNKS):
                for f in range(KD):
                    e = c * KD + f
                    o = f * T + s
                    pool.wait_ge(sem("n_hi"), n_split(k, e + 1))
                    pool.tensor_tensor(hlo[:, o:o + n], fbuf[:, e % 2, 0:n], hhi[:, o:o + n].bitcast(F32),
                                       ALU.subtract).then_inc(sem("n_lo"), 1)

        def h_ready(k):
            return lambda eng: (lambda c, f: eng.wait_ge(sem("n_lo"), n_split(k, KD * c + f + 1)))

        class Ffn:
            def __init__(self, layer):
                self.l = layer
                self.slab = (SLAB_FF0, SLAB_FF1)[layer]
                self.pair = (0, PAIR_FF1)[layer]
                self.acc = (ACC_FF0, ACC_FF1)[layer]
                self.hid = (0, 2 * PARTS * NC)[layer]
                self.norm = (1, 3)[layer]

        F = [Ffn(0), Ffn(1)]

        def ffn_sp(sp, f, skip=0):
            def gu(tile, t, i=None):
                o = step(tile * P, i, 2 * P)
                for w, tt in ((w_gate[f.l], t), (w_up[f.l], t + 1)):
                    load_slab(sp, tt, w[:, :, bass.ds(o, P)] if i is not None else w[:, :, o:o + P], i, 6)

            def down(tile, t, i=None):
                for j in range(2):
                    o = step((tile + j) * P, i, 2 * P)
                    load_slab(sp, t + j, w_down[f.l][bass.ds(o, P), :] if i is not None else w_down[f.l][o:o + P, :], i, 6)

            if not skip:
                gu(0, f.slab)
                return
            gu(1, f.slab + 2)
            with sp.Fori(0, PARTS - 1) as i:
                gu(2, f.slab + 4, i)
                gu(3, f.slab + 6, i)
                down(0, f.slab + 8, i)
            down(2 * PARTS - 2, f.slab + 64)

        def ffn_act(act, f, start_sem, start_count):
            def silu(v0, i=None):
                for c, (s, n) in enumerate(CHUNKS):
                    v = v0 + c
                    act.wait_ge(sem("pair_ready"), step(v + 1, i, 6))
                    if v >= 2:
                        act.wait_ge(sem("pair_used"), step(v - 1, i, 6))
                    act.activation(abuf[:, v % 2, 0:n], ps[:, 2 * (v % 2), 0:n], ACT.Silu).then_inc(sem("pair_act"), 1)

            for q in range(2):
                for j in range(2):
                    slab_hi(act, f.slab + 2 * q + 2 + j, start_sem, start_count)
                silu(f.pair + NC * q)
            with act.Fori(0, PARTS - 1) as i:
                t = f.slab + 4
                for j in range(2):
                    slab_hi(act, t + 2 + j, "pair_ready", f.pair + 2 * NC, i, 6, 6)
                silu(f.pair + 2 * NC, i)
                for j in range(2):
                    slab_hi(act, t + 4 + j, "acc_ready", f.acc, i, 6, KD * NC)
                silu(f.pair + 3 * NC, i)
                for j in range(2):
                    slab_hi(act, t + 6 + j, "pair_ready", f.pair + 3 * NC, i, 6, 6)
            if f.l == 0:
                for j in range(2):
                    slab_hi(act, SLAB_GLU + j, "pair_ready", PAIR_GLU)
            for c in range(NC):
                for m in range(KD):
                    act.wait_ge(sem("acc_used"), f.acc + (PARTS - 1) * KD * NC + c * KD + m + 1)
                    square(act, f.norm + 1, c, m)
                    if f.l == 1:
                        o, n = m * T + CHUNKS[c][0], CHUNKS[c][1]
                        act.activation(yf[:, o:o + n], x[:, o:o + n], ACT.Identity, scale=cols[:, 32 + m:33 + m]).then_inc(sem("yg"), 1)

        def ffn_pool(pool, f):
            def lo(v0, half, i=None):
                for c, (s, n) in enumerate(CHUNKS):
                    v, h = v0 + c, f.hid + v0 - f.pair + c
                    o = (half if i is None else ((i + 1) % 2) * (2 * T) + half) + s
                    pool.wait_ge(sem("hid_hi"), step(h + 1, i, 6))
                    pool.tensor_tensor(gl[:, bass.ds(o, n)], fbuf[:, v % 2, 0:n], gh[:, bass.ds(o, n)].bitcast(F32),
                                       ALU.subtract).then_inc(sem("hid_lo"), 1)

            for q in range(2):
                for j in range(2):
                    slab_lo(pool, f.slab + 2 * q + 2 + j)
                lo(f.pair + NC * q, q * T)
            with pool.Fori(0, PARTS - 1) as i:
                t = f.slab + 4
                for q in range(2):
                    for j in range(2):
                        slab_lo(pool, t + 2 * q + 2 + j, i, 6)
                    lo(f.pair + (2 + q) * NC, q * T, i)
                for j in range(2):
                    slab_lo(pool, t + 6 + j, i, 6)
            if f.l == 0:
                for j in range(2):
                    slab_lo(pool, SLAB_GLU + j)
            for c in range(NC):
                for m in range(KD):
                    add_square(pool, f.norm + 1, c, m)

        def ffn_pe(pe, f):
            def down(t, v0, h0, i=None, buf=None):
                buf = (i % 2) * (2 * T) if buf is None else buf
                pe.wait_ge(sem("w_lo"), step(t + 2, i, 6))
                for c, (s, n) in enumerate(CHUNKS):
                    pe.wait_ge(sem("hid_lo"), step(h0 + c + 1, i, 6))
                    for m in range(KD):
                        v = v0 + c * KD + m
                        pe.wait_ge(sem("acc_used"), step(v - 3, i, KD * NC))
                        for j in range(2):
                            o = buf + j * T + s
                            mm = three(pe, acc(v)[:, 0:n], slot(t + j), m * P, gh[:, bass.ds(o, n)], gl[:, bass.ds(o, n)],
                                       j == 0, j == 1)
                        mm.then_inc(sem("acc_ready"), 1)
                        if i is None and f.l == 0 and c == NC - 1 and m >= KD - 2:
                            sum_pe(pe, f.norm + 1, m - (KD - 2))
                if i is None and f.l == 0:
                    sum_pe(pe, f.norm + 1, NC - 1)

            pe_pair(pe, f.slab, f.pair, ready=h_ready(f.norm)(pe))
            pe_pair(pe, f.slab + 2, f.pair + NC)
            with pe.Fori(0, PARTS - 1) as i:
                pe_pair(pe, f.slab + 4, f.pair + 2 * NC, i, 6, 6)
                pe_pair(pe, f.slab + 6, f.pair + 3 * NC, i, 6, 6)
                down(f.slab + 8, f.acc, f.hid + NC, i)
            down(f.slab + 64, f.acc + (PARTS - 1) * KD * NC, f.hid + NC * (2 * PARTS - 1), buf=((PARTS - 1) % 2) * 2 * T)

        def ffn_dve(dve, f):
            def hidden(v0, half, i=None):
                for c, (s, n) in enumerate(CHUNKS):
                    v, h = v0 + c, f.hid + v0 - f.pair + c
                    o = (half if i is None else ((i + 1) % 2) * (2 * T) + half) + s
                    dve.wait_ge(sem("pair_act"), step(v + 1, i, 6))
                    if h >= 2:
                        dve.wait_ge(sem("hid_lo"), step(h - 1, i, 6))
                    dve.tensor_tensor(fbuf[:, v % 2, 0:n], ps[:, 2 * (v % 2) + 1, 0:n], abuf[:, v % 2, 0:n],
                                      ALU.mult).then_inc(sem("pair_used"), 1)
                    dve.wait_ge(sem("pair_used"), step(v + 1, i, 6))
                    dve.tensor_copy(gh[:, bass.ds(o, n)], fbuf[:, v % 2, 0:n]).then_inc(sem("hid_hi"), 1)

            def residual(v0, i=None):
                for c, (s, n) in enumerate(CHUNKS):
                    for m in range(KD):
                        v = v0 + c * KD + m
                        dve.wait_ge(sem("acc_ready"), step(v + 1, i, KD * NC))
                        xo = x[:, m * T + s:m * T + s + n]
                        dve.tensor_tensor(xo, acc(v)[:, 0:n], xo, ALU.add).then_inc(sem("acc_used"), 1)

            dve.wait_ge(sem("n_lo"), n_split(f.norm))
            hidden(f.pair, 0)
            hidden(f.pair + NC, T)
            with dve.Fori(0, PARTS - 1) as i:
                hidden(f.pair + 2 * NC, 0, i)
                hidden(f.pair + 3 * NC, T, i)
                residual(f.acc, i)
            residual(f.acc + (PARTS - 1) * KD * NC)

        def zrow(n):
            return (KT + n if n < 8 else GT + n - 12) * P

        tp_units = [(n, b) for n in range(8, 16) for b in range(1 if 8 <= n < 12 else NC)]
        tp_no = {nb: u for u, nb in enumerate(tp_units)}
        TP_V = sum(n < 12 for n, _ in tp_units)

        def tp_taken(eng, u):
            if u < TP_V:
                eng.wait_ge(sem("tp_used_v"), u + 1)
            else:
                eng.wait_ge(sem("tp_used_a"), u + 1 - TP_V)

        def kv_pe(pe, m, i=None, t=0):
            pe.wait_ge(sem("acc_used"), step(NC * (KT + m + 1), i, NC * 4))
            if i is not None or m:
                pe.wait_ge(sem("kv_used"), step(4 * m, i, 16))
            for q, (s, w) in enumerate(TILES):
                mm = pe.transpose(ps[0:w, q // 3, (q % 3) * P:(q % 3 + 1) * P], zst[:, m % 2, s:s + w], ident[:])
            mm.then_inc(sem("kv_mm"), 1)

        def kv_act(act, m):
            act.wait_ge(sem("kv_mm"), m + 1)
            if m >= 2:
                act.wait_ge(sem(f"kv_out{m % 2}"), 32 * (m // 2))
            for b, n in ((0, 3), (1, 3), (2, 2)):
                act.activation(tokkv[:, m % 2, 3 * b:3 * b + n, :], ps[:, b, 0:n * P].rearrange("p (b n) -> p b n", b=n), ACT.Copy
                               ).then_inc(sem("kv_used"), 1)
            act.activation(tokkv[0:DEC, m % 2, 8, :], ps[0:DEC, 2, 256:384], ACT.Copy).then_inc(sem("kv_used"), 1)

        def kv_store(sp, m):
            dst = (k_new, v_new)[m // 4]
            cs = slice((m % 4) * P, (m % 4 + 1) * P)
            sp.wait_ge(sem("kv_used"), 4 * m + 4)
            sp.dma_start(dst[0][:, cs].rearrange("(t p) n -> p t n", p=P), tokkv[:, m % 2, 0:8, :]).then_inc(sem(f"kv_out{m % 2}"), 16)
            sp.dma_start(dst[1][:, cs], tokkv[0:DEC, m % 2, 8, :]).then_inc(sem(f"kv_out{m % 2}"), 16)

        def tr_sp(sp):
            for n in range(3):
                sp.wait_ge(sem(f"prep_out{n}"), 64)
            sp.dma_start(wsr[:], A["sgu_w"][0].rearrange("g t s -> t g s")).then_inc(sem("ws_loaded"), 16)
            for j in range(4):
                for a in range(2):
                    sp.dma_start(bT[64 * a:64 * a + 64, j, :], A["sgu_b"][0, 2 * j + a:2 * j + a + 1, :].to_broadcast([64, P])
                                 ).then_inc(sem("bT_loaded"), 16)
            for n in range(8, 17):
                if n == 12:
                    sp.wait_ge(sem("z_stored0"), 16 * IN_TILES // 2)
                    sp.wait_ge(sem("z_stored1"), 16 * IN_TILES // 2)
                if n < 16:
                    if n >= 10:
                        sp.wait_ge(sem("tp_mm"), tp_no[(n - 1, 0)])
                    if 8 <= n < 12:
                        sp.dma_start(zt[:, n % 2, 0:512].rearrange("p (b n) -> p b n", b=4),
                                     ck[:, (n - 8) * P:(n - 7) * P].rearrange("(b p) n -> p b n", p=P)).then_inc(sem(f"zt_loaded{n % 2}"), 16)
                    else:
                        sp.dma_start(zt[:, n % 2, :], zT[zrow(n):zrow(n) + P, :]).then_inc(sem(f"zt_loaded{n % 2}"), 16)
                    if n >= 12:
                        j = n - 12
                        if j >= 2:
                            sp.wait_ge(sem("mix_f"), 2 * NC * (j - 1))
                        sp.dma_start(ug[:, j % 2, :], zT[(UT + j) * P:(UT + j + 1) * P, :]).then_inc(sem(f"ug_loaded{j % 2}"), 16)
                if n >= 9:
                    m = n - 1
                    tp_taken(sp, tp_no[(m, 0 if 8 <= m < 12 else 2)])
                    cs = slice((m % 4) * P, (m % 4 + 1) * P)
                    if m < 12:
                        sp.dma_start(kcT[cs, :], tok[:, m % 2, 0:4, :].rearrange("p b n -> p (b n)")).then_inc(sem(f"tok_out{m % 2}"), 16)
                    else:
                        sp.dma_start(g_new[:, cs], tok[0:DEC, m % 2, 8, :]).then_inc(sem(f"tok_out{m % 2}"), 16)
                if n == 15:
                    sp.wait_ge(sem("kv_out0"), 32 * 4)
                    sp.wait_ge(sem("kv_out1"), 32 * 4)
                    k_load(sp, 0)
                    q_load(sp, 0)

        def tok_free(eng, n):
            if n >= 10:
                eng.wait_ge(sem(f"tok_out{n % 2}"), 16 * ((n - 8) // 2))
            if n >= 14:
                eng.wait_ge(sem("mix_mm"), NC * (n - 13))

        def tr_pe(pe):
            pe.wait_ge(sem("ws_loaded"), 16)
            pe.wait_ge(sem("acc_used"), NC * IN_TILES)
            for g in range(8):
                mm = pe.transpose(ps[:, 6 + g // 4, (g % 4) * P:(g % 4 + 1) * P], wsr[:, g, :], ident[:])
            mm.then_inc(sem("ws_mm"), 1)
            for u, (n, b) in enumerate(tp_units):
                if b == 0:
                    pe.wait_ge(sem(f"zt_loaded{n % 2}"), 16 * ((n - 8) // 2 + 1))
                if u >= 6:
                    tp_taken(pe, u - 6)
                for r in range(4 if 8 <= n < 12 else 3):
                    if 8 <= n < 12:
                        mm = pe.transpose(ps[:, u % 6, r * P:(r + 1) * P], zt[:, n % 2, r * P:(r + 1) * P], ident[:])
                    else:
                        s, w = TILES[3 * b + r]
                        mm = pe.transpose(ps[0:w, u % 6, r * P:(r + 1) * P], zt[:, n % 2, s:s + w], ident[:])
                mm.then_inc(sem("tp_mm"), 1)
                if n >= 12 and b == 2:
                    gate_pe(pe, n - 12)

        def gate_pe(pe, j):
            tp_taken(pe, tp_no[(12 + j, 2)])
            pe.wait_ge(sem("ws_t"), 8)
            for c in range(NC):
                s = NC * j + c
                if s >= 2:
                    pe.wait_ge(sem("mix_f"), 2 * (s - 1) - 1)
                for r in range(3):
                    w = TILES[3 * c + r][1]
                    for a in range(2):
                        mm = pe.matmul(ps[64 * a:64 * a + 64, 6 + s % 2, r * P:r * P + w],
                                       tok[0:w, (12 + j) % 2, 3 * c + r, 64 * a:64 * a + 64], wsT[0:w, 2 * j + a, 0:w],
                                       start=True, stop=True, skip_group_check=True)
                mm.then_inc(sem("mix_mm"), 1)

        def tr_dve(dve):
            for u, (n, b) in enumerate(tp_units[:TP_V]):
                if b == 0:
                    tok_free(dve, n)
                dve.wait_ge(sem("tp_mm"), u + 1)
                if 8 <= n < 12:
                    dve.tensor_copy(tok[:, n % 2, 0:4, :], ps[:, u % 6, 0:512].rearrange("p (b n) -> p b n", b=4)).then_inc(sem("tp_used_v"), 1)
                elif b < 2:
                    dve.tensor_copy(tok[:, n % 2, 3 * b:3 * b + 3, :], ps[:, u % 6, 0:384].rearrange("p (b n) -> p b n", b=3)
                                    ).then_inc(sem("tp_used_v"), 1)
                else:
                    dve.tensor_copy(tok[0:DEC, n % 2, 8, :], ps[0:DEC, u % 6, 256:384]).then_inc(sem("tp_part"), 1)
                    dve.wait_ge(sem("tp_part"), sum(1 for m, bb in tp_units[:u + 1] if bb == 2))
                    dve.tensor_copy(tok[:, n % 2, 6:8, :], ps[:, u % 6, 0:256].rearrange("p (b n) -> p b n", b=2)).then_inc(sem("tp_used_v"), 1)
            dve.wait_ge(sem("ws_mm"), 1)
            dve.wait_ge(sem("tri0_made"), 1)
            for g in range(8):
                dve.tensor_tensor(wsT[:, g, :], ps[:, 6 + g // 4, (g % 4) * P:(g % 4 + 1) * P], tri0[:], ALU.mult).then_inc(sem("ws_t"), 1)
            dve.wait_ge(sem("bT_loaded"), 16 * 8)
            for s in range(4 * NC):
                j, c = divmod(s, NC)
                s0, n = CHUNKS[c]
                dve.wait_ge(sem("mix_mm"), s + 1)
                if s >= 2:
                    dve.wait_ge(sem("mix_lo"), s - 1)
                for r in range(3):
                    w = TILES[3 * c + r][1]
                    ins = dve.tensor_tensor(mg[:, s % 2, r * P:r * P + w], ps[:, 6 + s % 2, r * P:r * P + w], bT[:, j, 0:w], ALU.add)
                    ins.then_inc(sem("mix_f" if r == 2 else "mix_part"), 1)
                dve.wait_ge(sem("mix_f"), 2 * s + 1)
                dve.wait_ge(sem("mix_part"), 2 * s + 2)
                dve.wait_ge(sem("ug_act"), j + 1)
                dve.tensor_tensor(mg[:, s % 2, 0:n], mg[:, s % 2, 0:n], ug[:, j % 2, s0:s0 + n], ALU.mult).then_inc(sem("mix_f"), 1)

        def tr_act(act):
            for j in range(4):
                n = 12 + j
                act.wait_ge(sem(f"ug_loaded{j % 2}"), 16 * (j // 2 + 1))
                act.activation(ug[:, j % 2, :], ug[:, j % 2, :], GELU).then_inc(sem("ug_act"), 1)
                tok_free(act, n)
                for b in range(NC):
                    u = tp_no[(n, b)]
                    act.wait_ge(sem("tp_mm"), u + 1)
                    if b < 2:
                        act.activation(tok[:, n % 2, 3 * b:3 * b + 3, :], ps[:, u % 6, 0:384].rearrange("p (b n) -> p b n", b=3), GELU
                                       ).then_inc(sem("tp_used_a"), 1)
                    else:
                        act.activation(tok[0:DEC, n % 2, 8, :], ps[0:DEC, u % 6, 256:384], GELU).then_inc(sem("tp_part_a"), 1)
                        act.wait_ge(sem("tp_part_a"), j + 1)
                        act.activation(tok[:, n % 2, 6:8, :], ps[:, u % 6, 0:256].rearrange("p (b n) -> p b n", b=2), GELU
                                       ).then_inc(sem("tp_used_a"), 1)
                for c in range(NC):
                    s = NC * j + c
                    s0, w = CHUNKS[c]
                    act.wait_ge(sem("mix_f"), 2 * s + 2)
                    o = (4 + j) * T + s0
                    act.activation(hhi[:, o:o + w], mg[:, s % 2, 0:w], ACT.Copy).then_inc(sem("mix_hi"), 1)

        def tr_pool(pool):
            for n in range(3):
                pool.wait_ge(sem(f"prep_out{n}"), 64)
            pool.wait_ge(sem("p_out"), 16)
            pool.wait_ge(sem("z_stored0"), 16 * IN_TILES // 2)
            pool.wait_ge(sem("z_stored1"), 16 * IN_TILES // 2)
            pool.memset(tri0[:], 1.0).then_inc(sem("pool"), 1)
            pool.wait_ge(sem("pool"), POOL0 + 1)
            pool.affine_select(out=tri0[:], in_=tri0[:], compare_op=ALU.is_ge, fill=0.0, base=0, pattern=[[1, P]],
                               channel_multiplier=-1).then_inc(sem("tri0_made"), 1)
            for s in range(4 * NC):
                j, c = divmod(s, NC)
                s0, w = CHUNKS[c]
                o = (4 + j) * T + s0
                pool.wait_ge(sem("mix_hi"), s + 1)
                pool.tensor_tensor(hlo[:, o:o + w], mg[:, s % 2, 0:w], hhi[:, o:o + w].bitcast(F32), ALU.subtract).then_inc(sem("mix_lo"), 1)

        units = []
        for pr in range(HEADS // 2):
            for q0, w, blocks in ((0, 512, range(3, -1, -1)), (512, 512, range(7, -1, -1)), (SEQ, DEC, range(4, -1, -1))):
                blocks = list(blocks)
                for b in blocks:
                    if q0 < SEQ:
                        off = max(0, b * P - q0)
                        units.append(dict(pr=pr, q0=q0, off=off, w=w - off, kc=b * P, vb=b, diag=b * P >= q0))
                    else:
                        units.append(dict(pr=pr, q0=q0, off=0, w=w, kc=SEQ if b == 4 else T + 64 + b * P,
                                          vb=8 if b == 4 else 9 + b, diag=b == 4))
                    units[-1].update(first=b == blocks[0], last=b == blocks[-1], total=w)
        NU = len(units)
        PAIR_U = NU // (HEADS // 2)
        GROUPS = sum(v["last"] for v in units)
        LEAD = 3
        group_no = {i: sum(v["last"] for v in units[:i]) for i in range(NU)}
        diags = [sum(v["diag"] for v in units[:i]) for i in range(NU + 1)]
        prep_at = {PAIR_U * (g // 2 - 1) + 4 * (g % 2) + 2 * s + 3: (g, s) for g in range(2, HEADS) for s in range(2)}

        def copied(i):
            return i + 1 + diags[i + 1]

        def sums_used(eng, i):
            if units[i]["last"]:
                eng.wait_ge(sem("u_tri"), i + 1)
            else:
                eng.wait_ge(sem("u_rest"), i + 1 - group_no[i])

        def k_load(sp, g):
            kr = slice((KT * P + g * HD), (KT * P + g * HD + HD))
            for a in range(2):
                sp.dma_start(kst[64 * a:64 * a + 64, 0:T], zT[kr, :]).then_inc(sem("k_loaded"), 16)
                sp.dma_start(kst[64 * a:64 * a + 64, T:T + PAST], kcT[g * HD:g * HD + HD, :]).then_inc(sem("k_loaded"), 16)

        def q_load(sp, g):
            for a in range(2):
                sp.dma_start(qst[64 * a:64 * a + 64, :], zT[g * HD:g * HD + HD, :]).then_inc(sem("q_loaded"), 16)

        def at_sp(sp):
            sp.wait_ge(sem("mix_lo"), 4 * NC)
            sp.wait_ge(sem("tok_out0"), 16 * 4)
            sp.wait_ge(sem("kv_out0"), 32 * 4)
            sp.wait_ge(sem("tok_out1"), 16 * 4)
            sp.wait_ge(sem("kv_out1"), 32 * 4)
            sp.wait_ge(sem("at_made"), 2)
            for g in range(HEADS):
                if g:
                    sp.wait_ge(sem("k_lo"), 2 * g)
                    k_load(sp, g)
                    sp.wait_ge(sem("q_lo"), 2 * g)
                    q_load(sp, g)
                if g % 2 == 0:
                    pr = g // 2
                    if pr >= 2:
                        sp.wait_ge(sem("u_pv"), PAIR_U * (pr - 1))
                    cs = slice(pr * P, pr * P + P)
                    sp.dma_start(vv[:, pr % 2, 0:8, :], v_new[0][:, cs].rearrange("(t p) n -> p t n", p=P)).then_inc(sem("v_loaded"), 16)
                    sp.dma_start(vv[0:DEC, pr % 2, 8, :], v_new[1][:, cs]).then_inc(sem("v_loaded"), 16)
                    sp.dma_start(vv[:, pr % 2, 9:13, :], cv[:, cs].rearrange("(t p) n -> p t n", p=P)).then_inc(sem("v_loaded"), 16)
            sp.wait_ge(sem("u_z"), NU)
            sp.dma_start(x[:], xs).then_inc(sem("x_back"), 16)
            sp.wait_ge(sem("u_pv"), NU)

        def at_pool_make(pool):
            pool.wait_ge(sem("mix_lo"), 4 * NC)
            pool.wait_ge(sem("tok_out0"), 16 * 4)
            pool.wait_ge(sem("kv_out0"), 32 * 4)
            pool.wait_ge(sem("tok_out1"), 16 * 4)
            pool.wait_ge(sem("kv_out1"), 32 * 4)
            pool.memset(vv[:, :, 8, :], 0.0).then_inc(sem("pool"), 1)
            pool.memset(kS[:, :, T:T + 64].bitcast(F32), 0.0).then_inc(sem("pool"), 1)
            pool.memset(dneg, 0.0).then_inc(sem("pool"), 1)
            pool.memset(esp[:, 0, 0, 0:P], 1.0).then_inc(sem("pool"), 1)
            pool.memset(esp[:, 0, 1, 0:P], 1.0).then_inc(sem("pool"), 1)
            pool.wait_ge(sem("pool"), POOL0 + 6)
            pool.affine_select(out=dneg, in_=dneg, compare_op=ALU.is_gt, fill=NEG, base=0, pattern=[[1, P]],
                               channel_multiplier=-1).then_inc(sem("pool"), 1)
            pool.affine_select(out=esp[:, 0, 0, 0:P], in_=esp[:, 0, 0, 0:P], compare_op=ALU.is_ge, fill=0.0, base=0,
                               pattern=[[-1, P]], channel_multiplier=1).then_inc(sem("pool"), 1)
            pool.affine_select(out=esp[:, 0, 1, 0:P], in_=esp[:, 0, 1, 0:P], compare_op=ALU.is_gt, fill=0.0, base=0,
                               pattern=[[1, P]], channel_multiplier=-1).then_inc(sem("pool"), 1)
            pool.wait_ge(sem("pool"), POOL0 + 9)
            pool.tensor_copy(tri[:], esp[:, 0, 0, 0:P]).then_inc(sem("at_made"), 1)
            pool.tensor_copy(comp[:], esp[:, 0, 1, 0:P]).then_inc(sem("at_made"), 1)

        def pair_start(i):
            return i < NU and i % PAIR_U == 0

        def at_act(act):
            act.wait_ge(sem("at_made"), 2)
            nc.scalar.preload_act_table_set("natural_log_exp_and_others")

            def prepare(g, s):
                if s == 0:
                    act.wait_ge(sem("k_loaded"), 64 * (g + 1))
                    act.activation(kS[:, g % 4, 0:T], kst[:, 0:T], ACT.Copy).then_inc(sem("k_hi"), 1)
                    act.activation(kS[:, g % 4, T + 64:KCOL], kst[:, T:T + PAST], ACT.Copy).then_inc(sem("k_hi"), 1)
                else:
                    act.wait_ge(sem("q_loaded"), 32 * (g + 1))
                    for v in range(2):
                        act.activation(qS[:, g % 4, v, :], qst[:], ACT.Copy).then_inc(sem("q_hi"), 1)

            for g in range(2):
                for s in range(2):
                    prepare(g, s)
            for i in range(-LEAD, NU + 2):
                if 0 <= i < NU:
                    act.wait_ge(sem("u_t"), i + 1)
                    tb = tz[:, i % 4, :, 0:units[i]["w"]]
                    act.activation(tb, tb, ACT.Exp).then_inc(sem("u_w"), 1)
                if i >= 2 and units[i - 2]["last"]:
                    u, g = units[i - 2], group_no[i - 2]
                    act.wait_ge(sem("u_pv"), i - 1)
                    o = u["pr"] * T + u["q0"]
                    act.activation(hhi[:, o:o + u["total"]], ps[:, 6 + g % 2, 0:u["total"]], ACT.Copy).then_inc(sem("o_hi"), 1)
                n = i + LEAD
                if n < NU:
                    w = units[n]["w"]
                    e = esp[:, n % 4, :, 0:w]
                    act.wait_ge(sem("u_c"), copied(n))
                    if n >= 4:
                        sums_used(act, n - 4)
                    act.activation(e, tz[:, n % 4, :, 0:w], ACT.Abs).then_inc(sem("u_e"), 1)
                    act.wait_ge(sem("u_e"), 3 * n + 1)
                    act.activation(e, e, ACT.Exp, scale=-1.0).then_inc(sem("u_e"), 1)
                    act.wait_ge(sem("u_e"), 3 * n + 2)
                    act.activation(e, e, ACT.Ln, bias=1.0).then_inc(sem("u_e"), 1)
                if i in prep_at:
                    prepare(*prep_at[i])

        def at_dve(dve):
            def prepare(g, s):
                if s == 0:
                    dve.wait_ge(sem("k_hi"), 2 * g + 2)
                    for d0, s0, n in ((0, 0, T), (T + 64, T, PAST)):
                        kl = kS[64:P, g % 4, d0:d0 + n]
                        dve.tensor_tensor(kl, kst[64:P, s0:s0 + n], kl.bitcast(F32), ALU.subtract).then_inc(sem("k_lo"), 1)
                else:
                    dve.wait_ge(sem("q_hi"), 2 * g + 2)
                    for v in range(2):
                        r = slice(64, P) if v == 0 else slice(0, 64)
                        ql = qS[r, g % 4, v, :]
                        dve.tensor_tensor(ql, qst[r, :], ql.bitcast(F32), ALU.subtract).then_inc(sem("q_lo"), 1)

            for g in range(2):
                for s in range(2):
                    prepare(g, s)
            for i in range(-LEAD, NU + 2):
                if 0 <= i < NU:
                    u, w = units[i], units[i]["w"]
                    tb = tz[:, i % 4, :, 0:w]
                    dve.wait_ge(sem("u_tri"), i + 1)
                    dve.tensor_tensor(tb, tb, ps[:, 4:6, u["off"]:u["off"] + w], ALU.subtract).then_inc(sem("u_t"), 1)
                c = i + LEAD
                if c < NU:
                    u, w = units[c], units[c]["w"]
                    tb = tz[:, c % 4, :, 0:w]
                    dve.wait_ge(sem("u_z"), c + 1)
                    if c >= 4:
                        dve.wait_ge(sem("u_pv"), c - 3)
                    b = 2 * (c % 2)
                    dve.tensor_scalar(tb, ps[:, b:b + 2, 0:w], HD ** -0.5, None, ALU.mult).then_inc(sem("u_c"), 1)
                    if u["diag"]:
                        dve.wait_ge(sem("u_c"), c + 1 + diags[c])
                        dw = min(P, w)
                        tb = tz[:, c % 4, :, 0:dw]
                        dve.tensor_tensor(tb, tb, dneg[:, 0:dw].unsqueeze(1).to_broadcast([P, 2, dw]), ALU.add).then_inc(sem("u_c"), 1)
                n = i + 2
                if 0 <= n < NU:
                    w = units[n]["w"]
                    e = esp[:, n % 4, :, 0:w]
                    dve.wait_ge(sem("u_e"), 3 * n + 3)
                    dve.scalar_tensor_tensor(e, tz[:, n % 4, :, 0:w], 0.0, e, ALU.max, ALU.add).then_inc(sem("u_sp"), 1)
                if 0 <= n < NU:
                    dve.wait_ge(sem("u_sp"), n + 1)
                    if n >= 2:
                        sums_used(dve, n - 2)
                    w = units[n]["w"]
                    dve.tensor_copy(sphi[:, n % 2, :, 0:w], esp[:, n % 4, :, 0:w]).then_inc(sem("u_sphi"), 1)
                if i >= 2 and units[i - 2]["last"]:
                    u, g = units[i - 2], group_no[i - 2]
                    dve.wait_ge(sem("o_hi"), g + 1)
                    o, m = u["pr"] * T + u["q0"], u["total"]
                    dve.tensor_tensor(hlo[:, o:o + m], ps[:, 6 + g % 2, 0:m], hhi[:, o:o + m].bitcast(F32), ALU.subtract
                                      ).then_inc(sem("o_lo"), 1)
                if i - 1 in prep_at:
                    prepare(*prep_at[i - 1])

        def at_pool(pool):
            for i in range(-LEAD, NU):
                n = i + 2
                if 0 <= n < NU:
                    w = units[n]["w"]
                    pool.wait_ge(sem("u_sphi"), n + 1)
                    pool.tensor_tensor(splo[:, n % 4, :, 0:w], esp[:, n % 4, :, 0:w], sphi[:, n % 2, :, 0:w].bitcast(F32),
                                       ALU.subtract).then_inc(sem("u_splo"), 1)
        def at_pe(pe):
            def scores(i):
                u = units[i]
                if i >= 2:
                    pe.wait_ge(sem("u_c"), copied(i - 2))
                if pair_start(i):
                    pe.wait_ge(sem("k_lo"), 4 * (u["pr"] + 1))
                    pe.wait_ge(sem("q_lo"), 4 * (u["pr"] + 1))
                h = 2 * (u["pr"] % 2)
                for a in range(2):
                    q = u["q0"] + u["off"]
                    out = ps[:, 2 * (i % 2) + a, 0:u["w"]]
                    pe.matmul(out, kS[:, h + a, u["kc"]:u["kc"] + P], qS[:, h + a, 0, q:q + u["w"]], start=True, stop=False)
                    mm = pe.matmul(out, kS[:, h + a, u["kc"]:u["kc"] + P], qS[:, h + a, 1, q:q + u["w"]], start=False, stop=True)
                mm.then_inc(sem("u_z"), 1)

            def sums(i, mat):
                u, w = units[i], units[i]["w"]
                for a in range(2):
                    out = ps[:, 4 + a, u["off"]:u["off"] + w]
                    for j, r in enumerate((sphi[:, i % 2, a, 0:w], splo[:, i % 4, a, 0:w])):
                        mm = pe.matmul(out, mat[:], r, start=mat is tri and u["first"] and j == 0, stop=True, skip_group_check=True)
                return mm

            def values(i):
                u, g = units[i], group_no[i]
                pe.wait_ge(sem("u_w"), i + 1)
                if u["first"] and g >= 2:
                    pe.wait_ge(sem("o_lo"), g - 1)
                if pair_start(i):
                    pe.wait_ge(sem("v_loaded"), 48 * (u["pr"] + 1))
                for a in range(2):
                    out = ps[64 * a:64 * a + 64, 6 + g % 2, u["off"]:u["off"] + u["w"]]
                    mm = pe.matmul(out, vv[:, u["pr"] % 2, u["vb"], 64 * a:64 * a + 64], tz[:, i % 4, a, 0:u["w"]],
                                   start=u["first"], stop=True, skip_group_check=True)
                mm.then_inc(sem("u_pv"), 1)

            pe.wait_ge(sem("at_made"), 2)
            pe.wait_ge(sem("mix_f"), 8 * NC)
            for i in range(-LEAD, NU + 1):
                if 0 <= i < NU:
                    pe.wait_ge(sem("u_splo"), i + 1)
                    if units[i]["first"] and i:
                        pe.wait_ge(sem("u_t"), i)
                    sums(i, tri).then_inc(sem("u_tri"), 1)
                if i + LEAD < NU:
                    scores(i + LEAD)
                if i >= 1:
                    values(i - 1)
                if 0 <= i < NU and not units[i]["last"]:
                    pe.wait_ge(sem("u_t"), i + 1)
                    sums(i, comp).then_inc(sem("u_rest"), 1)

        def prep_sp(sp):
            for j, (src, n) in enumerate((("ssm_lam_re", 1), ("ssm_lam_im", 2), ("state_ssm_re", 3), ("state_ssm_im", 4))):
                v = A[src].rearrange("o g p -> (o g p)" if src[0:3] == "ssm" else "o b g p -> (o b g p)")
                sp.dma_start(lt[0:GP, n, :], v.rearrange("(j q) -> j q", q=P)).then_inc(sem("par_loaded"), 16)
            sp.dma_start(lstep[0:GP, :], A["ssm_log_step"].rearrange("o (j a) -> (o j) a", a=2)).then_inc(sem("step_loaded"), 16)
            for r, src in enumerate(("ssm_c_re", "ssm_c_im")):
                sp.dma_start(craw[:, r, :, :], A[src].rearrange("o g c p -> (o g c) p").rearrange("(t q) p -> q t p", q=P)
                             ).then_inc(sem("c_loaded"), 16)
            for r, src in enumerate(("ssm_b_re", "ssm_b_im")):
                sp.dma_start(bb[:, r, :, :], A[src].rearrange("o (j a) p c -> (o a p) j c", a=2)).then_inc(sem("b_loaded"), 16)

        def prep_pe(pe):
            pe.wait_ge(sem("par_loaded"), 16 * 4)
            pe.wait_ge(sem("step_spread"), 1)
            for n in range(5):
                mm = pe.transpose(ps[:, 4, 64 + n * GP:64 + (n + 1) * GP], lt[0:GP, n, :], ident[0:GP, 0:GP])
            mm.then_inc(sem("par_mm"), 1)
            pe.wait_ge(sem("c_loaded"), 32)
            for q in range(4):
                if q == 3:
                    pe.wait_ge(sem("ct_made"), 2)
                for t in range(4):
                    mm = pe.transpose(ps[0:64, 5 + q % 3, t * P:(t + 1) * P], craw[:, q // 2, 4 * (q % 2) + t, :], ident[:])
                mm.then_inc(sem("c_mm"), 1)

        def prep_dve_in(dve):
            dve.wait_ge(sem("step_loaded"), 16)
            dve.tensor_copy(lt[0:GP, 0, :].rearrange("j (a p) -> j a p", a=2), lstep[0:GP, :].unsqueeze(2).to_broadcast([GP, 2, 64])
                            ).then_inc(sem("step_spread"), 1)
            dve.wait_ge(sem("par_mm"), 1)
            dve.tensor_copy(par[:], ps[:, 4, 64:64 + 5 * GP].rearrange("p (n j) -> p n j", n=5)).then_inc(sem("par_made"), 1)
            for q in range(4):
                dve.wait_ge(sem("c_mm"), q + 1)
                v = ps[0:64, 5 + q % 3, :].rearrange("p (j a c) -> p j a c", a=2, c=16)
                for a in range(2):
                    dve.tensor_copy(ct[64 * a:64 * a + 64, q // 2, 16 * (q % 2):16 * (q % 2) + 16, :], v[:, :, a, :]
                                    ).then_inc(sem("ct_made"), 1)

        def prep_act_scalars(act, part):
            if part == 0:
                act.wait_ge(sem("par_made"), 1)
                act.activation(S_step, par[:, 0, :], ACT.Exp).then_inc(sem("pa"), 1)
            elif part == 1:
                act.wait_ge(sem("pd_exp"), 1)
                act.activation(S_mag, S_lrs, ACT.Exp).then_inc(sem("pa"), 1)
                act.activation(S_r8, S_lrs, ACT.Exp, scale=float(L)).then_inc(sem("pa"), 1)
            else:
                act.wait_ge(sem("pd_ang"), 1)
                act.activation(S_sin, S_r, ACT.Sin).then_inc(sem("pa"), 1)
                act.activation(S_cos, S_rc, ACT.Sin).then_inc(sem("pa"), 1)

        def prep_dve_scalars(dve):
            def own(ins):
                ins.then_inc(sem("pd"), 1)
                chain[0] += 1
                dve.wait_ge(sem("pd"), chain[0])

            def tt(out, a, b, op):
                own(dve.tensor_tensor(out, a, b, op))

            def cmul(outr, outi, ar, ai, br, bi, t1, t2):
                tt(t1, ar, br, ALU.mult)
                tt(t2, ai, bi, ALU.mult)
                tt(outr, t1, t2, ALU.subtract)
                tt(t1, ar, bi, ALU.mult)
                tt(t2, ai, br, ALU.mult)
                tt(outi, t1, t2, ALU.add)

            dve.wait_ge(sem("par_made"), 1)
            dve.wait_ge(sem("pa"), 1)
            tt(S_lrs, par[:, 1, :], S_step, ALU.mult)
            dve.tensor_tensor(S_ang, par[:, 2, :], S_step, ALU.mult).then_inc(sem("pd_exp"), 1)
            dve.wait_ge(sem("pd_exp"), 1)
            own(dve.tensor_scalar(S_k, S_ang, 1.0 / TWO_PI, MAGIC, ALU.mult, ALU.add))
            own(dve.tensor_scalar(S_k, S_k, MAGIC, None, ALU.subtract))
            own(dve.scalar_tensor_tensor(S_r, S_k, -TURN[0], S_ang, ALU.mult, ALU.add))
            own(dve.scalar_tensor_tensor(S_r, S_k, -TURN[1], S_r, ALU.mult, ALU.add))
            own(dve.scalar_tensor_tensor(S_r, S_k, -TURN[2], S_r, ALU.mult, ALU.add))
            own(dve.tensor_scalar(S_r, S_r, 3.1415925, -3.1415925, ALU.min, ALU.max))
            own(dve.scalar_tensor_tensor(S_rc, S_r, -1.0, S_r, ALU.mult, ALU.max))
            dve.tensor_scalar(S_rc, S_rc, -1.0, TWO_PI / 4, ALU.mult, ALU.add).then_inc(sem("pd_ang"), 1)
            dve.wait_ge(sem("pa"), 5)
            own(dve.memset(pc[:, 0, :, 0], 1.0))
            own(dve.memset(pc[:, 1, :, 0], 0.0))
            tt(pc[:, 0, :, 1], S_mag, S_cos, ALU.mult)
            tt(pc[:, 1, :, 1], S_mag, S_sin, ALU.mult)
            for k in (1, 2, 4):
                b = [pc[:, r, :, k:k + 1].to_broadcast([P, GP, k]) for r in range(2)]
                cmul(pc[:, 0, :, k + 1:2 * k + 1], pc[:, 1, :, k + 1:2 * k + 1], pc[:, 0, :, 1:k + 1], pc[:, 1, :, 1:k + 1],
                     b[0], b[1], t1[:, 0:GP * k].rearrange("p (j k) -> p j k", k=k), t2[:, 0:GP * k].rearrange("p (j k) -> p j k", k=k))
            for s in range(L):
                own(dve.tensor_copy(pb[:, :, :, s], pc[:, :, :, L - 1 - s]))
            lr, li = par[:, 1, :], par[:, 2, :]
            tt(S_a, lr, lr, ALU.mult)
            tt(S_b, li, li, ALU.mult)
            tt(S_a, S_a, S_b, ALU.add)
            own(dve.reciprocal(S_a, S_a))
            own(dve.tensor_scalar(S_nr, pc[:, 0, :, 1], 1.0, None, ALU.subtract))
            tt(S_b, S_nr, lr, ALU.mult)
            tt(S_c, pc[:, 1, :, 1], li, ALU.mult)
            tt(S_b, S_b, S_c, ALU.add)
            tt(S_cor, S_b, S_a, ALU.mult)
            tt(S_b, pc[:, 1, :, 1], lr, ALU.mult)
            tt(S_c, S_nr, li, ALU.mult)
            tt(S_b, S_b, S_c, ALU.subtract)
            tt(S_coi, S_b, S_a, ALU.mult)
            dve.wait_ge(sem("b_loaded"), 32)
            w = GP * 16
            co = [v.unsqueeze(2).to_broadcast([P, GP, 16]) for v in (S_cor, S_coi)]
            v1, v2, v3 = (t[:, o:o + w].rearrange("p (j c) -> p j c", c=16) for t, o in ((t1, 0), (t2, 0), (t1, w)))
            tt(v1, bb[:, 0], co[0], ALU.mult)
            tt(v2, bb[:, 1], co[1], ALU.mult)
            tt(v1, v1, v2, ALU.subtract)
            tt(v2, bb[:, 0], co[1], ALU.mult)
            tt(v3, bb[:, 1], co[0], ALU.mult)
            tt(bb[:, 1], v2, v3, ALU.add)
            own(dve.tensor_copy(bb[:, 0], v1))
            own(dve.tensor_copy(pp[:, 0:2, :], par[:, 3:5, :]))
            cmul(pp[:, 2, :], pp[:, 3, :], pc[:, 0, :, 8], pc[:, 1, :, 8], pp[:, 0, :], pp[:, 1, :], S_a, S_b)
            src = (S_cos, S_sin)
            for m in range(10):
                dst = (S_e[m % 2], S_f[m % 2]) if m < 3 else (ek[:, 0, :, m - 3], ek[:, 1, :, m - 3])
                if m:
                    cmul(dst[0], dst[1], src[0], src[1], src[0], src[1], S_a, S_b)
                else:
                    own(dve.tensor_copy(dst[0], src[0]))
                    own(dve.tensor_copy(dst[1], src[1]))
                unit(dve, own, dst[0], dst[1], S_a, S_b)
                src = dst
            dve.tensor_copy(S_c, S_a).then_inc(sem("pp_made"), 1)
            dve.wait_ge(sem("pp_made"), 1)

        def unit(dve, own, re, im, a, b):
            own(dve.tensor_tensor(a, re, re, ALU.mult))
            own(dve.tensor_tensor(b, im, im, ALU.mult))
            own(dve.tensor_tensor(a, a, b, ALU.add))
            own(dve.tensor_scalar(a, a, -0.5, 1.5, ALU.mult, ALU.add))
            own(dve.tensor_tensor(re, re, a, ALU.mult))
            own(dve.tensor_tensor(im, im, a, ALU.mult))

        chain = [0]

        def prep_dve_block(dve, n):
            blk, kind = divmod(n, 3)
            j0 = 8 * blk

            def own(ins):
                ins.then_inc(sem("pd"), 1)
                chain[0] += 1
                dve.wait_ge(sem("pd"), chain[0])

            def tt(out, a, b, op):
                own(dve.tensor_tensor(out, a, b, op))

            if n >= 3:
                dve.wait_ge(sem(f"prep_out{kind}"), 16 * blk)
            if kind == 0:
                own(dve.memset(eb[:, 0, :, 0:1], 1.0))
                own(dve.memset(eb[:, 1, :, 0:1], 0.0))
                for m in range(7):
                    k = 1 << m
                    er_, ei_ = eb[:, 0, :, 0:k], eb[:, 1, :, 0:k]
                    br_, bi_ = (ek[:, r, j0:j0 + 8, m:m + 1].to_broadcast([P, 8, k]) for r in range(2))
                    v1, v2 = (t[:, 0:8 * k].rearrange("p (j k) -> p j k", k=k) for t in (t1, t2))
                    tt(v1, er_, br_, ALU.mult)
                    tt(v2, ei_, bi_, ALU.mult)
                    tt(eb[:, 0, :, k:2 * k], v1, v2, ALU.subtract)
                    tt(v1, er_, bi_, ALU.mult)
                    tt(v2, ei_, br_, ALU.mult)
                    tt(eb[:, 1, :, k:2 * k], v1, v2, ALU.add)
                v1, v2 = (t[:, 0:8 * P].rearrange("p (j k) -> p j k", k=P) for t in (t1, t2))
                unit(dve, own, eb[:, 0, :, 0:P], eb[:, 1, :, 0:P], v1, v2)
                for r in range(2):
                    own(dve.tensor_copy(eb[:, r, :, P:NCH], eb[:, r, :, 0:NCH - P]))
                own(dve.tensor_copy(eb[:, 2, :, :], S_r8[:, j0:j0 + 8].unsqueeze(2).to_broadcast([P, 8, NCH])))
                own(dve.memset(eb[:, 2, :, 0:1], 0.0))
                dve.memset(eb[:, 2, :, P:P + 1], 0.0).then_inc(sem("prep_made"), 1)
            elif kind == 1:
                sh = [P, 8, L, 16]
                p_ = [pb[:, r, j0:j0 + 8, :].unsqueeze(3).to_broadcast(sh) for r in range(2)]
                b_ = [bb[:, r, j0:j0 + 8, :].unsqueeze(2).to_broadcast(sh) for r in range(2)]
                o_ = [bo[:, :, r, :].rearrange("p j (s c) -> p j s c", c=16) for r in range(2)]
                v1, v2 = (t[:, 0:8 * P].rearrange("p (j s c) -> p j s c", s=L, c=16) for t in (t1, t2))
                tt(v1, p_[0], b_[0], ALU.mult)
                tt(v2, p_[1], b_[1], ALU.mult)
                tt(o_[0], v1, v2, ALU.subtract)
                tt(v1, p_[0], b_[1], ALU.mult)
                tt(v2, p_[1], b_[0], ALU.mult)
                dve.tensor_tensor(o_[1], v1, v2, ALU.add).then_inc(sem("prep_made"), 1)
            else:
                sh = [P, 8, L + 1, 16]
                p_ = [pc[:, r, j0:j0 + 8, :].unsqueeze(3).to_broadcast(sh) for r in range(2)]
                c_ = [ct[:, r, j0:j0 + 8, :].unsqueeze(2).to_broadcast(sh) for r in range(2)]
                o_ = [co_[:, :, r, :].rearrange("p j (s c) -> p j s c", c=16) for r in range(2)]
                v1, v2 = (t[:, 0:8 * CW].rearrange("p (j s c) -> p j s c", s=L + 1, c=16) for t in (t1, t2))
                tt(v1, p_[0], c_[0], ALU.mult)
                tt(v2, p_[1], c_[1], ALU.mult)
                tt(o_[0], v1, v2, ALU.subtract)
                tt(v1, p_[0], c_[1], ALU.mult)
                tt(v2, p_[1], c_[0], ALU.mult)
                tt(v1, v1, v2, ALU.add)
                dve.tensor_scalar(o_[1], v1, -1.0, None, ALU.mult).then_inc(sem("prep_made"), 1)
            dve.wait_ge(sem("prep_made"), n + 1)

        def prep_pool_block(pool, n):
            blk, kind = divmod(n, 3)
            j0 = 8 * blk
            pool.wait_ge(sem("prep_made"), n + 1)
            if kind == 0:
                pool.dma_start(dE[:, :, j0:j0 + 8, :], eb[:]).then_inc(sem(f"prep_out{kind}"), 16)
            elif kind == 1:
                pool.dma_start(dB[:, j0:j0 + 8, :, :], bo[:]).then_inc(sem(f"prep_out{kind}"), 16)
            else:
                pool.dma_start(dC[:, j0:j0 + 8, :, :], co_[:]).then_inc(sem(f"prep_out{kind}"), 16)

        NF = KD

        def s5_sp(sp):
            for c, (s, n) in enumerate(CHUNKS):
                sp.wait_ge(sem("acc_used"), ACC_FF1 - KD * (2 - c))
                sp.dma_start(xs.rearrange("p (f t) -> p f t", f=KD)[:, :, s:s + n], x3[:, :, s:s + n]).then_inc(sem("x_out"), 16)
            sp.wait_ge(sem("p_out"), 16)
            sp.dma_start(p4[:], dP).then_inc(sem("p4_loaded"), 16)

            def store_h(f):
                sp.wait_ge(sem("n_f"), n_units(2, 2 * KD + f + 1))
                sp.dma_start(dU[f * P:(f + 1) * P, :], hp[:, f * T:(f + 1) * T]).then_inc(sem(f"u_out{f % 2}"), 16)

            def load(f):
                if f >= 1:
                    sp.wait_ge(sem("e_BT"), 2 * f)
                    sp.wait_ge(sem("s_K"), f)
                if f >= 3:
                    sp.wait_ge(sem("s_Y"), f - 2)
                js = slice(4 * f, 4 * f + 4)
                sp.dma_start(br[:], dB[:, js, :, :]).then_inc(sem("br_loaded"), 16)
                sp.dma_start(ca[:, f % 3], dC[:, js, :, :]).then_inc(sem(f"ca_loaded{f % 2}"), 16)
                if f >= 2:
                    sp.wait_ge(sem("s_Y"), f - 1)
                if f == 0:
                    store_h(0)
                    store_h(1)
                sp.wait_ge(sem(f"u_out{f % 2}"), 16 * (f // 2 + 1))
                if f + 2 < NF:
                    store_h(f + 2)
                for s in range(L):
                    sp.dma_start(u[16 * s:16 * s + 16, f % 2, :, :],
                                 dU[f * P:(f + 1) * P, s * NCH:(s + 1) * NCH].rearrange("(g c) n -> c g n", c=16)
                                 ).then_inc(sem(f"u_loaded{f % 2}"), 16)
                if f >= 1:
                    sp.wait_ge(sem("s_rot"), f)
                else:
                    sp.wait_ge(sem("x_out"), 16 * (1 + NC))
                    sp.wait_ge(sem("n_f"), n_units(2))
                sp.dma_start(e3[:], dE[:, :, js, :]).then_inc(sem("e3_loaded"), 16)

            load(0)
            for f in range(NF + 1):
                if f < NF:
                    sp.wait_ge(sem("e_K"), 2 * f + 2)
                    if f >= 2:
                        sp.wait_ge(sem("s_Y"), f - 1)
                    sp.wait_ge(sem("t_zero"), 1)
                    for s in range(L):
                        sp.dma_start(tm[16 * s:16 * s + 16, f % 2, :, 16 * s:P], kt[0:16, :, 0:P - 16 * s]).then_inc(sem(f"t_made{f % 2}"), 16)
                if f + 1 < NF:
                    load(f + 1)
                if f:
                    g = f - 1
                    sp.wait_ge(sem("e_Y"), 4 * g + 4)
                    if g >= 2:
                        sp.wait_ge(sem(f"z_loaded{g % 2}"), 16 * (g // 2))
                    for t in range(L):
                        sp.dma_start(dY[g * P:(g + 1) * P, t * NCH:(t + 1) * NCH].rearrange("(g c) n -> c g n", c=16),
                                     yy[16 * t:16 * t + 16, g % 2, :, :]).then_inc(sem(f"y_stored{g % 2}"), 16)
            sp.wait_ge(sem("y_f"), NF)
            sp.dma_start(x[:], xs).then_inc(sem("x_back"), 16)
            sp.wait_ge(sem("fin_t"), 1)
            for q, o in enumerate(("re_p", "im_p", "re_s", "im_s")):
                sp.dma_start(O[o].rearrange("o b g p -> (o b g p)").rearrange("(j q) -> j q", q=P), fout[0:GP, q, :]).then_inc(sem("fin_out"), 16)

        def s5_pe(pe):
            def first(f):
                if f >= 2:
                    pe.wait_ge(sem("e_Y"), 4 * (f - 1))
                elif f == 0:
                    pe.wait_ge(sem("n_rt"), NC * 3)
                pe.wait_ge(sem("br_loaded"), 16 * (f + 1))
                for q in range(8):
                    mm = pe.transpose(ps[:, q // 4, (q % 4) * P:(q % 4 + 1) * P], br[:, q // 2, q % 2, :], ident[:])
                mm.then_inc(sem("s_B"), 1)
                pe.wait_ge(sem(f"ca_loaded{f % 2}"), 16 * (f // 2 + 1))
                for g in range(8):
                    j, a = divmod(g, 2)
                    r = slice(64 * a, 64 * a + 64)
                    for q in range(2):
                        mm = pe.matmul(ps[0:16, 2 + a, j * P:(j + 1) * P], br[r, j, q, P - 16:P], ca[r, f % 3, j, q, 0:P],
                                       start=q == 0, stop=q == 1)
                mm.then_inc(sem("s_K"), 1)
                pe.wait_ge(sem(f"u_loaded{f % 2}"), 16 * L * (f // 2 + 1))
                pe.wait_ge(sem("e_BT"), 2 * f + 2)
                if f:
                    pe.wait_ge(sem("e_X"), 3 * f)
                for q in range(2):
                    for j in range(4):
                        n = 4 * q + j
                        for a in range(2):
                            mm = pe.matmul(ps[64 * a:64 * a + 64, 4 + n // 3, (n % 3) * NCH:(n % 3 + 1) * NCH],
                                           bt[:, j, q, 64 * a:64 * a + 64], u[:, f % 2, 2 * j + a, :], start=True, stop=True,
                                           skip_group_check=True)
                mm.then_inc(sem("s_X"), 1)

            def second(f):
                pe.wait_ge(sem(f"t_made{f % 2}"), 16 * L * (f // 2 + 1))
                pe.wait_ge(sem("s_sh"), 2 * f + 2)
                if f:
                    pe.wait_ge(sem("e_Y"), 4 * f)
                nxt = min(f + 1, NF - 1)
                pe.wait_ge(sem("e_BT"), 2 * nxt + 2)
                pe.wait_ge(sem("e_K"), 2 * nxt + 2)
                for g in range(8):
                    j, a = divmod(g, 2)
                    r = slice(64 * a, 64 * a + 64)
                    out = ps[:, 2 * a + j // 2, (j % 2) * NCH:(j % 2 + 1) * NCH]
                    pe.matmul(out, tm[:, f % 2, g, :], u[:, f % 2, g, :], start=True, stop=False)
                    for q in range(2):
                        mm = pe.matmul(out, ca[r, f % 3, j, q, 16:CW], sh[r, f % 2, q, j, :], start=False, stop=q == 1)
                mm.then_inc(sem("s_Y"), 1)
            for f in range(NF + 1):
                if f < NF:
                    first(f)
                if f:
                    second(f - 1)
            pe.wait_ge(sem("fin_made"), 4 * NF)
            for q in range(4):
                mm = pe.transpose(ps[0:GP, 4, q * P:(q + 1) * P], fin[:, q, :], ident[:])
            mm.then_inc(sem("fin_mm"), 1)

        def s5_act(act):
            def first(f):
                act.wait_ge(sem("s_B"), f + 1)
                if f:
                    act.wait_ge(sem("s_X"), f)
                for b in range(2):
                    act.activation(bt[:, 2 * b:2 * b + 2, :, :], ps[:, b, :].rearrange("p (j q n) -> p j q n", j=2, q=2), ACT.Copy
                                   ).then_inc(sem("e_BT"), 1)
                act.wait_ge(sem("s_X"), f + 1)
                if f:
                    act.wait_ge(sem("s_rot"), f)
                for b in range(3):
                    n = 3 if b < 2 else 2
                    act.activation(xx[:, 3 * b * NCH:(3 * b + n) * NCH], ps[:, 4 + b, 0:n * NCH], ACT.Copy).then_inc(sem("e_X"), 1)

            def second(f):
                act.wait_ge(sem("s_Y"), f + 1)
                if f >= 2:
                    act.wait_ge(sem(f"y_stored{f % 2}"), 16 * L * (f // 2))
                for b in range(4):
                    act.activation(yy[:, f % 2].rearrange("p (h l a) n -> p a h l n", l=2, a=2)[:, b // 2, b % 2],
                                   ps[:, b, 0:2 * NCH].rearrange("p (l n) -> p l n", l=2), ACT.Copy).then_inc(sem("e_Y"), 1)

            def third(f):
                act.wait_ge(sem("y_f"), f + 1)
                yt = yp[:, f * T:(f + 1) * T]
                act.activation(yt, yt, GELU).then_inc(sem("y_g"), 1)

            for f in range(NF + 3):
                if f < NF:
                    first(f)
                if 1 <= f <= NF:
                    second(f - 1)
                if f >= 3:
                    third(f - 3)

        def s5_pool(pool):
            for f in range(NF):
                pool.wait_ge(sem(f"y_stored{f % 2}"), 16 * L * (f // 2 + 1))
                if f >= 2:
                    pool.wait_ge(sem("y_f"), f - 1)
                pool.dma_start(zb[f % 2][:], dY[f * P:(f + 1) * P, :]).then_inc(sem(f"z_loaded{f % 2}"), 16)

        def s5_dve(dve):
            def own(ins):
                ins.then_inc(sem("sd"), 1)
                chain[1] += 1
                dve.wait_ge(sem("sd"), chain[1])

            def tt(out, a, b, op):
                own(dve.tensor_tensor(out, a, b, op))

            chain.append(0)
            W4 = 4 * NCH
            xr, xi = xx[:, 0:W4], xx[:, W4:2 * W4]
            er_, ei_, r8_ = (e3[:, q].rearrange("p j n -> p (j n)") for q in range(3))

            def first(f):
                dve.wait_ge(sem("s_K"), f + 1)
                if f:
                    dve.wait_ge(sem(f"t_made{(f - 1) % 2}"), 16 * L * ((f - 1) // 2 + 1))
                for b in range(2):
                    dve.tensor_copy(kt[0:16].rearrange("p (j a) n -> p a j n", a=2)[:, b], ps[0:16, 2 + b, :].rearrange("p (j n) -> p j n", j=4)).then_inc(sem("e_K"), 1)

            def scan(f):
                dve.wait_ge(sem("e_X"), 3 * f + 3)
                dve.wait_ge(sem("e3_loaded"), 16 * (f + 1))
                for q in range(2):
                    v = xx[:, q * W4:(q + 1) * W4].rearrange("p (j n) -> p j n", j=4)[:, :, P:P + 1]
                    own(dve.tensor_tensor(v, v, p4[:, 2 + q, 4 * f:4 * f + 4].unsqueeze(2), ALU.add))
                tt(v1, xr, er_, ALU.mult)
                tt(v2, xi, ei_, ALU.mult)
                tt(v1, v1, v2, ALU.add)
                tt(v2, xi, er_, ALU.mult)
                tt(v3, xr, ei_, ALU.mult)
                tt(v2, v2, v3, ALU.subtract)
                own(dve.tensor_tensor_scan(w1, r8_, v1, 0.0, ALU.mult, ALU.add))
                own(dve.tensor_tensor_scan(w2, r8_, v2, 0.0, ALU.mult, ALU.add))
                tt(v1, w1, er_, ALU.mult)
                tt(v2, w2, ei_, ALU.mult)
                tt(v1, v1, v2, ALU.subtract)
                tt(v2, w1, ei_, ALU.mult)
                tt(v3, w2, er_, ALU.mult)
                dve.tensor_tensor(v2, v2, v3, ALU.add).then_inc(sem("s_rot"), 1)
                dve.wait_ge(sem("s_rot"), f + 1)
                if f >= 2:
                    dve.wait_ge(sem("s_Y"), f - 1)
                for q, v in enumerate((v1, v2)):
                    v = v.rearrange("p (j n) -> p j n", j=4)
                    o = sh[:, f % 2, q, :, :]
                    for r, n in ((0, P - 1), (2, NCH - 1)):
                        dve.tensor_copy(fin[:, q + r, 4 * f:4 * f + 4], v[:, :, n]).then_inc(sem("fin_made"), 1)
                    own(dve.tensor_copy(o[:, :, 1:NCH], v[:, :, 0:NCH - 1]))
                    own(dve.memset(o[:, :, 0:1], 0.0))
                    dve.tensor_copy(o[:, :, P:P + 1], p4[:, q, 4 * f:4 * f + 4].unsqueeze(2)).then_inc(sem("s_sh"), 1)
                dve.wait_ge(sem("s_sh"), 2 * f + 2)

            def second(f):
                dve.wait_ge(sem(f"z_loaded{f % 2}"), 16 * (f // 2 + 1))
                dve.scalar_tensor_tensor(yp[:, f * T:(f + 1) * T].rearrange("p (n s) -> p s n", s=L),
                                         hp[:, f * T:(f + 1) * T].rearrange("p (s n) -> p s n", s=L), cols[:, 40 + f:41 + f],
                                         zb[f % 2][:].rearrange("p (s n) -> p s n", s=L), ALU.mult, ALU.add).then_inc(sem("y_f"), 1)

            dve.wait_ge(sem("p4_loaded"), 16)
            for f in range(NF + 2):
                if f < NF:
                    first(f)
                    scan(f)
                if f >= 2:
                    second(f - 2)
            dve.wait_ge(sem("fin_mm"), 1)
            dve.tensor_copy(fout[0:GP].rearrange("p q n -> p (q n)"), ps[0:GP, 4, :]).then_inc(sem("fin_t"), 1)

        def y_split_act(act):
            for c, (s, n) in enumerate(CHUNKS):
                for f in range(KD):
                    o = f * T + s
                    act.wait_ge(sem("y_g"), NF)
                    act.activation(hhi[:, o:o + n], yp[:, o:o + n], ACT.Copy).then_inc(sem("ys_hi"), 1)

        def y_split_lo(eng, odd):
            for c, (s, n) in enumerate(CHUNKS):
                for f in range(odd, KD, 2):
                    o = f * T + s
                    eng.wait_ge(sem("ys_hi"), c * KD + f + 1)
                    eng.tensor_tensor(hlo[:, o:o + n], yp[:, o:o + n], hhi[:, o:o + n].bitcast(F32), ALU.subtract
                                      ).then_inc(sem(("ys_lo_p", "ys_lo_v")[odd]), 1)

        def glu_slab(t):
            m, half = divmod(t - SLAB_GLU, 2)
            return w_glu[:, :, half * D + m * P:half * D + (m + 1) * P]

        def glu_pe(pe):
            for q in range(KD):
                pe_pair(pe, SLAB_GLU + 2 * q, PAIR_GLU + NC * q, ready=(lambda c, f: pe.wait_ge(sem(("ys_lo_p", "ys_lo_v")[f % 2]), 4 * c + f // 2 + 1)) if q == 0 else None)
            for c in range(NC):
                sum_pe(pe, 3, c)

        def glu_act(act):
            for q in range(KD):
                for j in range(2):
                    if q < 2:
                        slab_hi(act, SLAB_GLU + 2 * q + 2 + j)
                    else:
                        slab_hi(act, SLAB_GLU + 2 * q + 2 + j, "pair_ready", PAIR_GLU + NC * (q - 1))
                for c, (s, n) in enumerate(CHUNKS):
                    v = PAIR_GLU + NC * q + c
                    act.wait_ge(sem("pair_ready"), v + 1)
                    act.wait_ge(sem("pair_used"), v - 1)
                    act.activation(abuf[:, v % 2, 0:n], ps[:, 2 * (v % 2) + 1, 0:n], ACT.Sigmoid).then_inc(sem("pair_act"), 1)
                    if q:
                        act.wait_ge(sem("glu_res"), NC * (q - 1) + c + 1)
                        square(act, 3, c, q - 1)
            for c in range(NC):
                act.wait_ge(sem("glu_res"), NC * (KD - 1) + c + 1)
                square(act, 3, c, KD - 1)

        def glu_dve(dve):
            dve.wait_ge(sem("x_back"), 32)
            for q in range(KD):
                for c, (s, n) in enumerate(CHUNKS):
                    r = NC * q + c
                    v = PAIR_GLU + r
                    dve.wait_ge(sem("pair_act"), v + 1)
                    if r >= 2:
                        dve.wait_ge(sem("glu_res"), r - 1)
                    dve.tensor_tensor(fbuf[:, v % 2, 0:n], ps[:, 2 * (v % 2), 0:n], abuf[:, v % 2, 0:n], ALU.mult).then_inc(sem("pair_used"), 1)
                    dve.wait_ge(sem("pair_used"), v + 1)
                    xo = x[:, q * T + s:q * T + s + n]
                    dve.tensor_tensor(xo, xo, fbuf[:, v % 2, 0:n], ALU.add).then_inc(sem("glu_res"), 1)

        def out_pe(pe):
            for tt, (s, n) in enumerate(TILES):
                c, o = tt // 3, s - CHUNKS[tt // 3][0]
                pe.wait_ge(sem("n_add"), n_adds(4, (KD - 1) * (c + 1)))
                mm = pe.matmul(ps[0:n, 0, tt:tt + 1], ssum[:, c, o:o + n], ones[:, 0:1], start=True, stop=True, skip_group_check=True)
            mm.then_inc(sem("y_sum"), 1)
            for tt, (s, n) in enumerate(TILES):
                pe.wait_ge(sem("yg"), KD * (tt // 3 + 1))
                for b in range(2):
                    if tt >= 2:
                        pe.wait_ge(sem(("yo_v", "yo_a")[b]), tt - 1)
                    for f in range(4):
                        o = (4 * b + f) * T + s
                        mm = pe.transpose(ps[0:n, 4 + (2 * tt + b) % 4, f * P:(f + 1) * P], yf[:, o:o + n], ident[:])
                    mm.then_inc(sem("yo_mm"), 1)

        RT = ((P, slice(0, 8)), (DEC, slice(8, 9)))

        def out_root(act):
            act.wait_ge(sem("y_sum"), 1)
            for n, q in RT:
                act.activation(rms[0:n, 0, q], ps[0:n, 0, q], ACT.Sqrt, bias=epsb[0:n, 0:1], scale=1.0 / D).then_inc(sem("y_root"), 1)

        def out_factor(dve):
            dve.wait_ge(sem("y_root"), 2)
            for n, q in RT:
                dve.reciprocal(rms[0:n, 0, q], rms[0:n, 0, q]).then_inc(sem("y_factor"), 1)

        def out_take(eng, b, scaled):
            eng.wait_ge(sem("y_factor"), 2)
            for tt, (s, n) in enumerate(TILES):
                eng.wait_ge(sem("yo_mm"), 2 * tt + b + 1)
                if tt >= 2:
                    eng.wait_ge(sem(f"y_out{tt % 2}"), 16 * (tt // 2))
                scaled(yo[0:n, tt % 2, 512 * b:512 * b + 512], ps[0:n, 4 + (2 * tt + b) % 4, :], rms[0:n, 0, tt:tt + 1]).then_inc(sem(("yo_v", "yo_a")[b]), 1)

        def out_sp(sp):
            for tt, (s, n) in enumerate(TILES):
                sp.wait_ge(sem("yo_v"), tt + 1)
                sp.wait_ge(sem("yo_a"), tt + 1)
                sp.dma_start(y_new[0][s:s + n, :] if tt < 8 else y_new[1], yo[0:n, tt % 2, :]).then_inc(sem(f"y_out{tt % 2}"), 16)


        POOL0 = 2
        block = ctx.enter_context(nc.Block())

        @block.sync
        def _(sp):
            for tt, (s, n) in enumerate(TILES):
                if tt >= 2:
                    sp.wait_ge(sem("xt_mm"), 2 * (tt - 1))
                src = xp[s:s + n, :] if tt < 8 else xd
                sp.dma_start(xin[0:n, tt % 2, :], src).then_inc(sem(f"x_loaded{tt % 2}"), 16)
                if tt == 0:
                    for j, w in enumerate((A["norm_mix"][0], A["norm_mix"][1], A["norm_ffn"][0], A["norm_ffn"][1],
                                           A["norm_final"], A["ssm_d"][0])):
                        sp.dma_start(nrow[8 * j:8 * j + 8, :], w.rearrange("(f p) -> f p", p=P)).then_inc(sem("n_loaded"), 16)
                if tt in (2, 3):
                    load_slab(sp, tt - 2, w_in[:, :, (tt - 2) * P:(tt - 1) * P])
            prep_sp(sp)
            for t in range(2, 4):
                load_slab(sp, t, w_in[:, :, t * P:(t + 1) * P])
            sp.wait_ge(sem("n_f"), n_units(0))
            sp.dma_start(xs, x[:]).then_inc(sem("x_out"), 16)
            for t in range(4, IN_TILES):
                load_slab(sp, t, w_in[:, :, t * P:(t + 1) * P])
                if 0 <= t - 9 < 8:
                    kv_store(sp, t - 9)
            tr_sp(sp)
            at_sp(sp)
            for t in range(8):
                load_slab(sp, SLAB_OUT + t, w_out[:, :, t * P:(t + 1) * P])
            ffn_sp(sp, F[0])
            ffn_sp(sp, F[0], 1)
            for t in range(2):
                load_slab(sp, SLAB_GLU + t, glu_slab(SLAB_GLU + t))
            s5_sp(sp)
            for t in range(2, 2 * KD):
                load_slab(sp, SLAB_GLU + t, glu_slab(SLAB_GLU + t))
            ffn_sp(sp, F[1])
            ffn_sp(sp, F[1], 1)
            out_sp(sp)
            sp.wait_ge(sem("y_out0"), 16 * 5)
            sp.wait_ge(sem("y_out1"), 16 * 4)
            sp.wait_ge(sem("fin_out"), 16 * 4)

        @block.gpsimd
        def _(pool):
            pool.memset(ident[:], 0.0).then_inc(sem("pool"), 1)
            pool.memset(cols[:, 48:49], EPS).then_inc(sem("pool"), 1)
            pool.wait_ge(sem("pool"), 2)
            pool.memset(ones[:], 1.0).then_inc(sem("consts"), 1)
            pool.affine_select(out=ident[:], in_=ident[:], compare_op=ALU.not_equal, fill=1.0, base=0, pattern=[[-1, P]],
                               channel_multiplier=1).then_inc(sem("ident_made"), 1)
            for t in range(2):
                slab_lo(pool, t)
            norm_pool(pool, 0)

            def store(t, i=None, b=0):
                pool.wait_ge(sem("acc_used"), step(NC * (t + 1), i, NC * b))
                r = step(t * P, i, b * P)
                pool.dma_start(zT[bass.ds(r, P), :] if i is not None else zT[r:r + P, :], zst[:, t % 2, :]
                               ).then_inc(sem(f"z_stored{t % 2}"), 16)

            for t in range(IN_TILES):
                if t + 2 < IN_TILES:
                    slab_lo(pool, t + 2)
                store(t)
                if t == 4:
                    pool.wait_ge(sem("pp_made"), 1)
                    pool.dma_start(dP, pp[:]).then_inc(sem("p_out"), 16)
                if 6 <= t < 18:
                    prep_pool_block(pool, t - 6)
            tr_pool(pool)
            at_pool_make(pool)
            at_pool(pool)
            for t in range(-2, 9):
                if t < 8:
                    slab_lo(pool, SLAB_OUT + t + 2)
                if t >= 1:
                    for c in range(NC):
                        add_square(pool, 1, c, t - 1)
            norm_pool(pool, 1)
            ffn_pool(pool, F[0])
            pool.wait_ge(sem("n_f"), n_units(2))
            pool.memset(tm[:], 0.0).then_inc(sem("t_zero"), 1)
            s5_pool(pool)
            y_split_lo(pool, 0)
            for q in range(KD + 1):
                if q < KD:
                    for j in range(2):
                        slab_lo(pool, SLAB_GLU + 2 * q + 2 + j)
                if q:
                    for c in range(NC):
                        add_square(pool, 3, c, q - 1)
            norm_pool(pool, 3)
            ffn_pool(pool, F[1])

        @block.scalar
        def _(act):
            for tt, (s, n) in enumerate(TILES):
                act.wait_ge(sem("xt_mm"), 2 * tt + 2)
                act.activation(x3[:, 4:8, s:s + n], ps[:, (2 * tt + 1) % 4, :].rearrange("p (f n) -> p f n", f=4)[:, :, 0:n], ACT.Copy
                               ).then_inc(sem("xt_a"), 1)
                if tt in (4, 5):
                    slab_hi(act, tt - 4)

            act.wait_ge(sem("consts"), 1)
            norm_act(act, 0, True)
            for t in range(IN_TILES):
                if t + 2 < IN_TILES:
                    slab_hi(act, t + 2, "acc_ready" if t >= 2 else None, NC * (t - 1))
                if t < 3:
                    prep_act_scalars(act, t)
                if t >= 2:
                    act.wait_ge(sem(f"z_stored{t % 2}"), 16 * (t // 2))
                if 0 <= t - 2 - KT < 8:
                    act.wait_ge(sem("kv_mm"), t - 1 - KT)
                for c, (s, n) in enumerate(CHUNKS):
                    v = NC * t + c
                    act.wait_ge(sem("acc_ready"), v + 1)
                    act.activation(zst[:, t % 2, s:s + n], acc(v)[:, 0:n], ACT.Copy).then_inc(sem("acc_used"), 1)
                if 0 <= t - 1 - KT < 8:
                    kv_act(act, t - 1 - KT)
            tr_act(act)
            at_act(act)
            act.wait_ge(sem("o_lo"), GROUPS)
            for t in range(-2, 8):
                slab_hi(act, SLAB_OUT + t + 2, "acc_ready" if t >= 2 else None, ACC_OUT + NC * (t - 1))
                if t >= 1:
                    for c in range(NC):
                        act.wait_ge(sem("acc_used"), ACC_OUT + NC * (t - 1) + c + 1)
                        square(act, 1, c, t - 1)
            for c in range(NC):
                act.wait_ge(sem("acc_used"), ACC_FF0 - NC + c + 1)
                square(act, 1, c, KD - 1)
            norm_act(act, 1, True)
            ffn_act(act, F[0], "acc_ready", ACC_FF0)
            norm_act(act, 2, False)
            s5_act(act)
            y_split_act(act)
            glu_act(act)
            act.wait_ge(sem("fin_out"), 16 * 4)
            norm_act(act, 3, True)
            ffn_act(act, F[1], "pair_ready", PAIR_FF1)
            out_root(act)
            out_take(act, 1, lambda o, i, r: act.activation(o, i, ACT.Identity, scale=r))

        @block.vector
        def _(dve):
            dve.wait_ge(sem("cols_mm"), 1)
            dve.tensor_copy(cols[:, 0:48], ps[:, 4, 0:48]).then_inc(sem("cols_made"), 1)
            for tt, (s, n) in enumerate(TILES):
                dve.wait_ge(sem("xt_mm"), 2 * tt + 1)
                dve.tensor_copy(x3[:, 0:4, s:s + n], ps[:, (2 * tt) % 4, :].rearrange("p (f n) -> p f n", f=4)[:, :, 0:n]
                                ).then_inc(sem("xt_v"), 1)
            dve.wait_ge(sem("cols_made"), 1)
            prep_dve_in(dve)
            norm_dve(dve, 0, 0)

            prep_dve_scalars(dve)
            dve.wait_ge(sem("x_out"), 16)
            for n in range(12):
                prep_dve_block(dve, n)
            tr_dve(dve)
            dve.wait_ge(sem("at_made"), 2)
            at_dve(dve)
            dve.wait_ge(sem("x_back"), 16)
            for m in range(KD):
                for c, (s, n) in enumerate(CHUNKS):
                    v = ACC_OUT + m * NC + c
                    dve.wait_ge(sem("acc_ready"), v + 1)
                    xo = x[:, m * T + s:m * T + s + n]
                    dve.tensor_tensor(xo, acc(v)[:, 0:n], xo, ALU.add).then_inc(sem("acc_used"), 1)
            norm_dve(dve, 1, 16)
            ffn_dve(dve, F[0])
            norm_dve(dve, 2, 8, plain=hp, by_chunk=True)
            s5_dve(dve)
            y_split_lo(dve, 1)
            glu_dve(dve)
            norm_dve(dve, 3, 24)
            ffn_dve(dve, F[1])
            out_factor(dve)
            out_take(dve, 0, lambda o, i, r: dve.tensor_scalar(o, i, r, None, ALU.mult))

        @block.tensor
        def _(pe):
            pe.wait_ge(sem("ident_made"), 1)
            pe.wait_ge(sem("n_loaded"), 16 * 6)
            pe.transpose(ps[:, 4, 0:48], nrow[0:48, :], ident[0:48, 0:48]).then_inc(sem("cols_mm"), 1)
            for tt, (s, n) in enumerate(TILES):
                pe.wait_ge(sem(f"x_loaded{tt % 2}"), 16 * (tt // 2 + 1))
                for b in range(2):
                    if tt >= 2:
                        pe.wait_ge(sem(("xt_v", "xt_a")[b]), tt - 1)
                    for f in range(4):
                        mm = pe.transpose(ps[:, (2 * tt + b) % 4, f * P:f * P + n], xin[0:n, tt % 2, (4 * b + f) * P:(4 * b + f + 1) * P],
                                          ident[0:n, 0:n])
                    mm.then_inc(sem("xt_mm"), 1)
            pe.wait_ge(sem("cols_made"), 1)
            prep_pe(pe)
            pe.wait_ge(sem("par_made"), 1)
            pe.wait_ge(sem("ct_made"), 8)
            pe.wait_ge(sem("xt_v"), 9)
            pe.wait_ge(sem("xt_a"), 9)
            pe.wait_ge(sem("consts"), 1)
            sum_pe0(pe, 0)
            sum_pe0(pe, 1)

            def first_ready(c, k):
                if (c, k) == (1, 0):
                    sum_pe0(pe, 2)
                h_ready(0)(pe)(c, k)

            for t in range(5):
                pe_single(pe, t, ready=first_ready if t == 0 else None)
            with pe.Fori(0, 2) as i:
                for t in range(5, 9):
                    pe_single(pe, t, i, 4)
                    kv_pe(pe, t - 1 - KT, i)
            for t in range(13, IN_TILES):
                pe_single(pe, t)
            tr_pe(pe)
            at_pe(pe)
            pe.wait_ge(sem("o_lo"), GROUPS)
            pe.wait_ge(sem("mix_lo"), 4 * NC)
            for t in range(8):
                pe_single(pe, SLAB_OUT + t)
            for c in range(NC):
                sum_pe(pe, 1, c)
            ffn_pe(pe, F[0])
            s5_pe(pe)
            glu_pe(pe)
            pe.wait_ge(sem("glu_res"), NC * KD)
            ffn_pe(pe, F[1])
            out_pe(pe)


_INS = ["x_prompt", "x_sample", "cache_sb_k", "cache_sb_v", "state_ssm_re", "state_ssm_im", "norm_mix", "norm_ffn",
        "norm_final", "ab_w_in", "sgu_w", "sgu_b", "ab_w_out", "ssm_lam_re", "ssm_lam_im", "ssm_log_step", "ssm_b_re",
        "ssm_b_im", "ssm_c_re", "ssm_c_im", "ssm_d", "ssm_w_glu", "ffn_w_gate", "ffn_w_up", "ffn_w_down"]
_OUTS = {"y_p": (1, 1024, 1024), "y_s": (1, 64, 1024), "k_p": (1, 1, 1024, 8, 64), "v_p": (1, 1, 1024, 8, 64),
         "k_s": (1, 1, 64, 8, 64), "v_s": (1, 1, 64, 8, 64), "g_s": (1, 1, 64, 512), "re_p": (1, 1, 64, 64),
         "im_p": (1, 1, 64, 64), "re_s": (1, 1, 64, 64), "im_s": (1, 1, 64, 64)}


def kernel(**inputs):
    import numpy as np
    from concourse import bacc
    from concourse.bass_utils import run_bass_kernel_spmd

    nc = bacc.Bacc("TRN2", target_bir_lowering=False, num_devices=1)
    arrays, ins = {}, {}
    for name in _INS:
        a = np.ascontiguousarray(inputs[name])
        arrays[f"in_{name}"] = a
        ins[name] = nc.dram_tensor(f"in_{name}", a.shape, F32, kind="ExternalInput").ap()
    outs = {name: nc.dram_tensor(f"out_{name}", shape, F32, kind="ExternalOutput").ap() for name, shape in _OUTS.items()}
    build(nc, ins, outs)
    r = run_bass_kernel_spmd(nc, [arrays], core_ids=[0])
    return tuple(r.results[0][f"out_{name}"] for name in _OUTS)
```
